# Optimizing a Trainium2 kernel written in Bass

```python
import jax, jax.numpy as jnp
from jax import lax
import numpy as np

D_MODEL = 1024
BATCH = 1
SEQ = 1024
DEPTH = 1

CTX_LEN = 256
GRID_W = 64
N_HEADS = 8
HEAD_DIM = D_MODEL // N_HEADS
HGRN_WIDTH = N_HEADS * HEAD_DIM
CHUNK = 64
POOL_WINDOWS = (2, 4, 8, 16)
POOL_GROUP = 128
POOL_WIDTH = POOL_GROUP * len(POOL_WINDOWS)
N_EXPERTS = 16
CAPACITY_FACTOR = 2
EXPERT_FF = 1024
EPS = 1e-6

Q_OFF = 0
I_OFF = Q_OFF + HGRN_WIDTH
FF_OFF = I_OFF + HGRN_WIDTH
FB_OFF = FF_OFF + HGRN_WIDTH
OG_OFF = FB_OFF + HGRN_WIDTH
P_OFF = OG_OFF + HGRN_WIDTH
GA_OFF = P_OFF + POOL_WIDTH
GB_OFF = GA_OFF + D_MODEL
IN_COLS = GB_OFF + D_MODEL

kernel_name = "hybrid_hgrn2_pool_ec_moe_dit"

def rms_norm(x, g):
    xf = x.astype(jnp.float32)
    y = xf * lax.rsqrt(jnp.mean(xf * xf, axis=-1, keepdims=True) + EPS)
    return y.astype(x.dtype) * g

def modulate(x, shift, scale):
    return x * (1 + scale) + shift

def adaln(cvec, w_mod, b_mod):
    return jnp.split(jax.nn.silu(cvec) @ w_mod + b_mod, 6, axis=-1)

def to_heads(z):
    return z.astype(jnp.float32).reshape(z.shape[0], z.shape[1], N_HEADS, HEAD_DIM)

def hgrn_forget(z, lb):
    f = lb + (1.0 - lb) * jax.nn.sigmoid(z.astype(jnp.float32))
    return to_heads(1.0 - f), to_heads(jnp.log(f))

def flip(a):
    return a[:, ::-1]

def chunked_recurrence(q, k, v, logf, s0):
    bn, length, h, _ = q.shape
    dv = v.shape[-1]
    n = length // CHUNK

    def to_chunks(a):
        return a.reshape(bn, n, CHUNK, h, a.shape[-1]).transpose(1, 0, 3, 2, 4)

    causal = jnp.tril(jnp.ones((CHUNK, CHUNK), dtype=bool))

    def step(state, inp):
        qc, kc, vc, gc = inp
        b = jnp.cumsum(gc, axis=2)
        rel = jnp.where(causal[:, :, None], b[:, :, :, None, :] - b[:, :, None, :, :], -jnp.inf)
        scores = jnp.einsum('bhtd,bhsd,bhtsd->bhts', qc, kc, jnp.exp(rel))
        o = (jnp.einsum('bhts,bhsv->bhtv', scores, vc)
             + jnp.einsum('bhtd,bhdv->bhtv', qc * jnp.exp(b), state))
        b_end = b[:, :, -1:, :]
        state = (jnp.exp(b_end[:, :, 0, :])[..., None] * state
                 + jnp.einsum('bhsd,bhsv->bhdv', kc * jnp.exp(b_end - b), vc))
        return state, o

    s_fin, o = lax.scan(step, s0, (to_chunks(q), to_chunks(k), to_chunks(v), to_chunks(logf)))
    return o.transpose(1, 0, 3, 2, 4).reshape(bn, length, h, dv), s_fin

def final_state(k, v, logf, s0):
    b = jnp.cumsum(logf, axis=1)
    b_end = b[:, -1]
    return (jnp.exp(b_end)[..., None] * s0
            + jnp.einsum('blhd,blhv->bhdv', k * jnp.exp(b_end[:, None] - b), v))

def window_bounds(n, w):
    pos = jnp.arange(n)
    lo = jnp.clip(pos - w // 2, 0, n - 1)
    hi = jnp.clip(pos + w // 2 - 1, 0, n - 1) + 1
    return lo, hi

def centred_pool_residual(p, rows, cols, w):
    bn, length, ch = p.shape
    g = p.astype(jnp.float32).reshape(bn, rows, cols, ch)
    sat = jnp.pad(jnp.cumsum(jnp.cumsum(g, axis=1), axis=2), ((0, 0), (1, 0), (1, 0), (0, 0)))
    r0, r1 = window_bounds(rows, w)
    c0, c1 = window_bounds(cols, w)

    def corner(ri, ci):
        return sat[:, ri][:, :, ci]

    total = corner(r1, c1) - corner(r0, c1) - corner(r1, c0) + corner(r0, c0)
    count = ((r1 - r0)[:, None] * (c1 - c0)[None, :]).astype(jnp.float32)[None, :, :, None]
    return (total / count - g).reshape(bn, length, ch).astype(p.dtype)

def pool_branch(p, rows, cols, w_pool, pool_scale):
    outs = []
    for j, w in enumerate(POOL_WINDOWS):
        pj = p[..., j * POOL_GROUP:(j + 1) * POOL_GROUP]
        outs.append(centred_pool_residual(pj, rows, cols, w) @ w_pool[j])
    return jnp.concatenate(outs, axis=-1) * pool_scale

def merge_branches(o, z, rows, cols, hgrn_norm_g, w_a, w_pool, pool_scale, w_b, w_out):
    bn, length = z.shape[:2]
    o_gated = rms_norm(o, hgrn_norm_g).reshape(bn, length, HGRN_WIDTH).astype(z.dtype) * jax.nn.silu(z[..., OG_OFF:P_OFF])
    y_a = o_gated @ w_a
    y_b = pool_branch(z[..., P_OFF:GA_OFF], rows, cols, w_pool, pool_scale) @ w_b
    y = jax.nn.sigmoid(z[..., GA_OFF:GB_OFF]) * y_a + jax.nn.sigmoid(z[..., GB_OFF:IN_COLS]) * y_b
    return y @ w_out

def expert_choice_moe(u, w_router, w_e_gate, w_e_up, w_e_down):
    bn, n, _ = u.shape
    cap = CAPACITY_FACTOR * n // N_EXPERTS
    probs = jax.nn.softmax((u @ w_router).astype(jnp.float32), axis=-1)
    vals, idx = lax.top_k(jnp.swapaxes(probs, 1, 2), cap)
    bidx = jnp.arange(bn)[:, None, None]
    xg = u[bidx, idx]
    hid = jax.nn.silu(jnp.einsum('becd,edf->becf', xg, w_e_gate)) * jnp.einsum('becd,edf->becf', xg, w_e_up)
    y = jnp.einsum('becf,efd->becd', hid, w_e_down) * vals[..., None].astype(u.dtype)
    return jnp.zeros_like(u).at[bidx, idx].add(y)

def trunk_layer(hx, hc, c, c_ctx, lb_f, lb_b, w_mod, b_mod, norm1_g, w_in, hgrn_norm_g,
                w_a, w_pool, pool_scale, w_b, w_out, norm2_g, w_router, w_e_gate, w_e_up,
                w_e_down, rows, update_ctx):
    sh1x, sc1x, g1x, sh2x, sc2x, g2x = adaln(c[:, None, :], w_mod, b_mod)
    sh1c, sc1c, g1c, sh2c, sc2c, g2c = adaln(c_ctx, w_mod, b_mod)

    ux = modulate(rms_norm(hx, norm1_g), sh1x, sc1x)
    uc = modulate(rms_norm(hc, norm1_g), sh1c, sc1c)
    zx = ux @ w_in
    if update_ctx:
        zc = uc @ w_in
        zc_ifb = zc[..., I_OFF:OG_OFF]
    else:
        zc_ifb = uc @ w_in[:, I_OFF:OG_OFF]

    s0 = jnp.zeros((hc.shape[0], N_HEADS, HEAD_DIM, HEAD_DIM), jnp.float32)
    ic = to_heads(zc_ifb[..., :HGRN_WIDTH])
    kcf, gcf = hgrn_forget(zc_ifb[..., HGRN_WIDTH:2 * HGRN_WIDTH], lb_f)
    kcb, gcb = hgrn_forget(zc_ifb[..., 2 * HGRN_WIDTH:3 * HGRN_WIDTH], lb_b)
    if update_ctx:
        qc = to_heads(jax.nn.silu(zc[..., Q_OFF:I_OFF]))
        oc_f, sc_f = chunked_recurrence(qc, kcf, ic, gcf, s0)
        oc_b, sc_b = chunked_recurrence(flip(qc), flip(kcb), flip(ic), flip(gcb), s0)
        oc = oc_f + flip(oc_b)
    else:
        sc_f = final_state(kcf, ic, gcf, s0)
        sc_b = final_state(flip(kcb), flip(ic), flip(gcb), s0)

    qx = to_heads(jax.nn.silu(zx[..., Q_OFF:I_OFF]))
    ix = to_heads(zx[..., I_OFF:FF_OFF])
    kxf, gxf = hgrn_forget(zx[..., FF_OFF:FB_OFF], lb_f)
    kxb, gxb = hgrn_forget(zx[..., FB_OFF:OG_OFF], lb_b)
    ox_f, _ = chunked_recurrence(qx, kxf, ix, gxf, sc_f)
    ox_b, _ = chunked_recurrence(flip(qx), flip(kxb), flip(ix), flip(gxb), sc_b)
    ox = ox_f + flip(ox_b)

    new_hx = hx + g1x * merge_branches(ox, zx, rows, GRID_W, hgrn_norm_g, w_a, w_pool, pool_scale, w_b, w_out)
    if update_ctx:
        hc = hc + g1c * merge_branches(oc, zc, 1, hc.shape[1], hgrn_norm_g, w_a, w_pool, pool_scale, w_b, w_out)

    vx = modulate(rms_norm(new_hx, norm2_g), sh2x, sc2x)
    new_hx = new_hx + g2x * expert_choice_moe(vx, w_router, w_e_gate, w_e_up, w_e_down)
    if update_ctx:
        vc = modulate(rms_norm(hc, norm2_g), sh2c, sc2c)
        hc = hc + g2c * expert_choice_moe(vc, w_router, w_e_gate, w_e_up, w_e_down)
    return new_hx, hc

def setup_inputs(seed: int = 0) -> dict:
    key = jax.random.key(seed)
    ks = jax.random.split(key, 24)
    nrm = lambda k, shape, s: jax.random.normal(k, shape, jnp.float32) * s
    d = D_MODEL
    return {
        "x": nrm(ks[0], (BATCH, SEQ, d), 1.0),
        "c": nrm(ks[1], (BATCH, d), 1.0),
        "ctx": nrm(ks[2], (BATCH, CTX_LEN, d), 1.0),
        "c_ctx": nrm(ks[3], (d,), 1.0),
        "lb_logits": nrm(ks[4], (2, DEPTH + 1, HGRN_WIDTH), 0.5),
        "w_mod": nrm(ks[5], (DEPTH, d, 6 * d), 0.5 * d ** -0.5),
        "b_mod": nrm(ks[6], (DEPTH, 6 * d), 0.02),
        "norm1_g": 1.0 + nrm(ks[7], (DEPTH, d), 0.02),
        "w_in": nrm(ks[8], (DEPTH, d, IN_COLS), d ** -0.5),
        "hgrn_norm_g": 1.0 + nrm(ks[9], (DEPTH, HEAD_DIM), 0.02),
        "w_a": nrm(ks[10], (DEPTH, HGRN_WIDTH, d), HGRN_WIDTH ** -0.5),
        "w_pool": nrm(ks[11], (DEPTH, len(POOL_WINDOWS), POOL_GROUP, POOL_GROUP), POOL_GROUP ** -0.5),
        "pool_scale": 1.0 + nrm(ks[12], (DEPTH, POOL_WIDTH), 0.1),
        "w_b": nrm(ks[13], (DEPTH, POOL_WIDTH, d), POOL_WIDTH ** -0.5),
        "w_out": nrm(ks[14], (DEPTH, d, d), d ** -0.5),
        "norm2_g": 1.0 + nrm(ks[15], (DEPTH, d), 0.02),
        "w_router": nrm(ks[16], (DEPTH, d, N_EXPERTS), d ** -0.5),
        "w_e_gate": nrm(ks[17], (DEPTH, N_EXPERTS, d, EXPERT_FF), d ** -0.5),
        "w_e_up": nrm(ks[18], (DEPTH, N_EXPERTS, d, EXPERT_FF), d ** -0.5),
        "w_e_down": nrm(ks[19], (DEPTH, N_EXPERTS, EXPERT_FF, d), EXPERT_FF ** -0.5),
        "final_g": 1.0 + nrm(ks[20], (d,), 0.02),
    }

def reference(x, c, ctx, c_ctx, lb_logits, w_mod, b_mod, norm1_g, w_in, hgrn_norm_g, w_a,
              w_pool, pool_scale, w_b, w_out, norm2_g, w_router, w_e_gate, w_e_up, w_e_down,
              final_g):
    rows = x.shape[1] // GRID_W
    lb = jnp.cumsum(jax.nn.softmax(lb_logits.astype(jnp.float32), axis=1), axis=1)
    hx, hc = x, ctx
    for l in range(DEPTH):
        hx, hc = trunk_layer(hx, hc, c, c_ctx, lb[0, l], lb[1, l], w_mod[l], b_mod[l], norm1_g[l],
                             w_in[l], hgrn_norm_g[l], w_a[l], w_pool[l], pool_scale[l], w_b[l],
                             w_out[l], norm2_g[l], w_router[l], w_e_gate[l], w_e_up[l], w_e_down[l],
                             rows, l < DEPTH - 1)
    return rms_norm(hx, final_g)


_drawn_inputs = setup_inputs


def setup_inputs(seed=0):
    import zlib

    import numpy as np

    out = dict(_drawn_inputs(seed))
    spreads = {}
    factors = {'ctx': 8.0,
     'c_ctx': 8.0,
     'lb_logits': 8.0,
     'b_mod': 3.297,
     'norm1_g': 8.0,
     'hgrn_norm_g': 8.0,
     'pool_scale': 3.315,
     'norm2_g': 8.0,
     'final_g': 2.951}
    for name, (base, spread) in spreads.items():
        noise = np.random.default_rng([zlib.crc32(name.encode()), seed]).standard_normal(out[name].shape)
        drawn = base * np.exp(spread * noise) if base else spread * noise
        out[name] = __import__('jax').numpy.asarray(drawn.astype(out[name].dtype))
    for name, factor in factors.items():
        out[name] = (out[name] * factor).astype(out[name].dtype)
    return out
```

```python
from contextlib import ExitStack

import numpy as np

import concourse.bass as bass
from concourse import mybir

F32 = mybir.dt.float32
F32R = mybir.dt.float32r
I32 = mybir.dt.int32
U8 = mybir.dt.uint8
U32 = mybir.dt.uint32
ALU = mybir.AluOpType
ACT = mybir.ActivationFunctionType
AX = mybir.AxisListType

P = 128
D = 1024
T = 1024
TC = 256
TA = T + TC
KT = D // P
NT = T // P
NH = 8
NC = T // P
LEVELS = 7
GRID_W = 64
ROWS = T // GRID_W
WINDOWS = (2, 4, 8, 16)
NE = 16
CAP = 2 * T // NE
FF = 1024
EPS = 1e-6
N512 = 512

Q_OFF, I_OFF, FF_OFF, FB_OFF, OG_OFF = (j * D for j in range(5))
P_OFF = 5 * D
GA_OFF = P_OFF + P * len(WINDOWS)
GB_OFF = GA_OFF + D
IN_COLS = GB_OFF + D

R_BMOD, R_N1, R_N2, R_PS, R_HG, R_LB = 0, 48, 56, 64, 68, 69
N_PARAM = R_LB + 4 * NH


class Steps:

    def __init__(self, ctx, nc, name, steps, lead=1):
        self.sem = ctx.enter_context(nc.semaphore(name))
        self.n, self.lead = len(steps), lead
        self.credit = lead * self.n
        self.index = {s: i + 1 for i, s in enumerate(steps)}
        assert len(self.index) == self.n, name

    def after(self, it, step):
        return (it + self.lead) * self.n + self.index[step]


def matmul3(pe, out, w, x, start, stop):
    pe.matmul(out, w[0], x[0], start=start, stop=False)
    pe.matmul(out, w[0], x[1], start=False, stop=False)
    return pe.matmul(out, w[1], x[0], start=False, stop=stop)


def phase_modulate(nc, dram, keep, ux_head, ux_tail):
    NX = TA // P
    CH = 6 * D // N512
    WSLOTS = 3
    order = [0, 1, 2, 3, 6, 4, 7, 5, 8, 10, 9, 11]
    NBOTH = 4
    BATCH = NX // 2
    BY_ACT = 2
    with ExitStack() as ctx:
        def sb(name, shape, dt=F32):
            return ctx.enter_context(nc.sbuf_tensor(name, shape, dt))

        def psum(name, shape):
            return ctx.enter_context(nc.psum_tensor(name, shape, F32))

        def sem(name):
            return ctx.enter_context(nc.semaphore(name))

        prow = sb("prow", [P, P])
        cvec = sb("cvec", [P, 2, KT])
        csig = sb("csig", [P, 2, KT])
        csil = sb("csil", [P, KT, 2])
        cwide = sb("cwide", [P, KT, P])
        ones = sb("ones", [P, P])
        mod_rows = sb("mod_rows", [2, 2, N512])
        acc = sb("acc", [P, 2, N512])
        wmod = sb("wmod", [P, WSLOTS, KT, N512])
        xt = sb("xt", [P, NX, D])
        junk = sb("junk", [P, D])
        ssum = sb("ssum", [P, 16])
        mean = sb("mean", [P, 16])
        neghalf = sb("neghalf", [P, 16])
        rstd = sb("rstd", [P, 16])
        am = sb("am", [P, 16, 2])
        am2 = sb("am2", [P, 16])
        scale1 = sb("scale1", [P, 2, KT])
        lbd = sb("lbd", [P, 2, NH])
        ux = sb("ux", [P, 2, TA])
        ps_u = [psum(f"ps_u{i}", [P, 3, N512]) for i in range(2)]
        ps_col = psum("ps_col", [P, N512])
        ps_row = psum("ps_row", [P, N512])

        s_param = sem("a_param_landed")
        s_cvec = sem("a_cvec_landed")
        s_gate = sem("a_gate_bias_landed")
        s_wm = [sem(f"a_wmod_landed{i}") for i in range(WSLOTS)]
        s_x = [sem(f"a_x_landed{i}") for i in range(NX)]
        pe_cols = sem("a_pe_param_cols")
        pe_mod = sem("a_pe_mod_chunks")
        pe_turned = sem("a_pe_mod_rows_turned")
        pe_sum = sem("a_pe_weighed_summed")
        pe_ux = sem("a_pe_ux_tiles")
        act_cs = sem("a_act_csig")
        act_lb = sem("a_act_lb")
        act_ss = sem("a_act_sums")
        act_xn = sem("a_act_normalised")
        act_ux = sem("a_act_ux")
        v_set = sem("a_v_setup")
        v_norm = sem("a_v_norm")
        v_ux = sem("a_v_ux")
        v_gate = sem("a_v_gate")
        v_rows = sem("a_v_mod_rows")
        v_mean = sem("a_v_mean")
        v_scale1 = sem("a_v_scale1")
        v_acc = sem("a_v_weighed")
        v_chunk = sem("a_v_chunks")
        p_half = sem("a_pool_neghalf")
        p_rstd = sem("a_pool_rstd")

        cols, ident = keep["cols"], keep["ident"]
        scale2, shift2 = keep["scale2"], keep["shift2"]
        wm_v = dram["w_mod"].rearrange("a (p k) n -> (a p) k n", k=KT)

        block = ctx.enter_context(nc.Block())

        @block.sync
        def _(sp):
            sp.dma_start(ident[:], dram["ident"]).then_inc(s_param, 16)
            sp.dma_start(prow[R_BMOD:R_N1, :], dram["b_mod"].rearrange("a (m p) -> (a m) p", p=P)).then_inc(s_param, 16)
            sp.dma_start(prow[R_N1:R_N2, :], dram["norm1_g"].rearrange("a (m p) -> (a m) p", p=P)).then_inc(s_param, 16)
            sp.dma_start(prow[R_N2:R_PS, :], dram["norm2_g"].rearrange("a (m p) -> (a m) p", p=P)).then_inc(s_param, 16)
            sp.dma_start(prow[R_PS:R_HG, :], dram["pool_scale"].rearrange("a (m p) -> (a m) p", p=P)).then_inc(s_param, 16)
            sp.dma_start(prow[R_HG:R_LB, :], dram["hgrn_norm_g"]).then_inc(s_param, 16)
            sp.dma_start(prow[R_LB:N_PARAM, :], dram["lb_logits"].rearrange("a b (m p) -> (a b m) p", p=P)).then_inc(s_param, 16)
            sp.dma_start(cvec[:, 0, :], dram["c"].rearrange("a (p k) -> (a p) k", k=KT)).then_inc(s_cvec, 16)
            sp.dma_start(cvec[:, 1, :], dram["c_ctx"].rearrange("(p k) -> p k", k=KT)).then_inc(s_cvec, 16)

            def load_wmod(j):
                before = j - WSLOTS
                if before >= NBOTH and (before - NBOTH) % 2 == 0:
                    sp.wait_ge(v_chunk, (before - NBOTH) // 2 + 1)
                elif before >= 0:
                    sp.wait_ge(pe_mod, before + 1 if before < NBOTH else NBOTH + (before - NBOTH) // 2 + 1)
                n = order[j]
                sp.dma_start(wmod[:, j % WSLOTS, :, :], wm_v[:, :, n * N512:(n + 1) * N512]).then_inc(s_wm[j % WSLOTS], 16)

            for j in range(WSLOTS):
                load_wmod(j)
            for i in range(NX):
                src = dram["x"][0, i * P:(i + 1) * P, :] if i < NT else dram["ctx"][0, (i - NT) * P:(i - NT + 1) * P, :]
                sp.dma_start(xt[:, i, :], src).then_inc(s_x[i], 16)
            for g, off in ((0, 2 * D), (1, 5 * D)):
                sp.dma_start(keep["gates"][:, g, :], dram["b_mod"][0:1, off:off + D].broadcast_to([P, D])).then_inc(s_gate, 16)
            for j in range(WSLOTS, CH):
                load_wmod(j)

        @block.gpsimd
        def _(pool):
            pool.memset(neghalf[:], -0.5).then_inc(p_half, 1)
            pool.wait_ge(p_half, 1)
            for b in range(2):
                tiles = slice(b * BATCH, (b + 1) * BATCH)
                pool.wait_ge(v_mean, b + 1)
                pool.tensor_tensor(rstd[:, tiles], mean[:, tiles], neghalf[:, tiles], ALU.pow).then_inc(p_rstd, 1)

        @block.scalar
        def _(act):
            act.wait_ge(s_cvec, 32)
            act.activation(csig[:], cvec[:], ACT.Sigmoid).then_inc(act_cs, 1)
            act.wait_ge(v_set, 4)
            act.activation(keep["lb"][:], lbd[:], ACT.Sigmoid).then_inc(act_lb, 1)
            for i in range(NX):
                act.wait_ge(s_x[i], 16)
                if i:
                    act.wait_ge(act_ss, i)
                act.activation(junk[:], xt[:, i, :], ACT.Square, accum_out=ssum[:, i:i + 1]).then_inc(act_ss, 1)
            act.wait_ge(p_rstd, 2)
            for i in range(NX - BY_ACT, NX):
                act.activation(xt[:, i, :], xt[:, i, :], ACT.Copy, scale=rstd[:, i:i + 1]).then_inc(act_xn, 1)
            act.wait_ge(v_scale1, 1)
            for k in range(KT):
                act.wait_ge(pe_ux, k + 1)
                if k >= 2:
                    act.wait_ge(v_ux, 2 * (k - 1))
                for b in range(3):
                    side, width = (0, N512) if b < 2 else (1, TC)
                    last = act.activation(ux[:, k % 2, b * N512:b * N512 + width], ps_u[k % 2][:, b, 0:width], ACT.Identity,
                                          scale=scale1[:, side, k:k + 1], bias=am[:, k:k + 1, side])
                last.then_inc(act_ux, 1)

        @block.vector
        def _(v):
            v.wait_ge(act_cs, 1)
            for side in range(2):
                v.tensor_tensor(csil[:, :, side], cvec[:, side, :], csig[:, side, :], ALU.mult).then_inc(v_set, 1)
            v.wait_ge(pe_cols, 1)
            v.tensor_copy(cols[:, 0:N_PARAM], ps_col[:, 0:N_PARAM]).then_inc(v_set, 1)
            v.wait_ge(v_set, 3)
            lbl = cols[:, R_LB:N_PARAM].rearrange("p (a b m) -> p a b m", a=2, b=2)
            v.tensor_tensor(lbd[:], lbl[:, :, 0, :], lbl[:, :, 1, :], ALU.subtract).then_inc(v_set, 1)
            v.tensor_copy(cwide[:], csil[:, :, 0:1].broadcast_to([P, KT, P])).then_inc(v_set, 1)
            v.memset(ones[:], 1.0).then_inc(v_set, 1)
            v.wait_ge(act_lb, 1)
            v.tensor_scalar(keep["olb"][:], keep["lb"][:], -1.0, 1.0, ALU.mult, ALU.add).then_inc(v_set, 1)

            def take_rows(j):
                v.wait_ge(pe_mod, j + 1)
                if j >= 2:
                    v.wait_ge(pe_turned, j - 1)
                src = ps_u[1][0:2, j, :] if j < 3 else ps_row[0:2, :]
                v.tensor_copy(mod_rows[:, j % 2, :], src).then_inc(v_rows, 1)

            def means(b):
                tiles = slice(b * BATCH, (b + 1) * BATCH)
                v.wait_ge(act_ss, (b + 1) * BATCH)
                v.tensor_scalar(mean[:, tiles], ssum[:, tiles], 1.0 / D, EPS, ALU.mult, ALU.add).then_inc(v_mean, 1)

            def normalise(lo, hi):
                for i in range(lo, hi):
                    v.tensor_scalar(xt[:, i, :], xt[:, i, :], rstd[:, i:i + 1], None, ALU.mult).then_inc(v_norm, 1)

            for j in range(3):
                take_rows(j)
            means(0)
            v.wait_ge(p_rstd, 1)
            normalise(0, BATCH)
            means(1)
            v.wait_ge(p_rstd, 2)
            normalise(BATCH, NX - BY_ACT)
            take_rows(3)
            v.wait_ge(pe_turned, NBOTH)
            v.tensor_tensor(am[:, 0:16, :], ps_col[:, 0:32].rearrange("p (m s) -> p m s", s=2),
                            cols[:, 0:16].rearrange("p (m s) -> p m s", s=1).broadcast_to([P, 16, 2]), ALU.add).then_inc(v_set, 1)
            v.wait_ge(v_set, 8)
            for side in range(2):
                last = v.scalar_tensor_tensor(out=scale1[:, side, :], in0=am[:, KT:2 * KT, side], scalar=1.0,
                                              in1=cols[:, R_N1:R_N1 + KT], op0=ALU.add, op1=ALU.mult)
            last.then_inc(v_scale1, 1)

            weighed = 0

            def weigh(j):
                nonlocal weighed
                n = (j - NBOTH) // 2
                v.wait_ge(s_wm[j % WSLOTS], 16 * (j // WSLOTS + 1))
                if n >= 2:
                    v.wait_ge(pe_sum, n - 1)
                for k in range(KT):
                    src = wmod[:, j % WSLOTS, k, :]
                    if k == 0:
                        last = v.tensor_scalar(acc[:, n % 2, :], src, csil[:, k, 0:1], None, ALU.mult)
                    else:
                        v.wait_ge(v_acc, weighed)
                        last = v.scalar_tensor_tensor(out=acc[:, n % 2, :], in0=src, scalar=csil[:, k, 0:1],
                                                      in1=acc[:, n % 2, :], op0=ALU.mult, op1=ALU.add)
                    if k < KT - 1:
                        last.then_inc(v_acc, 1)
                        weighed += 1
                last.then_inc(v_chunk, 1)

            def gate_rows(n):
                v.wait_ge(pe_mod, NBOTH + n + 1)
                if n == 0:
                    v.wait_ge(s_gate, 32)
                g, h = divmod(n, 2)
                dst = keep["gates"][:, g, h * N512:(h + 1) * N512]
                v.tensor_tensor(dst, ps_row[:], dst, ALU.add).then_inc(v_gate, 1)

            for k in range(KT):
                v.wait_ge(act_ux, k + 1)
                v.tensor_copy(ux_head[:, k, :], ux[:, k % 2, :]).then_inc(v_ux, 1)
                v.wait_ge(v_ux, 2 * k + 1)
                v.tensor_tensor(ux_tail[:, k, :], ux[:, k % 2, :], ux_head[:, k, :].bitcast(F32), ALU.subtract).then_inc(v_ux, 1)
                if k % 2 == 1:
                    if k > 1:
                        gate_rows(k // 2 - 1)
                    weigh(NBOTH + k - 1)
            gate_rows(KT // 2 - 1)
            v.wait_ge(pe_sum, NBOTH)
            v.tensor_tensor(am2[:], ps_col[:, 32:48], cols[:, 24:40], ALU.add).then_inc(v_set, 1)
            v.wait_ge(v_set, 9)
            v.tensor_copy(shift2[:], am2[:, 0:8]).then_inc(v_set, 1)
            v.scalar_tensor_tensor(out=scale2[:], in0=am2[:, 8:16], scalar=1.0,
                                   in1=cols[:, R_N2:R_N2 + KT], op0=ALU.add, op1=ALU.mult).then_inc(v_set, 1)

        @block.tensor
        def _(pe):
            pe.wait_ge(s_param, 7 * 16)
            pe.transpose(ps_col[:, 0:N_PARAM], prow[0:N_PARAM, :], ident[0:N_PARAM, 0:N_PARAM]).then_inc(pe_cols, 1)

            def both_rows(j):
                pe.wait_ge(s_wm[j % WSLOTS], 16 * (j // WSLOTS + 1))
                dst = ps_u[1][0:2, j, :] if j < 3 else ps_row[0:2, :]
                for k in range(KT):
                    last = pe.matmul(dst, csil[:, k, :], wmod[:, j % WSLOTS, k, :], start=(k == 0), stop=(k == KT - 1))
                last.then_inc(pe_mod, 1)

            def turn_rows(j):
                pe.wait_ge(v_rows, j + 1)
                for m in range(4):
                    at = 2 * (4 * j + m)
                    last = pe.transpose(ps_col[:, at:at + 2], mod_rows[:, j % 2, m * P:(m + 1) * P], ident[0:2, 0:2])
                last.then_inc(pe_turned, 1)

            def gate_rows(n):
                j = NBOTH + 2 * n + 1
                pe.wait_ge(s_wm[j % WSLOTS], 16 * (j // WSLOTS + 1))
                if n:
                    pe.wait_ge(v_gate, n)
                for k in range(KT):
                    last = pe.matmul(ps_row[:], cwide[:, k, :], wmod[:, j % WSLOTS, k, :], start=(k == 0), stop=(k == KT - 1))
                last.then_inc(pe_mod, 1)

            def sum_weighed(n):
                pe.wait_ge(v_chunk, n + 1)
                for m in range(4):
                    at = 32 + 4 * n + m
                    last = pe.matmul(ps_col[:, at:at + 1], acc[:, n % 2, m * P:(m + 1) * P], ones[:, 0:1], start=True, stop=True)
                last.then_inc(pe_sum, 1)

            pe.wait_ge(v_set, 6)
            both_rows(0)
            both_rows(1)
            turn_rows(0)
            both_rows(2)
            turn_rows(1)
            turn_rows(2)
            both_rows(3)
            pe.wait_ge(v_norm, NX - BY_ACT)
            pe.wait_ge(act_xn, BY_ACT)
            for k in range(KT):
                if k >= 2:
                    pe.wait_ge(act_ux, k - 1)
                if k == 1:
                    turn_rows(3)
                for i in range(NX):
                    last = pe.transpose(ps_u[k % 2][:, i // 4, (i % 4) * P:(i % 4 + 1) * P], xt[:, i, k * P:(k + 1) * P], ident[:])
                last.then_inc(pe_ux, 1)
                if k % 2 == 1:
                    gate_rows(k // 2)
                    if k == 3:
                        pe.wait_ge(v_set, 8)
                    if k > 1:
                        sum_weighed(k // 2 - 1)
            sum_weighed(KT // 2 - 1)


def phase_pool_gates(nc, dram, keep, ux_head, ux_tail):
    NG = len(WINDOWS)
    PAD = max(WINDOWS) // 2
    with ExitStack() as ctx:
        def sb(name, shape, dt=F32):
            return ctx.enter_context(nc.sbuf_tensor(name, shape, dt))

        def psum(name, shape):
            return ctx.enter_context(nc.psum_tensor(name, shape, F32))

        def sem(name):
            return ctx.enter_context(nc.semaphore(name))

        w_raw = sb("b_w_raw", [P, 2, KT, P])
        w_head = sb("b_w_head", [P, 2, KT, P], F32R)
        w_tail = sb("b_w_tail", [P, 2, KT, P], F32R)
        wpool = sb("b_wpool", [P, NG, P])
        icount = sb("b_icount", [P, NG, T])
        colpad = sb("b_colpad", [P, ROWS, GRID_W + 2 * PAD])
        colsum = [sb(f"b_colsum{i}", [P, ROWS, GRID_W + 2 * PAD]) for i in range(2)]
        rowpad = sb("b_rowpad", [P, ROWS + 2 * PAD, GRID_W])
        rowsum = [sb(f"b_rowsum{i}", [P, ROWS + 2 * PAD, GRID_W]) for i in range(2)]
        resid = sb("b_resid", [P, 2, T])
        yb = sb("b_yb", [P, 2, T])
        zero = sb("b_zero", [P, 1])
        gate = sb("b_gate", [P, 2, T])
        ps_z = [psum(f"b_ps_z{i}", [P, T]) for i in range(2)]
        ps_y = psum("b_ps_y", [P, T])

        s_raw = [sem(f"b_w_landed{i}") for i in range(2)]
        s_const = sem("b_const_landed")
        s_yb = [sem(f"b_yb_stored{i}") for i in range(2)]
        s_gate = [sem(f"b_gate_stored{i}") for i in range(2)]
        pool_head = sem("b_pool_head")
        pool_tail = sem("b_pool_tail")
        pool_zero = sem("b_pool_zero")
        pe_block = sem("b_pe_block")
        pe_y = sem("b_pe_y")
        v_pool = sem("b_v_pooling")
        v_taken = sem("b_v_taken")
        v_resid = sem("b_v_resid")
        act_y = sem("b_act_y")
        act_gate = sem("b_act_gate")
        cols = keep["cols"]
        w_in = dram["w_in"].rearrange("a (k p) n -> p (a k) n", p=P)

        block = ctx.enter_context(nc.Block())

        @block.sync
        def _(sp):
            def load(n, src):
                sp.dma_start(w_raw[:, n % 2, :, :], src).then_inc(s_raw[n % 2], 16)

            for n in range(NG):
                if n >= 2:
                    sp.wait_ge(pool_tail, n - 1)
                load(n, w_in[:, :, P_OFF + n * P:P_OFF + (n + 1) * P])
                if n == 1:
                    sp.dma_start(wpool[:], dram["w_pool"].rearrange("a j ci co -> ci (a j) co")).then_inc(s_const, 16)
                    sp.dma_start(icount[:], dram["icount"].broadcast_to([P, NG, T])).then_inc(s_const, 16)
            with sp.Fori(0, KT) as m:
                for g, off in ((0, GA_OFF), (1, GB_OFF)):
                    at = sp.snap(off + m * P)
                    sp.wait_ge(pool_tail, NG + 2 * m + g - 1)
                    load(NG + g, w_in[:, :, bass.ds(at, P)])

        @block.gpsimd
        def _(pool):
            pool.memset(colpad[:], 0.0).then_inc(pool_zero, 1)
            pool.memset(rowpad[:], 0.0).then_inc(pool_zero, 1)
            pool.memset(zero[:], 0.0).then_inc(pool_zero, 1)
            pool.wait_ge(pool_zero, 3)

            def split(n, slot, landed):
                pool.wait_ge(s_raw[slot], landed)
                if not (isinstance(n, int) and n < 2):
                    pool.wait_ge(pe_block, n - 1)
                pool.tensor_tensor(w_head[:, slot], w_raw[:, slot], zero[:].unsqueeze(2).broadcast_to([P, KT, P]), ALU.add).then_inc(pool_head, 1)
                pool.wait_ge(pool_head, n + 1)
                pool.tensor_tensor(w_tail[:, slot], w_raw[:, slot], w_head[:, slot].bitcast(F32), ALU.subtract).then_inc(pool_tail, 1)

            for n in range(NG):
                split(n, n % 2, 16 * (n // 2 + 1))
            with pool.Fori(0, KT) as m:
                for g in range(2):
                    split(NG + 2 * m + g, g, 16 * (NG // 2 + 1) + 16 * m)

        @block.tensor
        def _(pe):
            def project(n, slot):
                pe.wait_ge(pool_tail, n + 1)
                for half in range(2):
                    for k in range(KT):
                        last = matmul3(pe, ps_z[slot][:, half * N512:(half + 1) * N512],
                                       (w_head[:, slot, k, :], w_tail[:, slot, k, :]),
                                       (ux_head[:, k, half * N512:(half + 1) * N512], ux_tail[:, k, half * N512:(half + 1) * N512]),
                                       k == 0, k == KT - 1)
                last.then_inc(pe_block, 1)

            def pool_product(j):
                pe.wait_ge(v_resid, j + 1)
                if j >= 1:
                    pe.wait_ge(act_y, j)
                if j == 0:
                    pe.wait_ge(s_const, 32)
                for half in range(2):
                    last = pe.matmul(ps_y[:, half * N512:(half + 1) * N512], wpool[:, j, :],
                                     resid[:, j % 2, half * N512:(half + 1) * N512], start=True, stop=True)
                last.then_inc(pe_y, 1)

            for n in range(NG):
                if n >= 2:
                    pe.wait_ge(v_taken, n - 1)
                project(n, n % 2)
                if n >= 2:
                    pool_product(n - 2)
            pe.wait_ge(v_taken, NG)
            with pe.Fori(0, KT) as m:
                for g in range(2):
                    pe.wait_ge(act_gate, 2 * m + g + 1)
                    project(NG + 2 * m + g, g)
            pool_product(NG - 2)
            pool_product(NG - 1)

        @block.scalar
        def _(act):
            act.sem_inc(act_gate, 2)

            def scale_y(j):
                act.wait_ge(pe_y, j + 1)
                if j >= 2:
                    act.wait_ge(s_yb[j % 2], 16 * (j // 2))
                act.activation(yb[:, j % 2, :], ps_y[:], ACT.Copy, scale=cols[:, R_PS + j:R_PS + j + 1]).then_inc(act_y, 1)
                act.wait_ge(act_y, j + 1)
                act.dma_start(dram["yb"][j * P:(j + 1) * P, :], yb[:, j % 2, :]).then_inc(s_yb[j % 2], 16)

            scale_y(0)
            scale_y(1)
            with act.Fori(0, KT) as m:
                for g in range(2):
                    act.wait_ge(pe_block, NG + 2 * m + g + 1)
                    act.wait_ge(s_gate[g], 16 * (m + 1))
                    act.activation(gate[:, g, :], ps_z[g][:], ACT.Sigmoid).then_inc(act_gate, 1)
                    act.wait_ge(act_gate, 2 * m + g + 3)
                    act.dma_start(dram["gates"][g, bass.ds(m * P, P), :], gate[:, g, :]).then_inc(s_gate[g], 16)
            scale_y(2)
            scale_y(3)
            for g in range(2):
                act.wait_ge(s_gate[g], 16 * (KT + 1))
                act.wait_ge(s_yb[g], 32)

        @block.vector
        def _(v):
            for g in range(2):
                v.sem_inc(s_gate[g], 16)
            v.wait_ge(pool_zero, 2)
            v.wait_ge(s_const, 32)
            done = 0
            for j, w in enumerate(WINDOWS):
                v.wait_ge(pe_block, j + 1)
                v.tensor_copy(colpad[:, :, PAD:PAD + GRID_W], ps_z[j % 2][:].rearrange("p (r c) -> p r c", c=GRID_W)).then_inc(v_taken, 1)
                v.wait_ge(v_taken, j + 1)
                src, span, base, turn = colpad, 1, PAD - w // 2, 0
                while span < w:
                    last_step = 2 * span == w
                    width = GRID_W + w - 2 * span
                    dst = rowpad[:, PAD:PAD + ROWS, :] if last_step else colsum[turn][:, :, 0:width]
                    v.tensor_tensor(dst, src[:, :, base:base + width], src[:, :, base + span:base + span + width], ALU.add).then_inc(v_pool, 1)
                    done += 1
                    v.wait_ge(v_pool, done)
                    src, base, turn = colsum[turn], 0, 1 - turn
                    span *= 2
                src, span, base, turn = rowpad, 1, PAD - w // 2, 0
                while span < w:
                    height = ROWS + w - 2 * span
                    dst = rowsum[turn]
                    v.tensor_tensor(dst[:, 0:height, :], src[:, base:base + height, :], src[:, base + span:base + span + height, :],
                                    ALU.add).then_inc(v_pool, 1)
                    done += 1
                    v.wait_ge(v_pool, done)
                    src, base, turn = dst, 0, 1 - turn
                    span *= 2
                total = src[:, 0:ROWS, :].rearrange("p r c -> p (r c)")
                v.tensor_tensor(rowsum[turn][:, 0:ROWS, :].rearrange("p r c -> p (r c)"), total, icount[:, j, :], ALU.mult).then_inc(v_pool, 1)
                done += 1
                v.wait_ge(v_pool, done)
                if j >= 2:
                    v.wait_ge(pe_y, j - 1)
                v.tensor_tensor(resid[:, j % 2, :].rearrange("p (r c) -> p r c", c=GRID_W), rowsum[turn][:, 0:ROWS, :],
                                colpad[:, :, PAD:PAD + GRID_W], ALU.subtract).then_inc(v_resid, 1)
                v.wait_ge(v_resid, j + 1)


def pair_view(t, level, cols, first):
    half = 1 << level
    step = (cols if first == 0 else -cols) + half
    return [[2 * half, cols // (2 * half)], [step, 2], [1, half]], first * cols, t


def pair_ap(t, level, first, lo=0, n=T):
    dims, base, tile = pair_view(t, level, T, first)
    dims[0][1] = n // dims[0][0]
    return bass.AP(tile, base + lo, [[2 * T, P]] + dims)


def total_ap(t, level, width, plane0, entry0, entry1):
    n = T >> level
    other = 1 - plane0
    step = (other - plane0) * n + entry1 - entry0
    return bass.AP(t, plane0 * n + entry0, [[2 * width, P], [2, n // 2], [step, 2], [0, 1 << level]])


def phase_heads(nc, dram, keep, ux_head, ux_tail):
    TASKS = ["q0", "q1", "a0", "a1", "b0", "b1", "c", "v0", "v1", "vc", "g0", "g1"]
    BLOCKS = [Q_OFF, FF_OFF, FB_OFF, I_OFF, OG_OFF]
    HALVES = 2 * len(BLOCKS)
    RING = 5
    LAST_USE = ["q1", "c", "c", "vc", "g1"]
    with ExitStack() as ctx:
        def sb(name, shape, dt=F32):
            return ctx.enter_context(nc.sbuf_tensor("h_" + name, shape, dt))

        def psum(name, shape):
            return ctx.enter_context(nc.psum_tensor("h_ps_" + name, shape, F32))

        def sem(name):
            return ctx.enter_context(nc.semaphore("h_" + name))

        w_raw = sb("w_raw", [P, RING, KT // 2, P])
        w_head = sb("w_head", [P, RING, KT // 2, P], F32R)
        w_tail = sb("w_tail", [P, RING, KT // 2, P], F32R)
        masks = sb("masks", [P, LEVELS, P], U8)
        sig = sb("sig", [P, N512])
        q_next = sb("q_next", [P, T])
        f_next = sb("f_next", [P, 2, TA])
        v_next = sb("v_next", [P, NC + TC // P, P])
        og_gate = sb("og_gate", [P, T])
        v_tok = sb("v_tok", [P, NC + TC // P, P])
        tot = [sb("tot_even", [P, 2, T]), sb("tot_odd", [P, 2, T // 2])]
        q2 = sb("q2", [P, 2, T])
        k2 = sb("k2", [P, 2, T])
        stage = sb("stage", [P, T])
        reach = sb("reach", [P, 2, TC])
        kc_tok = sb("kc_tok", [P, 2, TC // P, P])
        scores = sb("scores", [P, NC, P])
        k_tok = sb("k_tok", [P, NC, P])
        out = sb("out", [P, T])
        masks_wide = out[:, 0:LEVELS * P].bitcast(I32).rearrange("p (l t) -> p l t", t=P)
        state = sb("state", [P, 2, NC, P])
        zeros = sb("zeros", [P, TC])
        junk = sb("junk", [P, P])
        sumsq = sb("sumsq", [P, NC])
        meansq = sb("meansq", [P, NC])
        neghalf = sb("neghalf", [P, NC])
        rstd = sb("rstd", [P, NC])
        ps_z = psum("z", [P, 2, N512])
        ps_x = psum("x", [P, NC, P])
        ps_o = psum("o", [P, NC, P])
        ps_w = psum("w", [P, NC, P])

        s_raw = [sem(f"w_landed{i}") for i in range(RING)]
        s_mask = sem("masks_landed")
        s_out = sem("out_stored")
        s_zero = sem("constants_set")
        pe_z = Steps(ctx, nc, "h_pe_z", TASKS)
        act_z = Steps(ctx, nc, "h_act_z", TASKS)
        v_z = Steps(ctx, nc, "h_v_z", ["q0", "q1", "g0", "g1"])
        pool_w = Steps(ctx, nc, "h_pool_w", [f"{part}{n}" for n in range(HALVES) for part in ("head", "tail")])
        pe_r = Steps(ctx, nc, "h_pe_r", ["diag", "kc", "level0", "s0"] + [f"level{l}" for l in range(1, LEVELS)] +
                     ["kf", "uf", "kb", "ub", "o", "ot"])
        act_r = Steps(ctx, nc, "h_act_r", ["pairs0", "diag", "kc"] + [f"pairs{l}" for l in range(1, LEVELS)] +
                      ["kf", "kb"] + [f"sq{c}" for c in range(NC)] + ["scaled"])
        v_p = Steps(ctx, nc, "h_v_p", ["f0", "f1", "keys", "queries", "ksum", "fc0", "fc1", "reach", "kc", "krc"])
        level_steps = [[f"{s}{l}" for s in ("k", "q", "t", "p")] for l in range(LEVELS)]
        v_r = Steps(ctx, nc, "h_v_r", level_steps[0] + ["s0"] + sum(level_steps[1:], []) +
                    [f"sf{c}" for c in range(NC - 1)] + [f"sb{c}" for c in range(NC - 1)] + ["mean", "out"])
        pool_v = Steps(ctx, nc, "h_pool_v", ["v"])
        pool_r = Steps(ctx, nc, "h_pool_r", ["rstd"])

        cols, ident, lb, olb = keep["cols"], keep["ident"], keep["lb"], keep["olb"]
        w_in = dram["w_in"].rearrange("a (k p) n -> p (a k) n", p=P)

        block = ctx.enter_context(nc.Block())

        @block.sync
        def _(sp):
            sp.dma_start(masks_wide, dram["masks"]).then_inc(s_mask, 16)

            def load_weights(g):
                for n in range(HALVES):
                    at = sp.snap(BLOCKS[n // 2] + g * P) if not isinstance(g, int) else BLOCKS[n // 2] + g * P
                    k0 = (n % 2) * (KT // 2)
                    before = n - RING
                    sp.wait_ge(pool_w.sem, pool_w.after(g, f"tail{before}") if before >= 0 else pool_w.after(g - 1, f"tail{before + HALVES}"))
                    sp.dma_start(w_raw[:, n % RING], w_in[:, k0:k0 + KT // 2, bass.ds(at, P)]).then_inc(s_raw[n % RING], 16)

            load_weights(0)
            with sp.Fori(1, NH) as g:
                load_weights(g)

        @block.gpsimd
        def _(pool):
            pool.sem_inc(pool_w.sem, pool_w.credit)
            pool.sem_inc(pool_r.sem, pool_r.credit)
            pool.sem_inc(pool_v.sem, pool_v.credit)
            pool.memset(neghalf[:], -0.5).then_inc(s_zero, 1)
            pool.memset(zeros[:], 0.0).then_inc(s_zero, 1)
            pool.memset(reach[:], 1.0).then_inc(s_zero, 1)
            pool.wait_ge(s_zero, 3)

            def split(g, n):
                slot = n % RING
                pool.wait_ge(s_raw[slot], 32 * g + 16 * (n // RING + 1))
                before = n - RING
                pool.wait_ge(pe_z.sem, pe_z.after(g, LAST_USE[before // 2]) if before >= 0
                             else pe_z.after(g - 1, LAST_USE[(before + HALVES) // 2]))
                pool.tensor_tensor(w_head[:, slot], w_raw[:, slot], zeros[:, 0:1].unsqueeze(2).broadcast_to([P, KT // 2, P]), ALU.add).then_inc(pool_w.sem, 1)
                pool.wait_ge(pool_w.sem, pool_w.after(g, f"head{n}"))
                pool.tensor_tensor(w_tail[:, slot], w_raw[:, slot], w_head[:, slot].bitcast(F32), ALU.subtract).then_inc(pool_w.sem, 1)

            def copy_values(h):
                pool.wait_ge(act_z.sem, act_z.after(h, "vc"))
                pool.wait_ge(pe_r.sem, pe_r.after(h - 1, "o"))
                pool.tensor_tensor(v_tok[:], v_next[:], zeros[:, 0:1].unsqueeze(2).broadcast_to([P, NC + TC // P, P]), ALU.add).then_inc(pool_v.sem, 1)

            def head(h, g):
                if g is not None:
                    for n in range(HALVES):
                        split(g, n)
                pool.wait_ge(v_r.sem, v_r.after(h, "mean"))
                pool.tensor_tensor(rstd[:], meansq[:], neghalf[:], ALU.pow).then_inc(pool_r.sem, 1)
                if g is not None:
                    copy_values(g)

            for n in range(HALVES):
                split(0, n)
            copy_values(0)
            with pool.Fori(0, NH - 1) as h:
                head(h, h + 1)
            head(NH - 1, None)

        @block.tensor
        def _(pe):
            pe.sem_inc(pe_z.sem, pe_z.credit)
            pe.sem_inc(pe_r.sem, pe_r.credit)
            def weights(b, k):
                n = 2 * b + k // (KT // 2)
                return w_head[:, n % RING, k % (KT // 2), :], w_tail[:, n % RING, k % (KT // 2), :]

            def tokens(k, lo, n):
                return ux_head[:, k, lo:lo + n], ux_tail[:, k, lo:lo + n]

            def features(out_ap, b, lo, n):
                for k in range(KT):
                    last = matmul3(pe, out_ap, weights(b, k), tokens(k, lo, n), k == 0, k == KT - 1)
                return last

            def task(g, name):
                i = TASKS.index(name)
                bank = ps_z[:, i % 2, :]
                prev = TASKS[i - 2]
                at = g if i >= 2 else g - 1
                if prev in v_z.index:
                    pe.wait_ge(v_z.sem, v_z.after(at, prev))
                else:
                    pe.wait_ge(act_z.sem, act_z.after(at, prev))
                b = {"q": [0], "a": [1], "b": [2], "c": [1, 2], "v": [3], "g": [4]}[name[0]]
                pe.wait_ge(pool_w.sem, pool_w.after(g, f"tail{2 * b[-1] + 1}"))
                if name in ("q0", "a0", "b0", "g0"):
                    last = features(bank, b[0], 0, N512)
                elif name in ("q1", "a1", "b1", "g1"):
                    last = features(bank, b[0], N512, N512)
                elif name == "c":
                    for j in range(2):
                        last = features(bank[:, j * TC:(j + 1) * TC], b[j], T, TC)
                else:
                    t0, nt = {"v0": (0, 4), "v1": (4, 4), "vc": (8, 2)}[name]
                    for j in range(nt):
                        for k in range(KT):
                            last = matmul3(pe, bank[:, j * P:(j + 1) * P], tokens(k, (t0 + j) * P, P), weights(3, k), k == 0, k == KT - 1)
                last.then_inc(pe_z.sem, 1)

            def recur_context_keys(h):
                pe.wait_ge(v_p.sem, v_p.after(h, "krc"))
                pe.wait_ge(act_r.sem, act_r.after(h - 1, "scaled"))
                pe.wait_ge(v_r.sem, v_r.after(h - 1, "out"))
                for d in range(2):
                    for t in range(TC // P):
                        last = pe.transpose(ps_w[:, 2 * d + t, :], f_next[:, d, T + t * P:T + (t + 1) * P], ident[:])
                last.then_inc(pe_r.sem, 1)

            def recur_diagonal(h):
                pe.wait_ge(v_p.sem, v_p.after(h, "ksum"))
                pe.wait_ge(v_r.sem, v_r.after(h - 1, f"sb{NC - 2}"))
                for c in range(NC):
                    last = pe.matmul(ps_x[:, c, :], k_tok[:, c, :], q_next[:, c * P:(c + 1) * P], start=True, stop=True)
                last.then_inc(pe_r.sem, 1)

            def recur_start_state(h):
                pe.wait_ge(act_r.sem, act_r.after(h, "kc"))
                pe.wait_ge(pool_v.sem, pool_v.after(h, "v"))
                for d in range(2):
                    for t in range(TC // P):
                        last = pe.matmul(ps_w[:, 4 + d, :], kc_tok[:, d, t, :], v_tok[:, NC + t, :], start=(t == 0), stop=(t == TC // P - 1))
                last.then_inc(pe_r.sem, 1)

            def recur_level(h, l):
                if l == 0:
                    pe.wait_ge(act_r.sem, act_r.after(h, "diag"))
                else:
                    pe.wait_ge(act_r.sem, act_r.after(h, f"pairs{l}"))
                    pe.wait_ge(v_r.sem, v_r.after(h, f"p{l - 1}"))
                for c in range(NC):
                    last = pe.matmul(ps_x[:, c, :], stage[:, c * P:(c + 1) * P], pair_ap(q2, l, 0, c * P, P), start=True, stop=True)
                last.then_inc(pe_r.sem, 1)

            def recur_keys(h, plane):
                if plane == 0:
                    pe.wait_ge(v_r.sem, v_r.after(h, f"k{LEVELS - 1}"))
                    pe.wait_ge(v_r.sem, v_r.after(h, "s0"))
                else:
                    pe.wait_ge(act_r.sem, act_r.after(h, "kf"))
                for c in range(NC):
                    last = pe.transpose(ps_w[:, c, :], k2[:, plane, c * P:(c + 1) * P], ident[:])
                last.then_inc(pe_r.sem, 1)

            def recur_updates(h, plane):
                if plane == 0:
                    pe.wait_ge(act_r.sem, act_r.after(h, "kf"))
                    pe.wait_ge(v_r.sem, v_r.after(h, f"p{LEVELS - 1}"))
                else:
                    pe.wait_ge(act_r.sem, act_r.after(h, "kb"))
                    pe.wait_ge(v_r.sem, v_r.after(h, f"sf{NC - 2}"))
                for c in range(NC):
                    last = pe.matmul(ps_x[:, c, :], k_tok[:, c, :], v_tok[:, c, :], start=True, stop=True)
                last.then_inc(pe_r.sem, 1)

            def recur_output(h):
                pe.wait_ge(v_r.sem, v_r.after(h, f"sb{NC - 2}"))
                pe.wait_ge(act_r.sem, act_r.after(h - 1, "scaled"))
                for c in range(NC):
                    pe.matmul(ps_o[:, c, :], scores[:, c, :], v_tok[:, c, :], start=True, stop=False)
                    pe.matmul(ps_o[:, c, :], q2[:, 1, c * P:(c + 1) * P], state[:, 0, c, :], start=False, stop=False)
                    last = pe.matmul(ps_o[:, c, :], q2[:, 0, c * P:(c + 1) * P], state[:, 1, c, :], start=False, stop=True)
                last.then_inc(pe_r.sem, 1)

            def recur_turn(h):
                pe.wait_ge(act_r.sem, act_r.after(h, "scaled"))
                for c in range(NC):
                    last = pe.transpose(ps_w[:, c, :], stage[:, c * P:(c + 1) * P], ident[:])
                last.then_inc(pe_r.sem, 1)

            def head(h, g):
                def t(name):
                    if g is not None:
                        task(g, name)

                recur_diagonal(h)
                recur_context_keys(h)
                recur_level(h, 0)
                recur_start_state(h)
                for l, name in enumerate(("q0", "q1", "a0", "a1", "b0", "b1"), 1):
                    t(name)
                    recur_level(h, l)
                t("c")
                recur_keys(h, 0)
                t("v0")
                recur_updates(h, 0)
                recur_keys(h, 1)
                t("v1")
                recur_updates(h, 1)
                t("vc")
                recur_output(h)
                t("g0")
                t("g1")
                recur_turn(h)

            for name in TASKS:
                task(0, name)
            with pe.Fori(0, NH - 1) as h:
                head(h, h + 1)
            head(NH - 1, None)

        @block.scalar
        def _(act):
            act.sem_inc(act_z.sem, act_z.credit)
            act.sem_inc(act_r.sem, act_r.credit)

            def evacuate(g, name):
                i = TASKS.index(name)
                bank = ps_z[:, i % 2, :]
                act.wait_ge(pe_z.sem, pe_z.after(g, name))
                if name[0] in "qg":
                    prev = {"q0": ("g1", 1), "q1": ("q0", 0), "g0": ("q1", 0), "g1": ("g0", 0)}[name]
                    act.wait_ge(v_z.sem, v_z.after(g - prev[1] if prev[1] else g, prev[0]))
                    last = act.activation(sig[:], bank, ACT.Sigmoid)
                elif name[0] in "ab":
                    d, half = "ab".index(name[0]), int(name[1])
                    last = act.activation(f_next[:, d, half * N512:(half + 1) * N512], bank, ACT.Sigmoid)
                elif name == "c":
                    act.wait_ge(pe_r.sem, pe_r.after(g - 1, "kc"))
                    last = act.activation(f_next[:, :, T:TA], bank.rearrange("p (d t) -> p d t", d=2), ACT.Sigmoid)
                else:
                    t0, nt = {"v0": (0, 4), "v1": (4, 4), "vc": (8, 2)}[name]
                    act.wait_ge(pool_v.sem, pool_v.after(g - 1, "v"))
                    last = act.activation(v_next[:, t0:t0 + nt, :], bank[:, 0:nt * P].rearrange("p (t d) -> p t d", d=P), ACT.Copy)
                last.then_inc(act_z.sem, 1)

            def gather_pairs(h, l):
                if l == 0:
                    act.wait_ge(v_p.sem, v_p.after(h, "keys"))
                    act.wait_ge(pe_r.sem, pe_r.after(h - 1, "ot"))
                else:
                    act.wait_ge(v_r.sem, v_r.after(h, f"k{l - 1}"))
                act.activation(stage[:], pair_ap(k2, l, 0), ACT.Copy).then_inc(act_r.sem, 1)

            def head(h, g):
                def t(name):
                    if g is not None:
                        evacuate(g, name)

                gather_pairs(h, 0)
                act.wait_ge(pe_r.sem, pe_r.after(h, "diag"))
                act.activation(scores[:], ps_x[:], ACT.Copy).then_inc(act_r.sem, 1)
                act.wait_ge(pe_r.sem, pe_r.after(h, "kc"))
                act.activation(kc_tok[:].rearrange("p d t f -> p (d t) f"), ps_w[:, 0:4, :], ACT.Copy).then_inc(act_r.sem, 1)
                evacuate(h, "g1")
                if not isinstance(h, int) or h >= 1:
                    store(h - 1)
                for l, name in enumerate(("q0", "q1", "a0", "a1", "b0", "b1"), 1):
                    gather_pairs(h, l)
                    t(name)
                t("c")
                act.wait_ge(pe_r.sem, pe_r.after(h, "kf"))
                act.activation(k_tok[:], ps_w[:], ACT.Copy).then_inc(act_r.sem, 1)
                t("v0")
                act.wait_ge(pe_r.sem, pe_r.after(h, "kb"))
                act.activation(k_tok[:], ps_w[:], ACT.Copy).then_inc(act_r.sem, 1)
                t("v1")
                t("vc")
                act.wait_ge(pe_r.sem, pe_r.after(h, "o"))
                for c in range(NC):
                    act.wait_ge(act_r.sem, act_r.after(h, f"sq{c - 1}" if c else "kb"))
                    act.activation(junk[:], ps_o[:, c, :], ACT.Square, accum_out=sumsq[:, c:c + 1]).then_inc(act_r.sem, 1)
                act.wait_ge(pool_r.sem, pool_r.after(h, "rstd"))
                for c in range(NC):
                    last = act.activation(stage[:, c * P:(c + 1) * P], ps_o[:, c, :], ACT.Copy, scale=rstd[:, c:c + 1])
                last.then_inc(act_r.sem, 1)
                t("g0")

            def store(h):
                act.wait_ge(v_r.sem, v_r.after(h, "out"))
                act.dma_start(dram["og"][bass.ds(h * P, P), :], out[:]).then_inc(s_out, 16)

            for name in TASKS[:-1]:
                evacuate(0, name)
            head(0, 1)
            with act.Fori(1, NH - 1) as h:
                head(h, h + 1)
            head(NH - 1, None)
            store(NH - 1)
            act.wait_ge(s_out, 16 * (NH + 1))

        @block.vector
        def _(v):
            v.sem_inc(v_z.sem, v_z.credit)
            v.sem_inc(v_r.sem, v_r.credit)
            v.sem_inc(v_p.sem, v_p.credit)
            v.wait_ge(s_zero, 3)
            v.wait_ge(s_mask, 16)
            v.tensor_copy(masks[:], masks_wide).then_inc(s_zero, 1)
            v.wait_ge(s_zero, 4)

            def silu(g, name, dst):
                half = int(name[1])
                v.wait_ge(act_z.sem, act_z.after(g, name))
                bank = ps_z[:, TASKS.index(name) % 2, :]
                v.tensor_tensor(dst[:, half * N512:(half + 1) * N512], bank, sig[:], ALU.mult).then_inc(v_z.sem, 1)

            def done(h, step):
                v.wait_ge(v_r.sem, v_r.after(h, step))

            def prepared(h, step):
                v.wait_ge(v_p.sem, v_p.after(h, step))

            def prepare_keys(h):
                v.wait_ge(act_z.sem, act_z.after(h, "c"))
                v.wait_ge(pe_r.sem, pe_r.after(h - 1, "ub"))
                done(h - 1, f"sb{NC - 2}")
                for d in range(2):
                    v.tensor_scalar(tot[0][:, d, :], f_next[:, d, 0:T], olb[:, d, bass.ds(h, 1)], lb[:, d, bass.ds(h, 1)],
                                    ALU.mult, ALU.add).then_inc(v_p.sem, 1)
                prepared(h, "f1")
                v.tensor_scalar(k2[:], tot[0][:], -1.0, 1.0, ALU.mult, ALU.add).then_inc(v_p.sem, 1)

            def prepare_queries(h):
                v.wait_ge(v_z.sem, v_z.after(h, "q1"))
                v.wait_ge(pe_r.sem, pe_r.after(h - 1, "o"))
                v.tensor_tensor(q2[:, 0, :], tot[0][:, 1, :], q_next[:], ALU.mult)
                v.tensor_tensor(q2[:, 1, :], tot[0][:, 0, :], q_next[:], ALU.mult).then_inc(v_p.sem, 1)

            def prepare_context(h):
                prepared(h, "keys")
                v.tensor_tensor(k_tok[:].rearrange("p c t -> p (c t)"), k2[:, 0, :], k2[:, 1, :], ALU.add).then_inc(v_p.sem, 1)
                for d in range(2):
                    v.tensor_scalar(f_next[:, d, T:TA], f_next[:, d, T:TA], olb[:, d, bass.ds(h, 1)], lb[:, d, bass.ds(h, 1)],
                                    ALU.mult, ALU.add).then_inc(v_p.sem, 1)
                prepared(h, "fc1")
                row = 2 * TA
                v.tensor_tensor_scan(bass.AP(reach, TC - 2, [[2 * TC, P], [-1, TC - 1]]),
                                     bass.AP(f_next, TA - 1, [[row, P], [-1, TC - 1]]), zeros[:, 0:TC - 1], 1.0, ALU.mult, ALU.add)
                v.tensor_tensor_scan(reach[:, 1, 1:TC], f_next[:, 1, T:TA - 1], zeros[:, 0:TC - 1], 1.0, ALU.mult, ALU.add).then_inc(v_p.sem, 1)
                prepared(h, "reach")
                v.tensor_scalar(f_next[:, :, T:TA], f_next[:, :, T:TA], -1.0, 1.0, ALU.mult, ALU.add).then_inc(v_p.sem, 1)
                prepared(h, "kc")
                v.tensor_tensor(f_next[:, :, T:TA], f_next[:, :, T:TA], reach[:], ALU.mult).then_inc(v_p.sem, 1)

            def level(h, l):
                v.wait_ge(pe_r.sem, pe_r.after(h, f"level{l}"))
                if l:
                    done(h, f"t{l - 1}")
                src, width = tot[l % 2], T if l % 2 == 0 else T // 2
                n = T >> l
                v.tensor_tensor(pair_ap(k2, l, 0), pair_ap(k2, l, 0), total_ap(src, l, width, 0, 1, 0), ALU.mult).then_inc(v_r.sem, 1)
                v.tensor_tensor(pair_ap(q2, l, 0), pair_ap(q2, l, 0), total_ap(src, l, width, 1, 1, 0), ALU.mult).then_inc(v_r.sem, 1)
                dst, dwidth = tot[(l + 1) % 2], T if l % 2 else T // 2
                if l == 0:
                    v.wait_ge(act_r.sem, act_r.after(h, "diag"))
                else:
                    done(h, f"p{l - 1}")
                v.tensor_tensor(bass.AP(dst, 0, [[2 * dwidth, P], [n // 2, 2], [1, n // 2]]),
                                bass.AP(src, 0, [[2 * width, P], [n, 2], [2, n // 2]]),
                                bass.AP(src, 1, [[2 * width, P], [n, 2], [2, n // 2]]), ALU.mult).then_inc(v_r.sem, 1)
                for b in range(2):
                    last = v.copy_predicated(scores[:, 4 * b:4 * b + 4, :], masks[:, l:l + 1, :].broadcast_to([P, 4, P]), ps_x[:, 4 * b:4 * b + 4, :])
                last.then_inc(v_r.sem, 1)

            def head(h, g):
                def t(name, dst):
                    if g is not None:
                        silu(g, name, dst)

                level(h, 0)
                silu(h, "g1", og_gate)
                v.wait_ge(pe_r.sem, pe_r.after(h, "s0"))
                v.tensor_copy(state[:, 0, 0, :], ps_w[:, 4, :])
                v.tensor_copy(state[:, 1, NC - 1, :], ps_w[:, 5, :]).then_inc(v_r.sem, 1)
                for l in range(1, LEVELS):
                    level(h, l)
                    if l == 1:
                        t("q0", q_next)
                    if l == 2:
                        t("q1", q_next)
                last_tot, wide = tot[LEVELS % 2], T if LEVELS % 2 == 0 else T // 2
                done(h, f"t{LEVELS - 1}")
                v.wait_ge(pe_r.sem, pe_r.after(h, "uf"))
                for c in range(NC - 1):
                    done(h, f"sf{c - 1}" if c else "s0")
                    v.scalar_tensor_tensor(out=state[:, 0, c + 1, :], in0=state[:, 0, c, :],
                                           scalar=bass.AP(last_tot, c, [[2 * wide, P], [1, 1]]),
                                           in1=ps_x[:, c, :], op0=ALU.mult, op1=ALU.add).then_inc(v_r.sem, 1)
                v.wait_ge(pe_r.sem, pe_r.after(h, "ub"))
                for j in range(NC - 1):
                    c = NC - 1 - j
                    done(h, f"sb{j - 1}" if j else "s0")
                    v.scalar_tensor_tensor(out=state[:, 1, c - 1, :], in0=state[:, 1, c, :],
                                           scalar=bass.AP(last_tot, NC + c, [[2 * wide, P], [1, 1]]),
                                           in1=ps_x[:, c, :], op0=ALU.mult, op1=ALU.add).then_inc(v_r.sem, 1)
                if g is not None:
                    prepare_keys(g)
                    prepare_queries(g)
                v.wait_ge(act_r.sem, act_r.after(h, f"sq{NC - 1}"))
                v.tensor_scalar(meansq[:], sumsq[:], 1.0 / P, EPS, ALU.mult, ALU.add).then_inc(v_r.sem, 1)
                if g is not None:
                    prepare_context(g)
                v.wait_ge(pe_r.sem, pe_r.after(h, "ot"))
                v.wait_ge(s_out, 16 * (h + 1))
                for b in range(2):
                    last = v.scalar_tensor_tensor(out=out[:, b * N512:(b + 1) * N512], in0=ps_w[:, 4 * b:4 * b + 4, :].rearrange("p c t -> p (c t)"),
                                                  scalar=cols[:, R_HG:R_HG + 1], in1=og_gate[:, b * N512:(b + 1) * N512],
                                                  op0=ALU.mult, op1=ALU.mult)
                last.then_inc(v_r.sem, 1)
                done(h, "out")
                t("g0", og_gate)

            v.sem_inc(s_out, 16)
            silu(0, "q0", q_next)
            silu(0, "q1", q_next)
            prepare_keys(0)
            prepare_queries(0)
            prepare_context(0)
            silu(0, "g0", og_gate)
            with v.Fori(0, NH - 1) as h:
                head(h, h + 1)
            head(NH - 1, None)


def phase_merge(nc, dram, y):
    KB = len(WINDOWS)
    KA = KT + KB
    STAGES = 3
    with ExitStack() as ctx:
        def sb(name, shape, dt=F32):
            return ctx.enter_context(nc.sbuf_tensor("m_" + name, shape, dt))

        def psum(name, shape):
            return ctx.enter_context(nc.psum_tensor("m_ps_" + name, shape, F32))

        def sem(name):
            return ctx.enter_context(nc.semaphore("m_" + name))

        landing = sb("landing", [P, STAGES, T])
        in_head = sb("in_head", [P, KA, T], F32R)
        in_tail = sb("in_tail", [P, KA, T], F32R)
        w_raw = sb("w_raw", [P, 2, KA, P])
        w_head = sb("w_head", [P, KA, P], F32R)
        w_tail = sb("w_tail", [P, KA, P], F32R)
        gate = sb("gate", [P, 2, T])
        zero = sb("zero", [P, 1])
        ps_a = [psum(f"a{i}", [P, T]) for i in range(2)]
        ps_b = [psum(f"b{i}", [P, T]) for i in range(2)]

        s_in = [sem(f"in_landed{i}") for i in range(STAGES)]
        s_w = [sem(f"w_landed{i}") for i in range(2)]
        s_gate = [sem(f"gate_landed{i}") for i in range(2)]
        act_in = sem("act_in_head")
        v_in = sem("v_in_tail")
        pool_set = sem("pool_set")
        pool_w = Steps(ctx, nc, "m_pool_w", ["head_a", "tail_a", "head_b", "tail_b"])
        pe_m = Steps(ctx, nc, "m_pe", ["a", "b"])
        v_m = Steps(ctx, nc, "m_v", ["ga", "gb", "sum"], lead=2)

        w_a = dram["w_a"].rearrange("a (k p) n -> p (a k) n", p=P)
        w_b = dram["w_b"].rearrange("a (k p) n -> p (a k) n", p=P)

        block = ctx.enter_context(nc.Block())

        @block.sync
        def _(sp):
            def load_block(m, slot):
                at = m * P if isinstance(m, int) else sp.snap(m * P)
                if not isinstance(m, int):
                    sp.wait_ge(pool_w.sem, pool_w.after(m - 2, "tail_b"))
                sp.dma_start(w_raw[:, slot, 0:KT, :], w_a[:, :, bass.ds(at, P)]).then_inc(s_w[slot], 16)
                sp.dma_start(w_raw[:, slot, KT:KA, :], w_b[:, :, bass.ds(at, P)]).then_inc(s_w[slot], 16)

            def load_gates(m):
                for g in range(2):
                    at = (g * D + m * P) * T if isinstance(m, int) else sp.snap((g * D + m * P) * T)
                    sp.wait_ge(v_m.sem, v_m.after(m - 1, "sum"))
                    src = dram["gates"].rearrange("g d t -> (g d t)")[bass.ds(at, P * T)].rearrange("(p t) -> p t", t=T)
                    sp.dma_start(gate[:, g, :], src).then_inc(s_gate[g], 16)

            def load_input(k):
                if k >= STAGES:
                    sp.wait_ge(v_in, k - STAGES + 1)
                src = dram["og"][k * P:(k + 1) * P, :] if k < KT else dram["yb"][(k - KT) * P:(k - KT + 1) * P, :]
                sp.dma_start(landing[:, k % STAGES, :], src).then_inc(s_in[k % STAGES], 16)

            load_block(0, 0)
            for k in range(KA):
                load_input(k)
            load_gates(0)
            load_block(1, 1)
            load_gates(1)
            with sp.Fori(1, KT // 2) as j:
                for i in range(2):
                    load_block(2 * j + i, i)
                    load_gates(2 * j + i)

        @block.gpsimd
        def _(pool):
            pool.sem_inc(pool_w.sem, pool_w.credit)
            pool.memset(zero[:], 0.0).then_inc(pool_set, 1)
            pool.wait_ge(pool_set, 1)
            with pool.Fori(0, KT // 2) as j:
                for i in range(2):
                    m = 2 * j + i
                    pool.wait_ge(s_w[i], 32 * (j + 1))
                    for part, lo, hi in (("a", 0, KT), ("b", KT, KA)):
                        pool.wait_ge(pe_m.sem, pe_m.after(m - 1, part))
                        pool.tensor_tensor(w_head[:, lo:hi], w_raw[:, i, lo:hi], zero[:].unsqueeze(2).broadcast_to([P, hi - lo, P]),
                                           ALU.add).then_inc(pool_w.sem, 1)
                        pool.wait_ge(pool_w.sem, pool_w.after(m, "head_" + part))
                        pool.tensor_tensor(w_tail[:, lo:hi], w_raw[:, i, lo:hi], w_head[:, lo:hi].bitcast(F32),
                                           ALU.subtract).then_inc(pool_w.sem, 1)

        @block.tensor
        def _(pe):
            pe.sem_inc(pe_m.sem, pe_m.credit)

            def branch(m, slot, part, first):
                lo, hi, ps = (0, KT, ps_a) if part == "a" else (KT, KA, ps_b)
                pe.wait_ge(pool_w.sem, pool_w.after(m, "tail_" + part))
                if not first:
                    pe.wait_ge(v_m.sem, v_m.after(m - 2, "sum"))
                for k in range(lo, hi):
                    if first:
                        pe.wait_ge(v_in, k + 1)
                    for half in range(2):
                        cols = slice(half * N512, (half + 1) * N512)
                        last = matmul3(pe, ps[slot][:, cols], (w_head[:, k, :], w_tail[:, k, :]),
                                       (in_head[:, k, cols], in_tail[:, k, cols]), k == lo, k == hi - 1)
                last.then_inc(pe_m.sem, 1)

            for part in "ab":
                branch(0, 0, part, True)
            for part in "ab":
                branch(1, 1, part, False)
            with pe.Fori(1, KT // 2) as j:
                for i in range(2):
                    for part in "ab":
                        branch(2 * j + i, i, part, False)

        @block.scalar
        def _(act):
            for k in range(KA):
                act.wait_ge(s_in[k % STAGES], 16 * (k // STAGES + 1))
                act.activation(in_head[:, k, :], landing[:, k % STAGES, :], ACT.Copy).then_inc(act_in, 1)

        @block.vector
        def _(v):
            v.sem_inc(v_m.sem, v_m.credit)
            for k in range(KA):
                v.wait_ge(act_in, k + 1)
                v.tensor_tensor(in_tail[:, k, :], landing[:, k % STAGES, :], in_head[:, k, :].bitcast(F32), ALU.subtract).then_inc(v_in, 1)
            with v.Fori(0, KT // 2) as j:
                for i in range(2):
                    m = 2 * j + i
                    v.wait_ge(pe_m.sem, pe_m.after(m, "a"))
                    v.wait_ge(s_gate[0], 16 * (m + 1))
                    v.tensor_tensor(gate[:, 0, :], ps_a[i][:], gate[:, 0, :], ALU.mult).then_inc(v_m.sem, 1)
                    v.wait_ge(pe_m.sem, pe_m.after(m, "b"))
                    v.wait_ge(s_gate[1], 16 * (m + 1))
                    v.tensor_tensor(gate[:, 1, :], ps_b[i][:], gate[:, 1, :], ALU.mult).then_inc(v_m.sem, 1)
                    v.wait_ge(v_m.sem, v_m.after(m, "gb"))
                    v.tensor_tensor(y[:, bass.ds(m, 1), :].rearrange("p a t -> p (a t)"), gate[:, 0, :], gate[:, 1, :], ALU.add).then_inc(v_m.sem, 1)


def phase_project(nc, dram, keep, y, probs_t):
    with ExitStack() as ctx:
        def sb(name, shape, dt=F32):
            return ctx.enter_context(nc.sbuf_tensor("o_" + name, shape, dt))

        def psum(name, shape):
            return ctx.enter_context(nc.psum_tensor("o_ps_" + name, shape, F32))

        def sem(name):
            return ctx.enter_context(nc.semaphore("o_" + name))

        w_raw = sb("w_raw", [P, 2, D])
        w_head = sb("w_head", [P, KT, D], F32R)
        w_tail = sb("w_tail", [P, KT, D], F32R)
        w_router = sb("w_router", [P, KT, NE])
        y_head = [sb(f"y_head{i}", [P, KT, P], F32R) for i in range(2)]
        y_tail = [sb(f"y_tail{i}", [P, KT, P], F32R) for i in range(2)]
        x_tile = [sb(f"x_tile{i}", [P, D]) for i in range(2)]
        hx = [sb(f"hx{i}", [P, D]) for i in range(2)]
        vn = [sb(f"vn{i}", [P, D]) for i in range(2)]
        v_feat = sb("v_feat", [P, KT, P])
        junk = sb("junk", [P, D])
        sumsq = sb("sumsq", [P, 1])
        meansq = sb("meansq", [P, 1])
        neghalf = sb("neghalf", [P, 1])
        rstd = sb("rstd", [P, 1])
        negmax = sb("negmax", [P, 1])
        expsum = sb("expsum", [P, 1])
        inverse = sb("inverse", [P, 1])
        expd = sb("expd", [P, NE])
        probs = sb("probs", [P, NE])
        ps_o = [psum(f"out{i}", [P, D]) for i in range(2)]
        ps_v = psum("v", [P, KT, P])
        ps_l = psum("logits", [P, N512])
        ps_p = psum("probs", [P, N512])

        s_w = [sem(f"w_landed{i}") for i in range(2)]
        s_router = sem("router_landed")
        s_x = [sem(f"x_landed{i}") for i in range(2)]
        s_hx = [sem(f"hx_stored{i}") for i in range(2)]
        s_vn = [sem(f"vn_stored{i}") for i in range(2)]
        act_w = sem("act_w_head")
        v_w = sem("v_w_tail")
        pool_set = sem("pool_set")
        pe_main = Steps(ctx, nc, "o_pe_main", ["half0", "half1"], lead=2)
        pe_turn = Steps(ctx, nc, "o_pe_turn", ["turn"], lead=2)
        pe_route = Steps(ctx, nc, "o_pe_route", ["logits", "probs"])
        act_split = Steps(ctx, nc, "o_act_split", ["head"])
        act_main = Steps(ctx, nc, "o_act_main", ["square", "vn"])
        act_route = Steps(ctx, nc, "o_act_route", ["feat", "exp"])
        v_split = Steps(ctx, nc, "o_v_split", ["tail"])
        v_main = Steps(ctx, nc, "o_v_main", ["gated", "hx", "mean"], lead=2)
        v_route = Steps(ctx, nc, "o_v_route", ["max", "inverse", "probs", "probs_t"])
        pool_main = Steps(ctx, nc, "o_pool_main", ["rstd"])

        ident, gates = keep["ident"], keep["gates"]
        w_out = dram["w_out"].rearrange("a (k p) n -> p (a k) n", p=P)
        x_flat = dram["x"].rearrange("a t d -> (a t) d")

        block = ctx.enter_context(nc.Block())

        def known(i, lo=0, hi=NT):
            return not isinstance(i, int) or lo <= i < hi

        def iterations(eng, body):
            for i in range(4):
                body(i, i % 2)
            with eng.Fori(2, NT // 2 - 1) as j:
                for slot in range(2):
                    body(2 * j + slot, slot)
            for i in range(NT - 2, NT + 3):
                body(i, i % 2)

        @block.sync
        def _(sp):
            sp.dma_start(w_router[:], dram["w_router"].rearrange("a (k p) e -> p (a k) e", p=P)).then_inc(s_router, 16)
            for k in range(KT):
                if k >= 2:
                    sp.wait_ge(v_w, k - 1)
                sp.dma_start(w_raw[:, k % 2, :], w_out[:, k, :]).then_inc(s_w[k % 2], 16)
                if k < 2:
                    sp.dma_start(x_tile[k][:], x_flat[k * P:(k + 1) * P, :]).then_inc(s_x[k], 16)
            with sp.Fori(1, NT // 2) as j:
                for i in range(2):
                    at = sp.snap((2 * j + i) * P * D)
                    sp.wait_ge(v_main.sem, v_main.after(2 * j + i - 2, "hx"))
                    src = x_flat.rearrange("t d -> (t d)")[bass.ds(at, P * D)].rearrange("(p d) -> p d", d=D)
                    sp.dma_start(x_tile[i][:], src).then_inc(s_x[i], 16)

        @block.gpsimd
        def _(pool):
            pool.sem_inc(pool_main.sem, pool_main.credit)
            pool.memset(neghalf[:], -0.5).then_inc(pool_set, 1)
            pool.wait_ge(pool_set, 1)
            with pool.Fori(0, NT) as i:
                pool.wait_ge(v_main.sem, v_main.after(i, "mean"))
                pool.tensor_tensor(rstd[:], meansq[:], neghalf[:], ALU.pow).then_inc(pool_main.sem, 1)

        @block.tensor
        def _(pe):
            pe.sem_inc(pe_main.sem, pe_main.credit)
            pe.sem_inc(pe_route.sem, pe_route.credit)
            pe.wait_ge(s_router, 16)

            pe.sem_inc(pe_turn.sem, pe_turn.credit)

            def half(i, slot, h):
                if h == 0:
                    pe.wait_ge(v_split.sem, v_split.after(i, "tail"))
                    pe.wait_ge(v_main.sem, v_main.after(i - 2, "gated"))
                cols = slice(h * N512, (h + 1) * N512)
                for k in range(KT):
                    if isinstance(i, int) and i == 0:
                        pe.wait_ge(v_w, k + 1)
                    last = matmul3(pe, ps_o[slot][:, cols], (y_head[slot][:, k, :], y_tail[slot][:, k, :]),
                                   (w_head[:, k, cols], w_tail[:, k, cols]), k == 0, k == KT - 1)
                last.then_inc(pe_main.sem, 1)

            def turn(i, slot):
                pe.wait_ge(act_main.sem, act_main.after(i, "vn"))
                pe.wait_ge(act_route.sem, act_route.after(i - 1, "feat"))
                for k in range(KT):
                    last = pe.transpose(ps_v[:, k, :], vn[slot][:, k * P:(k + 1) * P], ident[:])
                last.then_inc(pe_turn.sem, 1)

            def logits(i):
                pe.wait_ge(act_route.sem, act_route.after(i, "feat"))
                for k in range(KT):
                    last = pe.matmul(ps_l[:, 0:NE], v_feat[:, k, :], w_router[:, k, :], start=(k == 0), stop=(k == KT - 1))
                last.then_inc(pe_route.sem, 1)

            def turn_probs(i):
                pe.wait_ge(v_route.sem, v_route.after(i, "probs"))
                pe.transpose(ps_p[0:NE, 0:P], probs[:], ident[:]).then_inc(pe_route.sem, 1)

            def body(i, slot):
                if known(i):
                    half(i, slot, 0)
                if known(i - 3):
                    turn_probs(i - 3)
                if known(i):
                    half(i, slot, 1)
                if known(i - 2):
                    logits(i - 2)
                if known(i - 1):
                    turn(i - 1, 1 - slot)

            iterations(pe, body)

        @block.scalar
        def _(act):
            act.sem_inc(act_main.sem, act_main.credit)
            act.sem_inc(act_route.sem, act_route.credit)
            act.sem_inc(act_split.sem, act_split.credit)


            def split(i, slot):
                act.wait_ge(pe_main.sem, pe_main.after(i - 2, "half1"))
                act.activation(y_head[slot][:], y[:, :, bass.ds(i * P, P)], ACT.Copy).then_inc(act_split.sem, 1)

            def main(i, slot):
                act.wait_ge(v_main.sem, v_main.after(i, "hx"))
                act.wait_ge(act_main.sem, act_main.after(i - 1, "vn"))
                act.activation(junk[:], hx[slot][:], ACT.Square, accum_out=sumsq[:]).then_inc(act_main.sem, 1)
                act.dma_start(dram["acc"][bass.ds(i * P, P), :], hx[slot][:]).then_inc(s_hx[slot], 16)
                act.wait_ge(s_vn[slot], 8 * (i - slot) + 16)
                act.wait_ge(pe_turn.sem, pe_turn.after(i - 2, "turn"))
                act.wait_ge(pool_main.sem, pool_main.after(i, "rstd"))
                act.activation(vn[slot][:], hx[slot][:], ACT.Copy, scale=rstd[:]).then_inc(act_main.sem, 1)
                act.wait_ge(act_main.sem, act_main.after(i, "vn"))
                act.dma_start(dram["vn"][bass.ds(i * P, P), :], vn[slot][:]).then_inc(s_vn[slot], 16)

            def features(i):
                act.wait_ge(pe_turn.sem, pe_turn.after(i, "turn"))
                act.wait_ge(pe_route.sem, pe_route.after(i - 1, "logits"))
                for k in range(KT):
                    last = act.activation(v_feat[:, k, :], ps_v[:, k, :], ACT.Identity, scale=keep["scale2"][:, k:k + 1],
                                          bias=keep["shift2"][:, k:k + 1])
                last.then_inc(act_route.sem, 1)

            def exponentials(i):
                act.wait_ge(v_route.sem, v_route.after(i, "max"))
                act.activation(expd[:], ps_l[:, 0:NE], ACT.Exp, bias=negmax[:], accum_out=expsum[:]).then_inc(act_route.sem, 1)

            def body(i, slot):
                if known(i - 2):
                    features(i - 2)
                if known(i + 1):
                    split(i + 1, 1 - slot)
                if known(i):
                    main(i, slot)
                if known(i - 2):
                    exponentials(i - 2)

            split(0, 0)
            for k in range(KT):
                act.wait_ge(s_w[k % 2], 16 * (k // 2 + 1))
                act.activation(w_head[:, k, :], w_raw[:, k % 2, :], ACT.Copy).then_inc(act_w, 1)
            iterations(act, body)
            for i in range(2):
                act.wait_ge(s_hx[i], 16 * (NT // 2 + 1))
                act.wait_ge(s_vn[i], 16 * (NT // 2 + 1))

        @block.vector
        def _(v):
            v.sem_inc(v_main.sem, v_main.credit)
            v.sem_inc(v_route.sem, v_route.credit)
            v.sem_inc(v_split.sem, v_split.credit)
            for i in range(2):
                v.sem_inc(s_hx[i], 16)
                v.sem_inc(s_vn[i], 16)

            def split(i, slot):
                v.wait_ge(act_split.sem, act_split.after(i, "head"))
                v.tensor_tensor(y_tail[slot][:], y[:, :, bass.ds(i * P, P)], y_head[slot][:].bitcast(F32), ALU.subtract).then_inc(v_split.sem, 1)

            def main(i, slot):
                v.wait_ge(pe_main.sem, pe_main.after(i, "half1"))
                v.wait_ge(s_hx[slot], 8 * (i - slot) + 16)
                v.wait_ge(act_main.sem, act_main.after(i - 1, "vn"))
                v.tensor_tensor(hx[slot][:], ps_o[slot][:], gates[:, 0, :], ALU.mult).then_inc(v_main.sem, 1)
                v.wait_ge(s_x[slot], 8 * (i - slot) + 16)
                v.wait_ge(v_main.sem, v_main.after(i, "gated"))
                v.tensor_tensor(hx[slot][:], hx[slot][:], x_tile[slot][:], ALU.add).then_inc(v_main.sem, 1)
                v.wait_ge(act_main.sem, act_main.after(i, "square"))
                v.wait_ge(pool_main.sem, pool_main.after(i - 1, "rstd"))
                v.tensor_scalar(meansq[:], sumsq[:], 1.0 / D, EPS, ALU.mult, ALU.add).then_inc(v_main.sem, 1)

            def route(i):
                v.wait_ge(pe_route.sem, pe_route.after(i, "logits"))
                v.tensor_reduce(negmax[:], ps_l[:, 0:NE], AX.X, ALU.max, negate=True).then_inc(v_route.sem, 1)
                v.wait_ge(act_route.sem, act_route.after(i, "exp"))
                v.reciprocal(inverse[:], expsum[:]).then_inc(v_route.sem, 1)
                v.wait_ge(v_route.sem, v_route.after(i, "inverse"))
                v.tensor_scalar(probs[:], expd[:], inverse[:], None, ALU.mult).then_inc(v_route.sem, 1)

            def keep_probs(i):
                v.wait_ge(pe_route.sem, pe_route.after(i, "probs"))
                v.tensor_copy(probs_t[:, bass.ds(i * P, P)], ps_p[0:NE, 0:P]).then_inc(v_route.sem, 1)

            def body(i, slot):
                if known(i + 1):
                    split(i + 1, 1 - slot)
                if known(i - 3):
                    keep_probs(i - 3)
                if known(i):
                    main(i, slot)
                if known(i - 2):
                    route(i - 2)

            split(0, 0)
            for k in range(KT):
                v.wait_ge(act_w, k + 1)
                v.tensor_tensor(w_tail[:, k, :], w_raw[:, k % 2, :], w_head[:, k, :].bitcast(F32), ALU.subtract).then_inc(v_w, 1)
            iterations(v, body)


def phase_experts(nc, dram, keep, probs_t):
    CK = 2
    NCH = KT // CK
    RAW, SPLIT = 6, 4
    GU = [f"g{c}" for c in range(NCH)] + [f"u{c}" for c in range(NCH)]
    DN = [f"d{c}" for c in range(NCH)]
    ROUNDS = CAP // 8
    TOP_STEPS = 3 * ROUNDS
    with ExitStack() as ctx:
        def sb(name, shape, dt=F32):
            return ctx.enter_context(nc.sbuf_tensor("e_" + name, shape, dt))

        def psum(name, shape):
            return ctx.enter_context(nc.psum_tensor("e_ps_" + name, shape, F32))

        def sem(name):
            return ctx.enter_context(nc.semaphore("e_" + name))

        w_raw = sb("w_raw", [P, RAW, CK, FF])
        w_head = sb("w_head", [P, SPLIT, CK, FF], F32R)
        w_tail = sb("w_tail", [P, SPLIT, CK, FF], F32R)
        left = [sb(f"left{i}", [NE, T]) for i in range(2)]
        best = sb("best", [NE, CAP])
        where = sb("where", [NE, CAP], U32)
        where_f = sb("where_f", [NE, CAP])
        token = sb("token", [P, NE], U32)
        weight = sb("weight", [P, NE])
        token_in = sb("token_in", [P, 1], U32)
        token_out = sb("token_out", [P, 1], U32)
        zero_u = sb("zero_u", [P, 1], U32)
        settled = sb("settled", [P, 2], U32)
        xg = sb("xg", [P, D])
        xm = sb("xm", [P, KT, P])
        x_head = sb("x_head", [P, KT, P], F32R)
        x_tail = sb("x_tail", [P, KT, P], F32R)
        sig = sb("sig", [P, FF])
        hid = sb("hid", [P, FF])
        h_head = sb("h_head", [P, KT, P], F32R)
        h_tail = sb("h_tail", [P, KT, P], F32R)
        rows = sb("rows", [P, D])
        ps_g = psum("gate", [P, FF])
        ps_u = psum("up", [P, FF])
        ps_y = psum("down", [P, D])
        ps_t = psum("turn", [P, KT, P])

        s_gu = [sem(f"w_landed_{n}") for n in GU]
        s_d = [sem(f"w_landed_{n}") for n in DN]
        s_xg = sem("tokens_gathered")
        s_add = sem("rows_added")
        v_top = sem("v_top")
        pool_set = sem("pool_set")
        pe_top = sem("pe_top")
        pool_in = sem("pool_token_in")
        pool_out = sem("pool_token_out")
        pe_gu = Steps(ctx, nc, "e_pe_gu", GU)
        pe_d = Steps(ctx, nc, "e_pe_d", DN)
        pe_xt = Steps(ctx, nc, "e_pe_xt", ["xt"])
        pe_ht = Steps(ctx, nc, "e_pe_ht", ["ht"])
        act_gu = Steps(ctx, nc, "e_act_gu", GU)
        act_d = Steps(ctx, nc, "e_act_d", DN)
        act_sig = Steps(ctx, nc, "e_act_sig", ["sig"])
        act_x = Steps(ctx, nc, "e_act_x", ["mod", "head"])
        act_h = Steps(ctx, nc, "e_act_h", ["head"])
        v_gu = Steps(ctx, nc, "e_v_gu", GU)
        v_d = Steps(ctx, nc, "e_v_d", DN)
        v_hid = Steps(ctx, nc, "e_v_hid", ["silu", "hid"])
        v_x = Steps(ctx, nc, "e_v_x", ["mod", "tail"])
        v_h = Steps(ctx, nc, "e_v_h", ["tail"])
        v_y = Steps(ctx, nc, "e_v_y", ["rows"])

        ident, gates, scale2, shift2 = keep["ident"], keep["gates"], keep["scale2"], keep["shift2"]

        block = ctx.enter_context(nc.Block())

        def known(e, lo, hi):
            return not isinstance(e, int) or lo <= e < hi

        def wait(eng, steps, it, step):
            if known(it, 0, NE):
                eng.wait_ge(steps.sem, steps.after(it, step))

        def iterations(eng, body):
            body(0)
            body(1)
            with eng.Fori(2, NE - 1) as e:
                body(e)
            for e in range(NE - 1, NE + 2):
                body(e)

        def position(name):
            return (GU + DN).index(name)

        def wait_slot(eng, gu_steps, d_steps, it, pos, ring):
            while True:
                pos -= ring
                if pos < 0:
                    pos, it = pos + 3 * NCH, it - 1
                if isinstance(it, int) and it < 0:
                    return
                if not isinstance(it, int) or (it < NE if pos < 2 * NCH else it >= 1):
                    break
            if pos < 2 * NCH:
                eng.wait_ge(gu_steps.sem, gu_steps.after(it, GU[pos]))
            else:
                eng.wait_ge(d_steps.sem, d_steps.after(it - 1, DN[pos - 2 * NCH]))

        @block.sync
        def _(sp):
            stack = {"g": dram["w_e_gate"], "u": dram["w_e_up"], "d": dram["w_e_down"]}
            flat = {k: a.rearrange("a e f n -> (a e f n)") for k, a in stack.items()}

            def load(expert, name, landed):
                pos = position(name)
                size = CK * P * FF
                at = expert * (FF * D) + int(name[1]) * size
                at = at if isinstance(expert, int) else sp.snap(at)
                it = expert + 1 if name[0] == "d" else expert
                wait_slot(sp, v_gu, v_d, it, pos, RAW)
                src = flat[name[0]][bass.ds(at, size)].rearrange("(k p n) -> p k n", p=P, n=FF)
                sp.dma_start(w_raw[:, pos % RAW], src).then_inc(landed, 16)

            def body(e):
                if known(e, 0, NE):
                    for n, name in enumerate(GU):
                        load(e, name, s_gu[n])
                if known(e, 1, NE + 1):
                    for n, name in enumerate(DN):
                        load(e - 1, name, s_d[n])

            iterations(sp, body)

        @block.gpsimd
        def _(pool):
            pool.memset(zero_u[:], 0).then_inc(pool_set, 1)
            pool.wait_ge(pool_set, 1)
            pool.wait_ge(v_top, TOP_STEPS + 2)


            def gather(x):
                wait(pool, pe_xt, x - 1, "xt")
                pool.tensor_tensor(token_in[:], token[:, bass.ds(x, 1)], zero_u[:], ALU.add).then_inc(pool_in, 1)
                pool.wait_ge(pool_in, 2 * x + 1)
                pool.tensor_tensor(settled[:, 0:1], zero_u[:], zero_u[:], ALU.add).then_inc(pool_in, 1)
                pool.indirect_dma_start(xg[:], None, dram["vn"], bass.IndirectOffsetOnAxis(ap=token_in[:], axis=0)).then_inc(s_xg, 16)

            def scatter(x):
                if known(x, 1, NE):
                    pool.wait_ge(s_add, 16 * x)
                pool.tensor_tensor(token_out[:], token[:, bass.ds(x, 1)], zero_u[:], ALU.add).then_inc(pool_out, 1)
                wait(pool, v_y, x, "rows")
                pool.wait_ge(pool_out, 2 * x + 1)
                pool.tensor_tensor(settled[:, 1:2], zero_u[:], zero_u[:], ALU.add).then_inc(pool_out, 1)
                pool.indirect_dma_start(dram["acc"], bass.IndirectOffsetOnAxis(ap=token_out[:], axis=0), rows[:], None,
                                        compute_op=ALU.add).then_inc(s_add, 16)

            def body(e):
                if known(e + 1, 1, NE):
                    gather(e + 1)
                if known(e - 2, 0, NE):
                    scatter(e - 2)

            gather(0)
            iterations(pool, body)
            pool.wait_ge(s_add, 16 * NE)

        @block.tensor
        def _(pe):
            for s in (pe_gu, pe_d, pe_xt, pe_ht):
                pe.sem_inc(s.sem, s.credit)

            def product(ps, lhs, slot, c):
                for k in range(CK):
                    kk = CK * c + k
                    for half in range(2):
                        cols = slice(half * N512, (half + 1) * N512)
                        last = matmul3(pe, ps[:, cols], (lhs[0][:, kk, :], lhs[1][:, kk, :]),
                                       (w_head[:, slot, k, cols], w_tail[:, slot, k, cols]), kk == 0, kk == KT - 1)
                return last

            def turn(ps, src):
                for k in range(KT):
                    last = pe.transpose(ps[:, k, :], src[:, k * P:(k + 1) * P], ident[:])
                return last

            def gate_up(e):
                wait(pe, v_x, e, "tail")
                for n, name in enumerate(GU):
                    if name == "g0":
                        wait(pe, v_hid, e - 1, "silu")
                    if name == "u0":
                        wait(pe, v_hid, e - 1, "hid")
                    wait(pe, v_gu, e, name)
                    product(ps_g if name[0] == "g" else ps_u, (x_head, x_tail), n % SPLIT, n % NCH).then_inc(pe_gu.sem, 1)

            def turn_tokens(x):
                pe.wait_ge(s_xg, 16 * (x + 1))
                wait(pe, v_h, x - 2, "tail")
                turn(ps_t, xg).then_inc(pe_xt.sem, 1)

            def down(x):
                wait(pe, v_h, x, "tail")
                wait(pe, v_y, x - 1, "rows")
                for c, name in enumerate(DN):
                    wait(pe, v_d, x, name)
                    product(ps_y, (h_head, h_tail), c % SPLIT, c).then_inc(pe_d.sem, 1)

            def turn_hidden(x):
                wait(pe, v_hid, x, "hid")
                if known(x + 1, 1, NE):
                    wait(pe, act_x, x + 1, "mod")
                    wait(pe, v_x, x + 1, "mod")
                turn(ps_t, hid).then_inc(pe_ht.sem, 1)

            pe.wait_ge(v_top, TOP_STEPS)
            pe.transpose(ps_g[:, 0:NE], where_f[:], ident[0:NE, 0:NE])
            pe.transpose(ps_g[:, NE:2 * NE], best[:], ident[0:NE, 0:NE]).then_inc(pe_top, 1)
            pe.wait_ge(v_top, TOP_STEPS + 2)
            turn_tokens(0)

            def body(e):
                if known(e, 0, NE):
                    gate_up(e)
                if known(e + 1, 1, NE):
                    turn_tokens(e + 1)
                if known(e - 1, 0, NE):
                    down(e - 1)
                if known(e, 0, NE):
                    turn_hidden(e)

            iterations(pe, body)

        @block.scalar
        def _(act):
            for s in (act_gu, act_d, act_sig, act_x, act_h):
                act.sem_inc(s.sem, s.credit)

            def split_gu(e, name):
                n = GU.index(name)
                act.wait_ge(s_gu[n], 16 * (e + 1))
                wait_slot(act, pe_gu, pe_d, e, position(name), SPLIT)
                act.activation(w_head[:, n % SPLIT], w_raw[:, n % RAW], ACT.Copy).then_inc(act_gu.sem, 1)

            def split_d(x, name):
                c = DN.index(name)
                act.wait_ge(s_d[c], 16 * (x + 1))
                wait_slot(act, pe_gu, pe_d, x + 1, position(name), SPLIT)
                act.activation(w_head[:, c % SPLIT], w_raw[:, (2 * NCH + c) % RAW], ACT.Copy).then_inc(act_d.sem, 1)

            def sigmoid(e):
                act.wait_ge(pe_gu.sem, pe_gu.after(e, GU[NCH - 1]))
                wait(act, v_hid, e - 1, "silu")
                act.activation(sig[:], ps_g[:], ACT.Sigmoid).then_inc(act_sig.sem, 1)

            def tokens(x):
                act.wait_ge(pe_xt.sem, pe_xt.after(x, "xt"))
                wait(act, v_x, x - 1, "tail")
                for k in range(KT // 2):
                    last = act.activation(xm[:, k, :], ps_t[:, k, :], ACT.Identity, scale=scale2[:, k:k + 1], bias=shift2[:, k:k + 1])
                last.then_inc(act_x.sem, 1)
                act.wait_ge(act_x.sem, act_x.after(x, "mod"))
                act.wait_ge(v_x.sem, v_x.after(x, "mod"))
                act.activation(x_head[:], xm[:], ACT.Copy).then_inc(act_x.sem, 1)

            def hidden(x):
                act.wait_ge(pe_ht.sem, pe_ht.after(x, "ht"))
                act.activation(h_head[:], ps_t[:], ACT.Copy).then_inc(act_h.sem, 1)

            def body(e):
                gu, d = known(e, 0, NE), known(e - 1, 0, NE)
                for n, name in enumerate(GU):
                    if gu:
                        split_gu(e, name)
                    if name == "g2" and d:
                        hidden(e - 1)
                    if name == "g3" and isinstance(e, int) and e == 0:
                        tokens(0)
                    if name == "u2" and gu:
                        sigmoid(e)
                for name in DN:
                    if d:
                        split_d(e - 1, name)
                    if name == "d2" and known(e + 1, 1, NE):
                        tokens(e + 1)

            iterations(act, body)

        @block.vector
        def _(v):
            for s in (v_gu, v_d, v_hid, v_x, v_h, v_y):
                v.sem_inc(s.sem, s.credit)

            step = 0
            src = probs_t
            for r in range(ROUNDS):
                eight = best[:, 8 * r:8 * r + 8]
                v.max(eight, src[:]).then_inc(v_top, 1)
                v.wait_ge(v_top, step + 1)
                v.max_index(where[:, 8 * r:8 * r + 8], eight, src[:]).then_inc(v_top, 1)
                step += 2
                if r < ROUNDS - 1:
                    v.match_replace(left[r % 2][:], eight, src[:], -1.0).then_inc(v_top, 1)
                    step += 1
                    v.wait_ge(v_top, step)
                    src = left[r % 2]
            v.wait_ge(v_top, step)
            v.tensor_copy(where_f[:], where[:]).then_inc(v_top, 1)
            assert step + 1 == TOP_STEPS
            v.wait_ge(pe_top, 1)
            v.tensor_copy(token[:], ps_g[:, 0:NE]).then_inc(v_top, 1)
            v.tensor_copy(weight[:], ps_g[:, NE:2 * NE]).then_inc(v_top, 1)
            v.wait_ge(v_top, TOP_STEPS + 2)

            def split_gu(e, name):
                n = GU.index(name)
                v.wait_ge(act_gu.sem, act_gu.after(e, name))
                v.tensor_tensor(w_tail[:, n % SPLIT], w_raw[:, n % RAW], w_head[:, n % SPLIT].bitcast(F32), ALU.subtract).then_inc(v_gu.sem, 1)

            def split_d(x, name):
                c = DN.index(name)
                v.wait_ge(act_d.sem, act_d.after(x, name))
                v.tensor_tensor(w_tail[:, c % SPLIT], w_raw[:, (2 * NCH + c) % RAW], w_head[:, c % SPLIT].bitcast(F32),
                                ALU.subtract).then_inc(v_d.sem, 1)

            def silu(e):
                v.wait_ge(act_sig.sem, act_sig.after(e, "sig"))
                v.wait_ge(pe_ht.sem, pe_ht.after(e - 1, "ht"))
                v.tensor_tensor(hid[:], ps_g[:], sig[:], ALU.mult).then_inc(v_hid.sem, 1)

            def gated(e):
                v.wait_ge(pe_gu.sem, pe_gu.after(e, GU[-1]))
                v.wait_ge(v_hid.sem, v_hid.after(e, "silu"))
                v.tensor_tensor(hid[:], hid[:], ps_u[:], ALU.mult).then_inc(v_hid.sem, 1)

            def tokens(x):
                v.wait_ge(pe_xt.sem, pe_xt.after(x, "xt"))
                v.wait_ge(act_x.sem, act_x.after(x - 1, "head"))
                wait(v, v_x, x - 1, "tail")
                for k in range(KT // 2, KT):
                    last = v.tensor_scalar(xm[:, k, :], ps_t[:, k, :], scale2[:, k:k + 1], shift2[:, k:k + 1], ALU.mult, ALU.add)
                last.then_inc(v_x.sem, 1)
                v.wait_ge(act_x.sem, act_x.after(x, "head"))
                v.tensor_tensor(x_tail[:], xm[:], x_head[:].bitcast(F32), ALU.subtract).then_inc(v_x.sem, 1)

            def hidden(x):
                v.wait_ge(act_h.sem, act_h.after(x, "head"))
                v.tensor_tensor(h_tail[:], ps_t[:], h_head[:].bitcast(F32), ALU.subtract).then_inc(v_h.sem, 1)

            def scale_rows(x):
                v.wait_ge(pe_d.sem, pe_d.after(x, DN[-1]))
                if known(x, 1, NE):
                    v.wait_ge(s_add, 16 * x)
                for half in range(2):
                    cols = slice(half * N512, (half + 1) * N512)
                    last = v.scalar_tensor_tensor(out=rows[:, cols], in0=ps_y[:, cols], scalar=weight[:, bass.ds(x, 1)],
                                                  in1=gates[:, 1, cols], op0=ALU.mult, op1=ALU.mult)
                last.then_inc(v_y.sem, 1)

            def body(e):
                gu, d = known(e, 0, NE), known(e - 1, 0, NE)
                for n, name in enumerate(GU):
                    if gu:
                        split_gu(e, name)
                    if name == "g2":
                        if d:
                            hidden(e - 1)
                        if known(e - 2, 0, NE):
                            scale_rows(e - 2)
                    if name == "g3" and isinstance(e, int) and e == 0:
                        tokens(0)
                    if name == "u2" and gu:
                        silu(e)
                for name in DN:
                    if d:
                        split_d(e - 1, name)
                    if name == "d2":
                        if gu:
                            gated(e)
                        if known(e + 1, 1, NE):
                            tokens(e + 1)

            iterations(v, body)


def phase_final(nc, dram):
    with ExitStack() as ctx:
        def sb(name, shape, dt=F32):
            return ctx.enter_context(nc.sbuf_tensor("f_" + name, shape, dt))

        def sem(name):
            return ctx.enter_context(nc.semaphore("f_" + name))

        hx = sb("hx", [P, NT, D])
        gain = sb("gain", [P, D])
        junk = sb("junk", [P, D])
        sumsq = sb("sumsq", [P, NT])
        meansq = sb("meansq", [P, NT])
        neghalf = sb("neghalf", [P, NT])
        rstd = sb("rstd", [P, NT])
        s_in = [sem(f"hx_landed{i}") for i in range(NT)]
        s_gain = sem("gain_landed")
        s_out = sem("out_stored")
        act_sq = sem("act_square")
        v_mean = sem("v_mean")
        v_out = sem("v_out")
        pool_set = sem("pool_set")
        pool_rstd = sem("pool_rstd")

        block = ctx.enter_context(nc.Block())

        @block.sync
        def _(sp):
            for i in range(NT):
                sp.dma_start(hx[:, i, :], dram["acc"][i * P:(i + 1) * P, :]).then_inc(s_in[i], 16)
                if i == 0:
                    sp.dma_start(gain[:], dram["final_g"].rearrange("(a d) -> a d", a=1).broadcast_to([P, D])).then_inc(s_gain, 16)
            for i in range(NT):
                sp.wait_ge(v_out, i + 1)
                sp.dma_start(dram["out"][0, i * P:(i + 1) * P, :], hx[:, i, :]).then_inc(s_out, 16)
            sp.wait_ge(s_out, 16 * NT)

        @block.gpsimd
        def _(pool):
            pool.memset(neghalf[:], -0.5).then_inc(pool_set, 1)
            pool.wait_ge(pool_set, 1)
            for i in range(NT):
                pool.wait_ge(v_mean, i + 1)
                pool.tensor_tensor(rstd[:, i:i + 1], meansq[:, i:i + 1], neghalf[:, i:i + 1], ALU.pow).then_inc(pool_rstd, 1)

        @block.scalar
        def _(act):
            for i in range(NT):
                act.wait_ge(s_in[i], 16)
                if i:
                    act.wait_ge(act_sq, i)
                act.activation(junk[:], hx[:, i, :], ACT.Square, accum_out=sumsq[:, i:i + 1]).then_inc(act_sq, 1)

        @block.vector
        def _(v):
            def mean(i):
                v.wait_ge(act_sq, i + 1)
                v.tensor_scalar(meansq[:, i:i + 1], sumsq[:, i:i + 1], 1.0 / D, EPS, ALU.mult, ALU.add).then_inc(v_mean, 1)

            def scaled(i):
                v.wait_ge(pool_rstd, i + 1)
                v.scalar_tensor_tensor(out=hx[:, i, :], in0=hx[:, i, :], scalar=rstd[:, i:i + 1], in1=gain[:],
                                       op0=ALU.mult, op1=ALU.mult).then_inc(v_out, 1)

            v.wait_ge(s_gain, 16)
            for i in range(NT):
                mean(i)
                if i >= 2:
                    scaled(i - 2)
            scaled(NT - 2)
            scaled(NT - 1)


_IN = ["x", "c", "ctx", "c_ctx", "lb_logits", "w_mod", "b_mod", "norm1_g", "w_in", "hgrn_norm_g", "w_a", "w_pool",
       "pool_scale", "w_b", "w_out", "norm2_g", "w_router", "w_e_gate", "w_e_up", "w_e_down", "final_g"]

_SCRATCH = {"og": (D, T), "yb": (P * len(WINDOWS), T), "gates": (2, D, T), "acc": (T, D), "vn": (T, D)}


def build(nc, dram):
    with ExitStack() as ctx:
        def sb(stack, name, shape, dt=F32):
            return stack.enter_context(nc.sbuf_tensor(name, shape, dt))

        keep = {"cols": sb(ctx, "cols", [P, P]), "ident": sb(ctx, "ident", [P, P]),
                "scale2": sb(ctx, "scale2", [P, KT]), "shift2": sb(ctx, "shift2", [P, KT]),
                "gates": sb(ctx, "gate_rows", [P, 2, D]),
                "lb": sb(ctx, "lb", [P, 2, NH]), "olb": sb(ctx, "olb", [P, 2, NH])}
        with ExitStack() as mixer:
            ux_head = sb(mixer, "ux_head", [P, KT, TA], F32R)
            ux_tail = sb(mixer, "ux_tail", [P, KT, TA], F32R)
            phase_modulate(nc, dram, keep, ux_head, ux_tail)
            phase_pool_gates(nc, dram, keep, ux_head, ux_tail)
            phase_heads(nc, dram, keep, ux_head, ux_tail)
        probs_t = sb(ctx, "probs_t", [NE, T])
        with ExitStack() as merge:
            y = sb(merge, "y", [P, KT, T])
            phase_merge(nc, dram, y)
            phase_project(nc, dram, keep, y, probs_t)
        phase_experts(nc, dram, keep, probs_t)
        phase_final(nc, dram)


def constants():
    s = np.arange(P)
    masks = np.stack([((s[:, None] >> (l + 1)) == (s[None, :] >> (l + 1))) & (((s[:, None] ^ s[None, :]) >> l) & 1 == 1)
                      for l in range(LEVELS)], axis=1).astype(np.int32)
    icount = []
    for w in WINDOWS:
        def span(n):
            pos = np.arange(n)
            return np.clip(pos + w // 2 - 1, 0, n - 1) + 1 - np.clip(pos - w // 2, 0, n - 1)
        icount.append((1.0 / (span(ROWS)[:, None] * span(GRID_W)[None, :])).reshape(-1))
    return {"ident": np.eye(P, dtype=np.float32), "masks": masks, "icount": np.stack(icount)[None].astype(np.float32)}


def kernel(**inputs):
    import concourse.bacc as _bacc
    from concourse.bass_utils import run_bass_kernel_spmd as _run

    nc = _bacc.Bacc("TRN2", target_bir_lowering=False, num_devices=1)
    arrays, dram = {}, {}
    for name, a in {**{n: np.ascontiguousarray(inputs[n]) for n in _IN}, **constants()}.items():
        arrays[f"in_{name}"] = a
        dram[name] = nc.dram_tensor(f"in_{name}", a.shape, mybir.dt.from_np(a.dtype), kind="ExternalInput").ap()
    for name, shape in _SCRATCH.items():
        dram[name] = nc.dram_tensor(f"scr_{name}", shape, F32).ap()
    dram["out"] = nc.dram_tensor("out", (1, T, D), F32, kind="ExternalOutput").ap()
    build(nc, dram)
    return _run(nc, [arrays], core_ids=[0]).results[0]["out"]
```

```python
from contextlib import ExitStack

import numpy as np

import concourse.bass as bass
from concourse import mybir

F32 = mybir.dt.float32
F32R = mybir.dt.float32r
I32 = mybir.dt.int32
U8 = mybir.dt.uint8
U32 = mybir.dt.uint32
ALU = mybir.AluOpType
ACT = mybir.ActivationFunctionType
AX = mybir.AxisListType

P = 128
D = 1024
T = 1024
TC = 256
TA = T + TC
KT = D // P
NT = T // P
NH = 8
NC = T // P
LEVELS = 7
GRID_W = 64
ROWS = T // GRID_W
WINDOWS = (2, 4, 8, 16)
NE = 16
CAP = 2 * T // NE
ROUNDS = CAP // 8
EARLY = 3 * P
FF = 1024
EPS = 1e-6
N512 = 512

Q_OFF, I_OFF, FF_OFF, FB_OFF, OG_OFF = (j * D for j in range(5))
P_OFF = 5 * D
GA_OFF = P_OFF + P * len(WINDOWS)
GB_OFF = GA_OFF + D
IN_COLS = GB_OFF + D

NFILL = 5

R_BMOD, R_N1, R_N2, R_PS, R_HG, R_LB = 0, 48, 56, 64, 68, 69
N_PARAM = R_LB + 4 * NH


class Steps:

    def __init__(self, ctx, nc, name, steps, lead=1):
        self.sem = ctx.enter_context(nc.semaphore(name))
        self.n, self.lead = len(steps), lead
        self.credit = lead * self.n
        self.index = {s: i + 1 for i, s in enumerate(steps)}
        assert len(self.index) == self.n, name

    def after(self, it, step):
        return (it + self.lead) * self.n + self.index[step]


def matmul3(pe, out, w, x, start, stop):
    pe.matmul(out, w[0], x[0], start=start, stop=False)
    pe.matmul(out, w[0], x[1], start=False, stop=False)
    return pe.matmul(out, w[1], x[0], start=False, stop=stop)


def phase_modulate(nc, dram, keep, ux_head, ux_tail):
    NX = TA // P
    WSLOTS = 3
    NBOTH = 2 * D // N512
    BATCH = NX // 2
    BY_ACT = 2
    with ExitStack() as ctx:
        def sb(name, shape, dt=F32):
            return ctx.enter_context(nc.sbuf_tensor(name, shape, dt))

        def psum(name, shape):
            return ctx.enter_context(nc.psum_tensor(name, shape, F32))

        def sem(name):
            return ctx.enter_context(nc.semaphore(name))

        prow = sb("prow", [P, P])
        cvec = sb("cvec", [P, 2, KT])
        csig = sb("csig", [P, 2, KT])
        mod_rows = sb("mod_rows", [2, 2, N512])
        wmod = sb("wmod", [P, WSLOTS, KT, N512])
        xt = sb("xt", [P, NX, D])
        junk = sb("junk", [P, D])
        ssum = sb("ssum", [P, 16])
        mean = sb("mean", [P, 16])
        neghalf = sb("neghalf", [P, 16])
        rstd = sb("rstd", [P, 16])
        am = sb("am", [P, 16, 2])
        scale1 = sb("scale1", [P, 2, KT])
        lbd = sb("lbd", [P, 2, NH])
        ux = sb("ux", [P, 2, TA])
        ps_u = [psum(f"ps_u{i}", [P, 3, N512]) for i in range(2)]
        ps_col = psum("ps_col", [P, N512])
        ps_row = psum("ps_row", [P, N512])

        s_param = sem("a_param_landed")
        s_cvec = sem("a_cvec_landed")
        s_wm = [sem(f"a_wmod_landed{i}") for i in range(WSLOTS)]
        s_x = [sem(f"a_x_landed{i}") for i in range(NX // 2)]
        pe_cols = sem("a_pe_param_cols")
        pe_mod = sem("a_pe_mod_chunks")
        pe_turned = sem("a_pe_mod_rows_turned")
        pe_ux = sem("a_pe_ux_tiles")
        act_cs = sem("a_act_csig")
        act_lb = sem("a_act_lb")
        act_ss = sem("a_act_sums")
        act_xn = sem("a_act_normalised")
        act_ux = sem("a_act_ux")
        act_head = sem("a_act_ux_head")
        v_set = sem("a_v_setup")
        v_norm = sem("a_v_norm")
        v_ux = sem("a_v_ux")
        v_head = sem("a_v_ux_head")
        v_rows = sem("a_v_mod_rows")
        v_mean = sem("a_v_mean")
        v_scale1 = sem("a_v_scale1")
        p_half = sem("a_pool_neghalf")
        p_rstd = sem("a_pool_rstd")

        cols, ident, csil = keep["cols"], keep["ident"], keep["csil"]
        wm_v = dram["w_mod"].rearrange("a (p k) n -> (a p) k n", k=KT)

        block = ctx.enter_context(nc.Block())

        @block.sync
        def _(sp):
            sp.dma_start(ident[:], dram["ident"]).then_inc(s_param, 16)
            sp.dma_start(prow[R_BMOD:R_N1, :], dram["b_mod"].rearrange("a (m p) -> (a m) p", p=P)).then_inc(s_param, 16)
            sp.dma_start(prow[R_N1:R_N2, :], dram["norm1_g"].rearrange("a (m p) -> (a m) p", p=P)).then_inc(s_param, 16)
            sp.dma_start(prow[R_N2:R_PS, :], dram["norm2_g"].rearrange("a (m p) -> (a m) p", p=P)).then_inc(s_param, 16)
            sp.dma_start(prow[R_PS:R_HG, :], dram["pool_scale"].rearrange("a (m p) -> (a m) p", p=P)).then_inc(s_param, 16)
            sp.dma_start(prow[R_HG:R_LB, :], dram["hgrn_norm_g"]).then_inc(s_param, 16)
            sp.dma_start(prow[R_LB:N_PARAM, :], dram["lb_logits"].rearrange("a b (m p) -> (a b m) p", p=P)).then_inc(s_param, 16)
            sp.dma_start(cvec[:, 0, :], dram["c"].rearrange("a (p k) -> (a p) k", k=KT)).then_inc(s_cvec, 16)
            sp.dma_start(cvec[:, 1, :], dram["c_ctx"].rearrange("(p k) -> p k", k=KT)).then_inc(s_cvec, 16)

            def load_wmod(j):
                if j >= WSLOTS:
                    sp.wait_ge(pe_mod, j - WSLOTS + 1)
                sp.dma_start(wmod[:, j % WSLOTS, :, :], wm_v[:, :, j * N512:(j + 1) * N512]).then_inc(s_wm[j % WSLOTS], 16)

            for j in range(WSLOTS):
                load_wmod(j)
            for i in range(0, NX, 2):
                src = dram["x"][0, i * P:(i + 2) * P, :] if i < NT else dram["ctx"][0]
                sp.dma_start(xt[:, i:i + 2, :], src.rearrange("(t p) d -> p t d", p=P)).then_inc(s_x[i // 2], 16)
            for j in range(WSLOTS, NBOTH):
                load_wmod(j)

        @block.gpsimd
        def _(pool):
            pool.memset(neghalf[:], -0.5).then_inc(p_half, 1)
            pool.wait_ge(p_half, 1)
            for b in range(2):
                tiles = slice(b * BATCH, (b + 1) * BATCH)
                pool.wait_ge(v_mean, b + 1)
                pool.tensor_tensor(rstd[:, tiles], mean[:, tiles], neghalf[:, tiles], ALU.pow).then_inc(p_rstd, 1)

        @block.scalar
        def _(act):
            act.wait_ge(s_cvec, 32)
            act.activation(csig[:], cvec[:], ACT.Sigmoid).then_inc(act_cs, 1)
            act.wait_ge(v_set, 4)
            act.activation(keep["lb"][:], lbd[:], ACT.Sigmoid).then_inc(act_lb, 1)
            for i in range(NX):
                act.wait_ge(s_x[i // 2], 16)
                if i:
                    act.wait_ge(act_ss, i)
                act.activation(junk[:], xt[:, i, :], ACT.Square, accum_out=ssum[:, i:i + 1]).then_inc(act_ss, 1)
            act.wait_ge(p_rstd, 2)
            for i in range(NX - BY_ACT, NX):
                act.activation(xt[:, i, :], xt[:, i, :], ACT.Copy, scale=rstd[:, i:i + 1]).then_inc(act_xn, 1)
            act.wait_ge(v_scale1, 1)
            for k in range(KT):
                act.wait_ge(pe_ux, k + 1)
                if k >= 2:
                    act.wait_ge(v_ux, k - 1)
                for b in range(3):
                    side, width = (0, N512) if b < 2 else (1, TC)
                    last = act.activation(ux[:, k % 2, b * N512:b * N512 + width], ps_u[k % 2][:, b, 0:width], ACT.Identity,
                                          scale=scale1[:, side, k:k + 1], bias=am[:, k:k + 1, side])
                last.then_inc(act_ux, 1)
                if k % 2 == 0:
                    act.wait_ge(act_ux, k + 1)
                    act.activation(ux_head[:, k, :], ux[:, k % 2, :], ACT.Copy).then_inc(act_head, 1)

        @block.vector
        def _(v):
            v.wait_ge(act_cs, 1)
            for side in range(2):
                v.tensor_tensor(csil[:, :, side], cvec[:, side, :], csig[:, side, :], ALU.mult).then_inc(v_set, 1)
            v.wait_ge(pe_cols, 1)
            v.tensor_copy(cols[:, 0:N_PARAM], ps_col[:, 0:N_PARAM]).then_inc(v_set, 1)
            v.wait_ge(v_set, 3)
            lbl = cols[:, R_LB:N_PARAM].rearrange("p (a b m) -> p a b m", a=2, b=2)
            v.tensor_tensor(lbd[:], lbl[:, :, 0, :], lbl[:, :, 1, :], ALU.subtract).then_inc(v_set, 1)
            v.wait_ge(act_lb, 1)
            v.tensor_scalar(keep["olb"][:], keep["lb"][:], -1.0, 1.0, ALU.mult, ALU.add).then_inc(v_set, 1)

            def take_rows(j):
                v.wait_ge(pe_mod, j + 1)
                if j >= 2:
                    v.wait_ge(pe_turned, j - 1)
                src = ps_u[1][0:2, j, :] if j < 3 else ps_row[0:2, :]
                v.tensor_copy(mod_rows[:, j % 2, :], src).then_inc(v_rows, 1)

            def means(b):
                tiles = slice(b * BATCH, (b + 1) * BATCH)
                v.wait_ge(act_ss, (b + 1) * BATCH)
                v.tensor_scalar(mean[:, tiles], ssum[:, tiles], 1.0 / D, EPS, ALU.mult, ALU.add).then_inc(v_mean, 1)

            def normalise(lo, hi):
                for i in range(lo, hi):
                    v.tensor_scalar(xt[:, i, :], xt[:, i, :], rstd[:, i:i + 1], None, ALU.mult).then_inc(v_norm, 1)

            for j in range(3):
                take_rows(j)
            means(0)
            v.wait_ge(p_rstd, 1)
            normalise(0, BATCH)
            means(1)
            v.wait_ge(p_rstd, 2)
            normalise(BATCH, NX - BY_ACT)
            take_rows(3)
            v.wait_ge(pe_turned, NBOTH)
            v.tensor_tensor(am[:, 0:16, :], ps_col[:, 0:32].rearrange("p (m s) -> p m s", s=2),
                            cols[:, 0:16].rearrange("p (m s) -> p m s", s=1).broadcast_to([P, 16, 2]), ALU.add).then_inc(v_set, 1)
            v.wait_ge(v_set, 6)
            for side in range(2):
                last = v.scalar_tensor_tensor(out=scale1[:, side, :], in0=am[:, KT:2 * KT, side], scalar=1.0,
                                              in1=cols[:, R_N1:R_N1 + KT], op0=ALU.add, op1=ALU.mult)
            last.then_inc(v_scale1, 1)

            for k in range(KT):
                if k % 2 == 0:
                    v.wait_ge(act_head, k // 2 + 1)
                else:
                    v.wait_ge(act_ux, k + 1)
                    v.tensor_copy(ux_head[:, k, :], ux[:, k % 2, :]).then_inc(v_head, 1)
                    v.wait_ge(v_head, k // 2 + 1)
                v.tensor_tensor(ux_tail[:, k, :], ux[:, k % 2, :], ux_head[:, k, :].bitcast(F32), ALU.subtract).then_inc(v_ux, 1)

        @block.tensor
        def _(pe):
            pe.wait_ge(s_param, 7 * 16)
            pe.transpose(ps_col[:, 0:N_PARAM], prow[0:N_PARAM, :], ident[0:N_PARAM, 0:N_PARAM]).then_inc(pe_cols, 1)

            def both_rows(j):
                pe.wait_ge(s_wm[j % WSLOTS], 16 * (j // WSLOTS + 1))
                dst = ps_u[1][0:2, j, :] if j < 3 else ps_row[0:2, :]
                for k in range(KT):
                    last = pe.matmul(dst, csil[:, k, :], wmod[:, j % WSLOTS, k, :], start=(k == 0), stop=(k == KT - 1))
                last.then_inc(pe_mod, 1)

            def turn_rows(j):
                pe.wait_ge(v_rows, j + 1)
                for m in range(4):
                    at = 2 * (4 * j + m)
                    last = pe.transpose(ps_col[:, at:at + 2], mod_rows[:, j % 2, m * P:(m + 1) * P], ident[0:2, 0:2])
                last.then_inc(pe_turned, 1)

            pe.wait_ge(v_set, 3)
            both_rows(0)
            both_rows(1)
            turn_rows(0)
            both_rows(2)
            turn_rows(1)
            turn_rows(2)
            both_rows(3)
            pe.wait_ge(v_norm, NX - BY_ACT)
            pe.wait_ge(act_xn, BY_ACT)
            for k in range(KT):
                if k >= 2:
                    pe.wait_ge(act_ux, k - 1)
                if k == 1:
                    turn_rows(3)
                for i in range(NX):
                    last = pe.transpose(ps_u[k % 2][:, i // 4, (i % 4) * P:(i % 4 + 1) * P], xt[:, i, k * P:(k + 1) * P], ident[:])
                last.then_inc(pe_ux, 1)


def phase_pool_gates(nc, dram, keep, ux_head, ux_tail):
    NG = len(WINDOWS)
    NB = 2 * KT - NFILL
    PAD = max(WINDOWS) // 2
    with ExitStack() as ctx:
        def sb(name, shape, dt=F32):
            return ctx.enter_context(nc.sbuf_tensor(name, shape, dt))

        def psum(name, shape):
            return ctx.enter_context(nc.psum_tensor(name, shape, F32))

        def sem(name):
            return ctx.enter_context(nc.semaphore(name))

        w_raw = sb("b_w_raw", [P, 2, KT, P])
        w_head = sb("b_w_head", [P, 2, KT, P], F32R)
        w_tail = sb("b_w_tail", [P, 2, KT, P], F32R)
        wpool = sb("b_wpool", [P, NG, P])
        icount = sb("b_icount", [P, NG, T])
        colpad = sb("b_colpad", [P, ROWS, GRID_W + 2 * PAD])
        colsum = [sb(f"b_colsum{i}", [P, ROWS, GRID_W + 2 * PAD]) for i in range(2)]
        rowpad = sb("b_rowpad", [P, ROWS + 2 * PAD, GRID_W])
        rowsum = [sb(f"b_rowsum{i}", [P, ROWS + 2 * PAD, GRID_W]) for i in range(2)]
        resid = sb("b_resid", [P, 2, T])
        yb = sb("b_yb", [P, 2, T])
        zero = sb("b_zero", [P, 1])
        gate = sb("b_gate", [P, 2, T])
        ps_z = [psum(f"b_ps_z{i}", [P, T]) for i in range(2)]
        ps_y = psum("b_ps_y", [P, T])

        s_raw = [sem(f"b_w_landed{i}") for i in range(2)]
        s_const = sem("b_const_landed")
        s_yb = [sem(f"b_yb_stored{i}") for i in range(2)]
        s_gate = [sem(f"b_gate_stored{i}") for i in range(2)]
        pool_head = sem("b_pool_head")
        pool_tail = sem("b_pool_tail")
        pool_zero = sem("b_pool_zero")
        pe_block = sem("b_pe_block")
        pe_y = sem("b_pe_y")
        v_pool = sem("b_v_pooling")
        v_taken = sem("b_v_taken")
        v_resid = sem("b_v_resid")
        act_y = sem("b_act_y")
        act_gate = sem("b_act_gate")
        cols = keep["cols"]
        w_in = dram["w_in"].rearrange("a (k p) n -> p (a k) n", p=P)

        block = ctx.enter_context(nc.Block())

        @block.sync
        def _(sp):
            def load(n, src):
                sp.dma_start(w_raw[:, n % 2, :, :], src).then_inc(s_raw[n % 2], 16)

            for n in range(NG):
                if n >= 2:
                    sp.wait_ge(pool_tail, n - 1)
                load(n, w_in[:, :, P_OFF + n * P:P_OFF + (n + 1) * P])
                if n == 1:
                    sp.dma_start(wpool[:], dram["w_pool"].rearrange("a j ci co -> ci (a j) co")).then_inc(s_const, 16)
                    sp.dma_start(icount[:], dram["icount"].broadcast_to([P, NG, T])).then_inc(s_const, 16)
            def load_gate(b, slot):
                at = GA_OFF + (NFILL + b) * P
                at = at if isinstance(b, int) else sp.snap(at)
                sp.wait_ge(pool_tail, NG + b - 1)
                load(slot, w_in[:, :, bass.ds(at, P)])

            with sp.Fori(0, NB // 2) as m:
                load_gate(2 * m, 0)
                load_gate(2 * m + 1, 1)
            load_gate(NB - 1, 0)

        @block.gpsimd
        def _(pool):
            pool.memset(colpad[:], 0.0).then_inc(pool_zero, 1)
            pool.memset(rowpad[:], 0.0).then_inc(pool_zero, 1)
            pool.memset(zero[:], 0.0).then_inc(pool_zero, 1)
            pool.wait_ge(pool_zero, 3)

            def split(n, slot, landed):
                pool.wait_ge(s_raw[slot], landed)
                if not (isinstance(n, int) and n < 2):
                    pool.wait_ge(pe_block, n - 1)
                pool.tensor_tensor(w_head[:, slot], w_raw[:, slot], zero[:].unsqueeze(2).broadcast_to([P, KT, P]), ALU.add).then_inc(pool_head, 1)
                pool.wait_ge(pool_head, n + 1)
                pool.tensor_tensor(w_tail[:, slot], w_raw[:, slot], w_head[:, slot].bitcast(F32), ALU.subtract).then_inc(pool_tail, 1)

            for n in range(NG):
                split(n, n % 2, 16 * (n // 2 + 1))
            with pool.Fori(0, NB // 2) as m:
                for g in range(2):
                    split(NG + 2 * m + g, g, 16 * (NG // 2 + 1) + 16 * m)
            split(NG + NB - 1, 0, 16 * (NG // 2 + 1) + 16 * (NB // 2))

        @block.tensor
        def _(pe):
            def project(n, slot):
                pe.wait_ge(pool_tail, n + 1)
                for half in range(2):
                    for k in range(KT):
                        last = matmul3(pe, ps_z[slot][:, half * N512:(half + 1) * N512],
                                       (w_head[:, slot, k, :], w_tail[:, slot, k, :]),
                                       (ux_head[:, k, half * N512:(half + 1) * N512], ux_tail[:, k, half * N512:(half + 1) * N512]),
                                       k == 0, k == KT - 1)
                last.then_inc(pe_block, 1)

            def pool_product(j):
                pe.wait_ge(v_resid, j + 1)
                if j >= 1:
                    pe.wait_ge(act_y, j)
                if j == 0:
                    pe.wait_ge(s_const, 32)
                for half in range(2):
                    last = pe.matmul(ps_y[:, half * N512:(half + 1) * N512], wpool[:, j, :],
                                     resid[:, j % 2, half * N512:(half + 1) * N512], start=True, stop=True)
                last.then_inc(pe_y, 1)

            for n in range(NG):
                if n >= 2:
                    pe.wait_ge(v_taken, n - 1)
                project(n, n % 2)
                if n >= 2:
                    pool_product(n - 2)
            pe.wait_ge(v_taken, NG)
            with pe.Fori(0, NB // 2) as m:
                for g in range(2):
                    pe.wait_ge(act_gate, 2 * m + g + 1)
                    project(NG + 2 * m + g, g)
            pe.wait_ge(act_gate, NB)
            project(NG + NB - 1, 0)
            pool_product(NG - 2)
            pool_product(NG - 1)

        @block.scalar
        def _(act):
            act.sem_inc(act_gate, 2)

            def scale_y(j):
                act.wait_ge(pe_y, j + 1)
                if j >= 2:
                    act.wait_ge(s_yb[j % 2], 16 * (j // 2))
                act.activation(yb[:, j % 2, :], ps_y[:], ACT.Copy, scale=cols[:, R_PS + j:R_PS + j + 1]).then_inc(act_y, 1)
                act.wait_ge(act_y, j + 1)
                act.dma_start(dram["yb"][j * P:(j + 1) * P, :], yb[:, j % 2, :]).then_inc(s_yb[j % 2], 16)

            scale_y(0)
            scale_y(1)
            gate_rows = dram["gates"].rearrange("g d t -> (g d) t")

            def gate_block(m, g):
                b = 2 * m + g
                act.wait_ge(pe_block, NG + b + 1)
                act.wait_ge(s_gate[g], 16 * (m + 1))
                act.activation(gate[:, g, :], ps_z[g][:], ACT.Sigmoid).then_inc(act_gate, 1)
                act.wait_ge(act_gate, b + 3)
                act.dma_start(gate_rows[bass.ds((NFILL + b) * P, P), :], gate[:, g, :]).then_inc(s_gate[g], 16)

            with act.Fori(0, NB // 2) as m:
                gate_block(m, 0)
                gate_block(m, 1)
            gate_block(NB // 2, 0)
            scale_y(2)
            scale_y(3)
            for g in range(2):
                act.wait_ge(s_gate[g], 16 * (NB // 2 + 2 - g))
                act.wait_ge(s_yb[g], 32)

        @block.vector
        def _(v):
            for g in range(2):
                v.sem_inc(s_gate[g], 16)
            v.wait_ge(pool_zero, 2)
            v.wait_ge(s_const, 32)
            done = 0
            for j, w in enumerate(WINDOWS):
                v.wait_ge(pe_block, j + 1)
                v.tensor_copy(colpad[:, :, PAD:PAD + GRID_W], ps_z[j % 2][:].rearrange("p (r c) -> p r c", c=GRID_W)).then_inc(v_taken, 1)
                v.wait_ge(v_taken, j + 1)
                src, span, base, turn = colpad, 1, PAD - w // 2, 0
                while span < w:
                    last_step = 2 * span == w
                    width = GRID_W + w - 2 * span
                    dst = rowpad[:, PAD:PAD + ROWS, :] if last_step else colsum[turn][:, :, 0:width]
                    v.tensor_tensor(dst, src[:, :, base:base + width], src[:, :, base + span:base + span + width], ALU.add).then_inc(v_pool, 1)
                    done += 1
                    v.wait_ge(v_pool, done)
                    src, base, turn = colsum[turn], 0, 1 - turn
                    span *= 2
                src, span, base, turn = rowpad, 1, PAD - w // 2, 0
                while span < w:
                    height = ROWS + w - 2 * span
                    dst = rowsum[turn]
                    v.tensor_tensor(dst[:, 0:height, :], src[:, base:base + height, :], src[:, base + span:base + span + height, :],
                                    ALU.add).then_inc(v_pool, 1)
                    done += 1
                    v.wait_ge(v_pool, done)
                    src, base, turn = dst, 0, 1 - turn
                    span *= 2
                total = src[:, 0:ROWS, :].rearrange("p r c -> p (r c)")
                v.tensor_tensor(rowsum[turn][:, 0:ROWS, :].rearrange("p r c -> p (r c)"), total, icount[:, j, :], ALU.mult).then_inc(v_pool, 1)
                done += 1
                v.wait_ge(v_pool, done)
                if j >= 2:
                    v.wait_ge(pe_y, j - 1)
                v.tensor_tensor(resid[:, j % 2, :].rearrange("p (r c) -> p r c", c=GRID_W), rowsum[turn][:, 0:ROWS, :],
                                colpad[:, :, PAD:PAD + GRID_W], ALU.subtract).then_inc(v_resid, 1)
                v.wait_ge(v_resid, j + 1)


def pair_view(t, level, cols, first):
    half = 1 << level
    step = (cols if first == 0 else -cols) + half
    return [[2 * half, cols // (2 * half)], [step, 2], [1, half]], first * cols, t


def pair_ap(t, level, first, lo=0, n=T):
    dims, base, tile = pair_view(t, level, T, first)
    dims[0][1] = n // dims[0][0]
    return bass.AP(tile, base + lo, [[2 * T, P]] + dims)


def total_ap(t, level, width, plane0, entry0, entry1):
    n = T >> level
    other = 1 - plane0
    step = (other - plane0) * n + entry1 - entry0
    return bass.AP(t, plane0 * n + entry0, [[2 * width, P], [2, n // 2], [step, 2], [0, 1 << level]])


def phase_heads(nc, dram, keep, ux_head, ux_tail):
    TASKS = ["q0", "q1", "a0", "a1", "b0", "b1", "c", "v0", "v1", "vc", "g0", "g1"]
    BLOCKS = [Q_OFF, FF_OFF, FB_OFF, I_OFF, OG_OFF]
    HALVES = 2 * len(BLOCKS)
    RING = 5
    LAST_USE = ["q1", "c", "c", "vc", "g1"]
    FILL = [name for name in TASKS if name not in ("c", "vc")]
    assert len(FILL) == 2 * NFILL

    def fill_steps(name):
        return 2 if name in ("b1", "v1") else 1

    with ExitStack() as ctx:
        def sb(name, shape, dt=F32):
            return ctx.enter_context(nc.sbuf_tensor("h_" + name, shape, dt))

        def psum(name, shape):
            return ctx.enter_context(nc.psum_tensor("h_ps_" + name, shape, F32))

        def sem(name):
            return ctx.enter_context(nc.semaphore("h_" + name))

        w_raw = sb("w_raw", [P, RING, KT // 2, P])
        w_head = sb("w_head", [P, RING, KT // 2, P], F32R)
        w_tail = sb("w_tail", [P, RING, KT // 2, P], F32R)
        masks = sb("masks", [P, LEVELS, P], U8)
        sig = sb("sig", [P, N512])
        q_next = sb("q_next", [P, T])
        f_next = sb("f_next", [P, 2, TA])
        v_next = sb("v_next", [P, TA])
        og_gate = sb("og_gate", [P, T])
        v_tok = sb("v_tok", [P, NC + TC // P, P])
        tot = [sb("tot_even", [P, 2, T]), sb("tot_odd", [P, 2, T // 2])]
        q2 = sb("q2", [P, 2, T])
        k2 = sb("k2", [P, 2, T])
        stage = sb("stage", [P, T])
        reach = sb("reach", [P, 2, TC])
        kc_tok = sb("kc_tok", [P, 2, TC // P, P])
        scores = sb("scores", [P, NC, P])
        k_tok = sb("k_tok", [P, NC, P])
        out = sb("out", [P, T])
        masks_wide = out[:, 0:LEVELS * P].bitcast(I32).rearrange("p (l t) -> p l t", t=P)
        state = sb("state", [P, 2, NC, P])
        zeros = sb("zeros", [P, TC])
        junk = sb("junk", [P, P])
        sumsq = sb("sumsq", [P, NC])
        meansq = sb("meansq", [P, NC])
        neghalf = sb("neghalf", [P, NC])
        rstd = sb("rstd", [P, NC])
        ps_z = psum("z", [P, 2, N512])
        ps_x = psum("x", [P, NC, P])
        ps_o = psum("o", [P, NC, P])
        ps_w = psum("w", [P, NC, P])

        s_raw = [sem(f"w_landed{i}") for i in range(RING)]
        s_mask = sem("masks_landed")
        s_out = sem("out_stored")
        s_zero = sem("constants_set")
        s_fill = sem("gates_stored")
        pe_z = Steps(ctx, nc, "h_pe_z", TASKS)
        act_z = Steps(ctx, nc, "h_act_z", TASKS)
        v_z = Steps(ctx, nc, "h_v_z", ["q0", "q1", "g0", "g1"])
        pool_w = Steps(ctx, nc, "h_pool_w", [f"{part}{n}" for n in range(HALVES) for part in ("head", "tail")])
        pe_r = Steps(ctx, nc, "h_pe_r", ["diag", "kc", "level0", "s0"] + [f"level{l}" for l in range(1, LEVELS)] +
                     ["kf", "uf", "kb", "ub", "o", "ot"])
        act_r = Steps(ctx, nc, "h_act_r", ["pairs0", "diag", "kc"] + [f"pairs{l}" for l in range(1, LEVELS)] +
                      ["kf", "kb"] + [f"sq{c}" for c in range(NC)] + ["scaled"])
        v_p = Steps(ctx, nc, "h_v_p", ["f0", "f1", "keys", "queries", "ksum", "fc0", "fc1", "reach", "kc", "krc"])
        level_steps = [[f"{s}{l}" for s in ("k", "q", "t", "p")] for l in range(LEVELS)]
        v_r = Steps(ctx, nc, "h_v_r", level_steps[0] + ["s0"] + sum(level_steps[1:], []) +
                    [f"sf{c}" for c in range(NC - 1)] + [f"sb{c}" for c in range(NC - 1)] + ["mean", "out"])
        pe_v = Steps(ctx, nc, "h_pe_v", ["v"])
        act_v = Steps(ctx, nc, "h_act_v", ["v"])
        pool_r = Steps(ctx, nc, "h_pool_r", ["rstd"])

        cols, ident, lb, olb = keep["cols"], keep["ident"], keep["lb"], keep["olb"]
        w_in = dram["w_in"].rearrange("a (k p) n -> p (a k) n", p=P)

        block = ctx.enter_context(nc.Block())

        @block.sync
        def _(sp):
            sp.dma_start(masks_wide, dram["masks"]).then_inc(s_mask, 16)

            def load_weights(g):
                for n in range(HALVES):
                    if isinstance(g, int):
                        at = BLOCKS[n // 2] + g * P if g < NH else GA_OFF + (n // 2) * P
                    else:
                        at = sp.snap(BLOCKS[n // 2] + g * P)
                    k0 = (n % 2) * (KT // 2)
                    before = n - RING
                    sp.wait_ge(pool_w.sem, pool_w.after(g, f"tail{before}") if before >= 0 else pool_w.after(g - 1, f"tail{before + HALVES}"))
                    sp.dma_start(w_raw[:, n % RING], w_in[:, k0:k0 + KT // 2, bass.ds(at, P)]).then_inc(s_raw[n % RING], 16)

            load_weights(0)
            with sp.Fori(1, NH) as g:
                load_weights(g)
            load_weights(NH)

        @block.gpsimd
        def _(pool):
            pool.sem_inc(pool_w.sem, pool_w.credit)
            pool.sem_inc(pool_r.sem, pool_r.credit)
            pool.memset(neghalf[:], -0.5).then_inc(s_zero, 1)
            pool.memset(zeros[:], 0.0).then_inc(s_zero, 1)
            pool.memset(reach[:], 1.0).then_inc(s_zero, 1)
            pool.wait_ge(s_zero, 3)

            def split(g, n):
                slot = n % RING
                pool.wait_ge(s_raw[slot], 32 * g + 16 * (n // RING + 1))
                before = n - RING
                pool.wait_ge(pe_z.sem, pe_z.after(g, LAST_USE[before // 2]) if before >= 0
                             else pe_z.after(g - 1, LAST_USE[(before + HALVES) // 2]))
                pool.tensor_tensor(w_head[:, slot], w_raw[:, slot], zeros[:, 0:1].unsqueeze(2).broadcast_to([P, KT // 2, P]), ALU.add).then_inc(pool_w.sem, 1)
                pool.wait_ge(pool_w.sem, pool_w.after(g, f"head{n}"))
                pool.tensor_tensor(w_tail[:, slot], w_raw[:, slot], w_head[:, slot].bitcast(F32), ALU.subtract).then_inc(pool_w.sem, 1)

            def head(h, g):
                for n in range(HALVES):
                    split(g, n)
                pool.wait_ge(v_r.sem, v_r.after(h, "mean"))
                pool.tensor_tensor(rstd[:], meansq[:], neghalf[:], ALU.pow).then_inc(pool_r.sem, 1)

            for n in range(HALVES):
                split(0, n)
            with pool.Fori(0, NH) as h:
                head(h, h + 1)

        @block.tensor
        def _(pe):
            pe.sem_inc(pe_z.sem, pe_z.credit)
            pe.sem_inc(pe_r.sem, pe_r.credit)
            pe.sem_inc(pe_v.sem, pe_v.credit)
            def weights(b, k):
                n = 2 * b + k // (KT // 2)
                return w_head[:, n % RING, k % (KT // 2), :], w_tail[:, n % RING, k % (KT // 2), :]

            def tokens(k, lo, n):
                return ux_head[:, k, lo:lo + n], ux_tail[:, k, lo:lo + n]

            def features(out_ap, b, lo, n):
                for k in range(KT):
                    last = matmul3(pe, out_ap, weights(b, k), tokens(k, lo, n), k == 0, k == KT - 1)
                return last

            def task(g, name, fill=False):
                i = TASKS.index(name)
                bank = ps_z[:, i % 2, :]
                prev = TASKS[i - 2]
                at = g if i >= 2 else g - 1
                if prev in v_z.index and not (fill and i >= 2):
                    pe.wait_ge(v_z.sem, v_z.after(at, prev))
                else:
                    pe.wait_ge(act_z.sem, act_z.after(at, prev))
                b = {"q": [0], "a": [1], "b": [2], "c": [1, 2], "v": [3], "g": [4]}[name[0]]
                pe.wait_ge(pool_w.sem, pool_w.after(g, f"tail{2 * b[-1] + 1}"))
                if name == "c":
                    for j in range(2):
                        last = features(bank[:, j * TC:(j + 1) * TC], b[j], T, TC)
                elif name == "vc":
                    last = features(bank[:, 0:TC], b[0], T, TC)
                elif name[1] == "0":
                    last = features(bank, b[0], 0, N512)
                else:
                    last = features(bank, b[0], N512, N512)
                last.then_inc(pe_z.sem, fill_steps(name) if fill else 1)

            def turn_values(h):
                pe.wait_ge(act_z.sem, act_z.after(h, "vc"))
                pe.wait_ge(v_r.sem, v_r.after(h - 1, f"sb{NC - 2}"))
                pe.wait_ge(act_r.sem, act_r.after(h - 1, "kb"))
                for c in range(NC):
                    pe.transpose(ps_x[:, c, :], v_next[:, c * P:(c + 1) * P], ident[:])
                for t in range(TC // P):
                    last = pe.transpose(ps_w[:, 6 + t, :], v_next[:, T + t * P:T + (t + 1) * P], ident[:])
                last.then_inc(pe_v.sem, 1)

            def recur_context_keys(h):
                pe.wait_ge(v_p.sem, v_p.after(h, "krc"))
                pe.wait_ge(act_r.sem, act_r.after(h - 1, "scaled"))
                pe.wait_ge(v_r.sem, v_r.after(h - 1, "out"))
                for d in range(2):
                    for t in range(TC // P):
                        last = pe.transpose(ps_w[:, 2 * d + t, :], f_next[:, d, T + t * P:T + (t + 1) * P], ident[:])
                last.then_inc(pe_r.sem, 1)

            def recur_diagonal(h):
                pe.wait_ge(v_p.sem, v_p.after(h, "ksum"))
                pe.wait_ge(act_v.sem, act_v.after(h, "v"))
                for c in range(NC):
                    last = pe.matmul(ps_x[:, c, :], k_tok[:, c, :], q_next[:, c * P:(c + 1) * P], start=True, stop=True)
                last.then_inc(pe_r.sem, 1)

            def recur_start_state(h):
                pe.wait_ge(act_r.sem, act_r.after(h, "kc"))
                pe.wait_ge(act_v.sem, act_v.after(h, "v"))
                for d in range(2):
                    for t in range(TC // P):
                        last = pe.matmul(ps_w[:, 4 + d, :], kc_tok[:, d, t, :], v_tok[:, NC + t, :], start=(t == 0), stop=(t == TC // P - 1))
                last.then_inc(pe_r.sem, 1)

            def recur_level(h, l):
                if l == 0:
                    pe.wait_ge(act_r.sem, act_r.after(h, "diag"))
                else:
                    pe.wait_ge(act_r.sem, act_r.after(h, f"pairs{l}"))
                    pe.wait_ge(v_r.sem, v_r.after(h, f"p{l - 1}"))
                for c in range(NC):
                    last = pe.matmul(ps_x[:, c, :], stage[:, c * P:(c + 1) * P], pair_ap(q2, l, 0, c * P, P), start=True, stop=True)
                last.then_inc(pe_r.sem, 1)

            def recur_keys(h, plane):
                if plane == 0:
                    pe.wait_ge(v_r.sem, v_r.after(h, f"k{LEVELS - 1}"))
                    pe.wait_ge(v_r.sem, v_r.after(h, "s0"))
                else:
                    pe.wait_ge(act_r.sem, act_r.after(h, "kf"))
                for c in range(NC):
                    last = pe.transpose(ps_w[:, c, :], k2[:, plane, c * P:(c + 1) * P], ident[:])
                last.then_inc(pe_r.sem, 1)

            def recur_updates(h, plane):
                if plane == 0:
                    pe.wait_ge(act_r.sem, act_r.after(h, "kf"))
                    pe.wait_ge(v_r.sem, v_r.after(h, f"p{LEVELS - 1}"))
                else:
                    pe.wait_ge(act_r.sem, act_r.after(h, "kb"))
                    pe.wait_ge(v_r.sem, v_r.after(h, f"sf{NC - 2}"))
                for c in range(NC):
                    last = pe.matmul(ps_x[:, c, :], k_tok[:, c, :], v_tok[:, c, :], start=True, stop=True)
                last.then_inc(pe_r.sem, 1)

            def recur_output(h):
                pe.wait_ge(v_r.sem, v_r.after(h, f"sb{NC - 2}"))
                pe.wait_ge(act_r.sem, act_r.after(h - 1, "scaled"))
                for c in range(NC):
                    pe.matmul(ps_o[:, c, :], scores[:, c, :], v_tok[:, c, :], start=True, stop=False)
                    pe.matmul(ps_o[:, c, :], q2[:, 1, c * P:(c + 1) * P], state[:, 0, c, :], start=False, stop=False)
                    last = pe.matmul(ps_o[:, c, :], q2[:, 0, c * P:(c + 1) * P], state[:, 1, c, :], start=False, stop=True)
                last.then_inc(pe_r.sem, 1)

            def recur_turn(h):
                pe.wait_ge(act_r.sem, act_r.after(h, "scaled"))
                for c in range(NC):
                    last = pe.transpose(ps_w[:, c, :], stage[:, c * P:(c + 1) * P], ident[:])
                last.then_inc(pe_r.sem, 1)

            def head(h, g):
                def t(name):
                    if g is not None:
                        task(g, name)
                    elif name in FILL:
                        task(NH, name, fill=True)

                recur_diagonal(h)
                recur_context_keys(h)
                recur_level(h, 0)
                recur_start_state(h)
                for l, name in enumerate(("q0", "q1", "a0", "a1", "b0", "b1"), 1):
                    t(name)
                    recur_level(h, l)
                t("c")
                recur_keys(h, 0)
                t("v0")
                recur_updates(h, 0)
                recur_keys(h, 1)
                t("v1")
                recur_updates(h, 1)
                t("vc")
                recur_output(h)
                if g is not None:
                    turn_values(g)
                t("g0")
                t("g1")
                recur_turn(h)

            for name in TASKS:
                task(0, name)
                if name == "vc":
                    turn_values(0)
            with pe.Fori(0, NH - 1) as h:
                head(h, h + 1)
            head(NH - 1, None)

        @block.scalar
        def _(act):
            act.sem_inc(act_z.sem, act_z.credit)
            act.sem_inc(act_r.sem, act_r.credit)
            act.sem_inc(act_v.sem, act_v.credit)

            def evacuate(g, name):
                i = TASKS.index(name)
                bank = ps_z[:, i % 2, :]
                act.wait_ge(pe_z.sem, pe_z.after(g, name))
                if name[0] in "qg":
                    prev = {"q0": ("g1", 1), "q1": ("q0", 0), "g0": ("q1", 0), "g1": ("g0", 0)}[name]
                    act.wait_ge(v_z.sem, v_z.after(g - prev[1] if prev[1] else g, prev[0]))
                    last = act.activation(sig[:], bank, ACT.Sigmoid)
                elif name[0] in "ab":
                    d, half = "ab".index(name[0]), int(name[1])
                    last = act.activation(f_next[:, d, half * N512:(half + 1) * N512], bank, ACT.Sigmoid)
                elif name == "c":
                    act.wait_ge(pe_r.sem, pe_r.after(g - 1, "kc"))
                    last = act.activation(f_next[:, :, T:TA], bank.rearrange("p (d t) -> p d t", d=2), ACT.Sigmoid)
                else:
                    lo, n = {"v0": (0, N512), "v1": (N512, N512), "vc": (T, TC)}[name]
                    act.wait_ge(pe_v.sem, pe_v.after(g - 1, "v"))
                    last = act.activation(v_next[:, lo:lo + n], bank[:, 0:n], ACT.Copy)
                last.then_inc(act_z.sem, 1)

            def evacuate_gate(name):
                n = FILL.index(name)
                dst = [f_next[:, 0, 0:N512], f_next[:, 0, N512:T], f_next[:, 1, 0:N512], f_next[:, 1, N512:T],
                       q_next[:, 0:N512], q_next[:, N512:T], v_next[:, 0:N512], v_next[:, N512:T],
                       kc_tok[:].rearrange("p d t f -> p (d t f)"), sig[:]][n]
                act.wait_ge(pe_z.sem, pe_z.after(NH, name))
                act.activation(dst, ps_z[:, TASKS.index(name) % 2, :], ACT.Sigmoid).then_inc(act_z.sem, fill_steps(name))
                act.wait_ge(act_z.sem, act_z.after(NH, name))
                at = n // 2 * P
                act.dma_start(dram["gates"][0, at:at + P, n % 2 * N512:(n % 2 + 1) * N512], dst).then_inc(s_fill, 16)

            def take_values(h):
                act.wait_ge(pe_v.sem, pe_v.after(h, "v"))
                act.activation(v_tok[:, 0:NC, :], ps_x[:], ACT.Copy)
                act.activation(v_tok[:, NC:NC + TC // P, :], ps_w[:, 6:8, :], ACT.Copy).then_inc(act_v.sem, 1)

            def gather_pairs(h, l):
                if l == 0:
                    act.wait_ge(v_p.sem, v_p.after(h, "keys"))
                    act.wait_ge(pe_r.sem, pe_r.after(h - 1, "ot"))
                else:
                    act.wait_ge(v_r.sem, v_r.after(h, f"k{l - 1}"))
                act.activation(stage[:], pair_ap(k2, l, 0), ACT.Copy).then_inc(act_r.sem, 1)

            def head(h, g):
                def t(name):
                    if g is not None:
                        evacuate(g, name)
                    elif name in FILL:
                        evacuate_gate(name)

                gather_pairs(h, 0)
                act.wait_ge(pe_r.sem, pe_r.after(h, "diag"))
                act.activation(scores[:], ps_x[:], ACT.Copy).then_inc(act_r.sem, 1)
                act.wait_ge(pe_r.sem, pe_r.after(h, "kc"))
                act.activation(kc_tok[:].rearrange("p d t f -> p (d t) f"), ps_w[:, 0:4, :], ACT.Copy).then_inc(act_r.sem, 1)
                evacuate(h, "g1")
                if not isinstance(h, int) or h >= 1:
                    store(h - 1)
                for l, name in enumerate(("q0", "q1", "a0", "a1", "b0", "b1"), 1):
                    gather_pairs(h, l)
                    t(name)
                t("c")
                act.wait_ge(pe_r.sem, pe_r.after(h, "kf"))
                act.activation(k_tok[:], ps_w[:], ACT.Copy).then_inc(act_r.sem, 1)
                t("v0")
                act.wait_ge(pe_r.sem, pe_r.after(h, "kb"))
                act.activation(k_tok[:], ps_w[:], ACT.Copy).then_inc(act_r.sem, 1)
                t("v1")
                t("vc")
                act.wait_ge(pe_r.sem, pe_r.after(h, "o"))
                for c in range(NC):
                    act.wait_ge(act_r.sem, act_r.after(h, f"sq{c - 1}" if c else "kb"))
                    act.activation(junk[:], ps_o[:, c, :], ACT.Square, accum_out=sumsq[:, c:c + 1]).then_inc(act_r.sem, 1)
                if g is not None:
                    take_values(g)
                act.wait_ge(pool_r.sem, pool_r.after(h, "rstd"))
                for c in range(NC):
                    last = act.activation(stage[:, c * P:(c + 1) * P], ps_o[:, c, :], ACT.Copy, scale=rstd[:, c:c + 1])
                last.then_inc(act_r.sem, 1)
                t("g0")
                if g is None:
                    t("g1")

            def store(h):
                act.wait_ge(v_r.sem, v_r.after(h, "out"))
                act.dma_start(dram["og"][bass.ds(h * P, P), :], out[:]).then_inc(s_out, 16)

            for name in TASKS[:-1]:
                evacuate(0, name)
            take_values(0)
            head(0, 1)
            with act.Fori(1, NH - 1) as h:
                head(h, h + 1)
            head(NH - 1, None)
            store(NH - 1)
            act.wait_ge(s_out, 16 * (NH + 1))
            act.wait_ge(s_fill, 16 * len(FILL))

        @block.vector
        def _(v):
            v.sem_inc(v_z.sem, v_z.credit)
            v.sem_inc(v_r.sem, v_r.credit)
            v.sem_inc(v_p.sem, v_p.credit)
            v.wait_ge(s_zero, 3)
            v.wait_ge(s_mask, 16)
            v.tensor_copy(masks[:], masks_wide).then_inc(s_zero, 1)
            v.wait_ge(s_zero, 4)

            def silu(g, name, dst):
                half = int(name[1])
                v.wait_ge(act_z.sem, act_z.after(g, name))
                bank = ps_z[:, TASKS.index(name) % 2, :]
                v.tensor_tensor(dst[:, half * N512:(half + 1) * N512], bank, sig[:], ALU.mult).then_inc(v_z.sem, 1)

            def done(h, step):
                v.wait_ge(v_r.sem, v_r.after(h, step))

            def prepared(h, step):
                v.wait_ge(v_p.sem, v_p.after(h, step))

            def prepare_keys(h):
                v.wait_ge(act_z.sem, act_z.after(h, "c"))
                v.wait_ge(pe_r.sem, pe_r.after(h - 1, "ub"))
                done(h - 1, f"sb{NC - 2}")
                for d in range(2):
                    v.tensor_scalar(tot[0][:, d, :], f_next[:, d, 0:T], olb[:, d, bass.ds(h, 1)], lb[:, d, bass.ds(h, 1)],
                                    ALU.mult, ALU.add).then_inc(v_p.sem, 1)
                prepared(h, "f1")
                v.tensor_scalar(k2[:], tot[0][:], -1.0, 1.0, ALU.mult, ALU.add).then_inc(v_p.sem, 1)

            def prepare_queries(h):
                v.wait_ge(v_z.sem, v_z.after(h, "q1"))
                v.wait_ge(pe_r.sem, pe_r.after(h - 1, "o"))
                v.tensor_tensor(q2[:, 0, :], tot[0][:, 1, :], q_next[:], ALU.mult)
                v.tensor_tensor(q2[:, 1, :], tot[0][:, 0, :], q_next[:], ALU.mult).then_inc(v_p.sem, 1)

            def prepare_context(h):
                prepared(h, "keys")
                v.tensor_tensor(k_tok[:].rearrange("p c t -> p (c t)"), k2[:, 0, :], k2[:, 1, :], ALU.add).then_inc(v_p.sem, 1)
                for d in range(2):
                    v.tensor_scalar(f_next[:, d, T:TA], f_next[:, d, T:TA], olb[:, d, bass.ds(h, 1)], lb[:, d, bass.ds(h, 1)],
                                    ALU.mult, ALU.add).then_inc(v_p.sem, 1)
                prepared(h, "fc1")
                row = 2 * TA
                v.tensor_tensor_scan(bass.AP(reach, TC - 2, [[2 * TC, P], [-1, TC - 1]]),
                                     bass.AP(f_next, TA - 1, [[row, P], [-1, TC - 1]]), zeros[:, 0:TC - 1], 1.0, ALU.mult, ALU.add)
                v.tensor_tensor_scan(reach[:, 1, 1:TC], f_next[:, 1, T:TA - 1], zeros[:, 0:TC - 1], 1.0, ALU.mult, ALU.add).then_inc(v_p.sem, 1)
                prepared(h, "reach")
                v.tensor_scalar(f_next[:, :, T:TA], f_next[:, :, T:TA], -1.0, 1.0, ALU.mult, ALU.add).then_inc(v_p.sem, 1)
                prepared(h, "kc")
                v.tensor_tensor(f_next[:, :, T:TA], f_next[:, :, T:TA], reach[:], ALU.mult).then_inc(v_p.sem, 1)

            def level(h, l):
                v.wait_ge(pe_r.sem, pe_r.after(h, f"level{l}"))
                if l:
                    done(h, f"t{l - 1}")
                src, width = tot[l % 2], T if l % 2 == 0 else T // 2
                n = T >> l
                v.tensor_tensor(pair_ap(k2, l, 0), pair_ap(k2, l, 0), total_ap(src, l, width, 0, 1, 0), ALU.mult).then_inc(v_r.sem, 1)
                v.tensor_tensor(pair_ap(q2, l, 0), pair_ap(q2, l, 0), total_ap(src, l, width, 1, 1, 0), ALU.mult).then_inc(v_r.sem, 1)
                dst, dwidth = tot[(l + 1) % 2], T if l % 2 else T // 2
                if l == 0:
                    v.wait_ge(act_r.sem, act_r.after(h, "diag"))
                else:
                    done(h, f"p{l - 1}")
                v.tensor_tensor(bass.AP(dst, 0, [[2 * dwidth, P], [n // 2, 2], [1, n // 2]]),
                                bass.AP(src, 0, [[2 * width, P], [n, 2], [2, n // 2]]),
                                bass.AP(src, 1, [[2 * width, P], [n, 2], [2, n // 2]]), ALU.mult).then_inc(v_r.sem, 1)
                for b in range(2):
                    last = v.copy_predicated(scores[:, 4 * b:4 * b + 4, :], masks[:, l:l + 1, :].broadcast_to([P, 4, P]), ps_x[:, 4 * b:4 * b + 4, :])
                last.then_inc(v_r.sem, 1)

            def head(h, g):
                def t(name, dst):
                    if g is not None:
                        silu(g, name, dst)

                level(h, 0)
                silu(h, "g1", og_gate)
                v.wait_ge(pe_r.sem, pe_r.after(h, "s0"))
                v.tensor_copy(state[:, 0, 0, :], ps_w[:, 4, :])
                v.tensor_copy(state[:, 1, NC - 1, :], ps_w[:, 5, :]).then_inc(v_r.sem, 1)
                for l in range(1, LEVELS):
                    level(h, l)
                    if l == 1:
                        t("q0", q_next)
                    if l == 2:
                        t("q1", q_next)
                last_tot, wide = tot[LEVELS % 2], T if LEVELS % 2 == 0 else T // 2
                done(h, f"t{LEVELS - 1}")
                v.wait_ge(pe_r.sem, pe_r.after(h, "uf"))
                for c in range(NC - 1):
                    done(h, f"sf{c - 1}" if c else "s0")
                    v.scalar_tensor_tensor(out=state[:, 0, c + 1, :], in0=state[:, 0, c, :],
                                           scalar=bass.AP(last_tot, c, [[2 * wide, P], [1, 1]]),
                                           in1=ps_x[:, c, :], op0=ALU.mult, op1=ALU.add).then_inc(v_r.sem, 1)
                v.wait_ge(pe_r.sem, pe_r.after(h, "ub"))
                for j in range(NC - 1):
                    c = NC - 1 - j
                    done(h, f"sb{j - 1}" if j else "s0")
                    v.scalar_tensor_tensor(out=state[:, 1, c - 1, :], in0=state[:, 1, c, :],
                                           scalar=bass.AP(last_tot, NC + c, [[2 * wide, P], [1, 1]]),
                                           in1=ps_x[:, c, :], op0=ALU.mult, op1=ALU.add).then_inc(v_r.sem, 1)
                if g is not None:
                    prepare_keys(g)
                    prepare_queries(g)
                v.wait_ge(act_r.sem, act_r.after(h, f"sq{NC - 1}"))
                v.tensor_scalar(meansq[:], sumsq[:], 1.0 / P, EPS, ALU.mult, ALU.add).then_inc(v_r.sem, 1)
                if g is not None:
                    prepare_context(g)
                v.wait_ge(pe_r.sem, pe_r.after(h, "ot"))
                v.wait_ge(s_out, 16 * (h + 1))
                for b in range(2):
                    last = v.scalar_tensor_tensor(out=out[:, b * N512:(b + 1) * N512], in0=ps_w[:, 4 * b:4 * b + 4, :].rearrange("p c t -> p (c t)"),
                                                  scalar=cols[:, R_HG:R_HG + 1], in1=og_gate[:, b * N512:(b + 1) * N512],
                                                  op0=ALU.mult, op1=ALU.mult)
                last.then_inc(v_r.sem, 1)
                done(h, "out")
                t("g0", og_gate)

            v.sem_inc(s_out, 16)
            silu(0, "q0", q_next)
            silu(0, "q1", q_next)
            prepare_keys(0)
            prepare_queries(0)
            prepare_context(0)
            silu(0, "g0", og_gate)
            with v.Fori(0, NH - 1) as h:
                head(h, h + 1)
            head(NH - 1, None)


def phase_merge(nc, dram, keep, y, weighed, spare):
    KB = len(WINDOWS)
    KA = KT + KB
    STAGES = 3
    MC = D // (KT // 2)
    with ExitStack() as ctx:
        def sb(name, shape, dt=F32):
            return ctx.enter_context(nc.sbuf_tensor("m_" + name, shape, dt))

        def psum(name, shape):
            return ctx.enter_context(nc.psum_tensor("m_ps_" + name, shape, F32))

        def sem(name):
            return ctx.enter_context(nc.semaphore("m_" + name))

        landing = [sb(f"landing{i}", [P, T]) for i in range(STAGES - 1)] + [spare]
        in_head = sb("in_head", [P, KA, T], F32R)
        in_tail = sb("in_tail", [P, KA, T], F32R)
        w_raw = sb("w_raw", [P, 2, KA, P])
        w_head = sb("w_head", [P, KA, P], F32R)
        w_tail = sb("w_tail", [P, KA, P], F32R)
        gate = sb("gate", [P, 2, T])
        zero = sb("zero", [P, 1])
        w_mod = sb("w_mod", [P, 2, KT, MC])
        ps_a = [psum(f"a{i}", [P, T]) for i in range(2)]
        ps_b = [psum(f"b{i}", [P, T]) for i in range(2)]

        s_in = [sem(f"in_landed{i}") for i in range(STAGES)]
        s_w = [sem(f"w_landed{i}") for i in range(2)]
        s_gate = [sem(f"gate_landed{i}") for i in range(2)]
        act_in = sem("act_in_head")
        v_in = sem("v_in_tail")
        pool_set = sem("pool_set")
        s_mod = [sem(f"mod_landed{i}") for i in range(2)]
        s_bias = sem("bias_landed")
        pool_w = Steps(ctx, nc, "m_pool_w", ["head_a", "tail_a", "head_b", "tail_b"])
        pe_m = Steps(ctx, nc, "m_pe", ["a", "b"])
        v_m = Steps(ctx, nc, "m_v", ["ga", "gb", "sum"], lead=2)
        v_mod = Steps(ctx, nc, "m_v_mod", [f"{part}{k}" for part in "cr" for k in range(KT)])

        w_a = dram["w_a"].rearrange("a (k p) n -> p (a k) n", p=P)
        w_b = dram["w_b"].rearrange("a (k p) n -> p (a k) n", p=P)

        mod_columns = dram["w_mod"].rearrange("a (p k) n -> (a p) k n", k=KT)
        gates, csil = keep["gates"], keep["csil"]

        block = ctx.enter_context(nc.Block())

        @block.sync
        def _(sp):
            def load_block(m, slot):
                at = m * P if isinstance(m, int) else sp.snap(m * P)
                if not (isinstance(m, int) and m < 2):
                    sp.wait_ge(pool_w.sem, pool_w.after(m - 2, "tail_b"))
                sp.dma_start(w_raw[:, slot, 0:KT, :], w_a[:, :, bass.ds(at, P)]).then_inc(s_w[slot], 16)
                sp.dma_start(w_raw[:, slot, KT:KA, :], w_b[:, :, bass.ds(at, P)]).then_inc(s_w[slot], 16)

            def load_gates(m):
                for g in range(2):
                    at = (g * D + m * P) * T if isinstance(m, int) else sp.snap((g * D + m * P) * T)
                    sp.wait_ge(v_m.sem, v_m.after(m - 1, "sum"))
                    src = dram["gates"].rearrange("g d t -> (g d t)")[bass.ds(at, P * T)].rearrange("(p t) -> p t", t=T)
                    sp.dma_start(gate[:, g, :], src).then_inc(s_gate[g], 16)

            def load_modulation(j, i):
                for slot, group, part in ((0, 3 + i, "c"), (1, 2 + 3 * i, "r")):
                    at = group * D + j * MC if isinstance(j, int) else sp.snap(group * D + j * MC)
                    sp.wait_ge(v_mod.sem, v_mod.after(2 * j + i - 1, f"{part}{KT - 1}"))
                    sp.dma_start(w_mod[:, slot], mod_columns[:, :, bass.ds(at, MC)]).then_inc(s_mod[slot], 16)

            def load_input(k):
                if k >= STAGES:
                    sp.wait_ge(v_in, k - STAGES + 1)
                src = dram["og"][k * P:(k + 1) * P, :] if k < KT else dram["yb"][(k - KT) * P:(k - KT + 1) * P, :]
                sp.dma_start(landing[k % STAGES][:], src).then_inc(s_in[k % STAGES], 16)

            load_block(0, 0)
            for k in range(KA):
                load_input(k)
                if k == STAGES:
                    load_block(1, 1)
            sp.wait_ge(pool_set, 2)
            sp.dma_start(gates[0:1, 0, :], dram["b_mod"][0:1, 2 * D:3 * D]).then_inc(s_bias, 16)
            sp.dma_start(gates[0:1, 1, :], dram["b_mod"][0:1, 5 * D:6 * D]).then_inc(s_bias, 16)
            load_gates(0)
            load_modulation(0, 0)

            def ahead(j, i, last=False):
                if not last:
                    load_block(2 * j + i + 1, 1 - i)
                load_gates(2 * j + i)
                load_modulation(j, i)

            ahead(0, 1)
            with sp.Fori(1, KT // 2 - 1) as j:
                ahead(j, 0)
                ahead(j, 1)
            ahead(KT // 2 - 1, 0)
            ahead(KT // 2 - 1, 1, last=True)

        @block.gpsimd
        def _(pool):
            pool.sem_inc(pool_w.sem, pool_w.credit)
            pool.memset(zero[:], 0.0).then_inc(pool_set, 1)
            pool.memset(gates[:], 0.0).then_inc(pool_set, 1)
            pool.wait_ge(pool_set, 1)
            with pool.Fori(0, KT // 2) as j:
                for i in range(2):
                    m = 2 * j + i
                    pool.wait_ge(s_w[i], 32 * (j + 1))
                    for part, lo, hi in (("a", 0, KT), ("b", KT, KA)):
                        pool.wait_ge(pe_m.sem, pe_m.after(m - 1, part))
                        pool.tensor_tensor(w_head[:, lo:hi], w_raw[:, i, lo:hi], zero[:].unsqueeze(2).broadcast_to([P, hi - lo, P]),
                                           ALU.add).then_inc(pool_w.sem, 1)
                        pool.wait_ge(pool_w.sem, pool_w.after(m, "head_" + part))
                        pool.tensor_tensor(w_tail[:, lo:hi], w_raw[:, i, lo:hi], w_head[:, lo:hi].bitcast(F32),
                                           ALU.subtract).then_inc(pool_w.sem, 1)

        @block.tensor
        def _(pe):
            pe.sem_inc(pe_m.sem, pe_m.credit)

            def branch(m, slot, part, first):
                lo, hi, ps = (0, KT, ps_a) if part == "a" else (KT, KA, ps_b)
                pe.wait_ge(pool_w.sem, pool_w.after(m, "tail_" + part))
                if not first:
                    pe.wait_ge(v_m.sem, v_m.after(m - 2, "sum"))
                for k in range(lo, hi):
                    if first:
                        pe.wait_ge(v_in, k + 1)
                    for half in range(2):
                        cols = slice(half * N512, (half + 1) * N512)
                        last = matmul3(pe, ps[slot][:, cols], (w_head[:, k, :], w_tail[:, k, :]),
                                       (in_head[:, k, cols], in_tail[:, k, cols]), k == lo, k == hi - 1)
                last.then_inc(pe_m.sem, 1)

            for part in "ab":
                branch(0, 0, part, True)
            for part in "ab":
                branch(1, 1, part, False)
            with pe.Fori(1, KT // 2) as j:
                for i in range(2):
                    for part in "ab":
                        branch(2 * j + i, i, part, False)

        @block.scalar
        def _(act):
            for k in range(KA):
                act.wait_ge(s_in[k % STAGES], 16 * (k // STAGES + 1))
                act.activation(in_head[:, k, :], landing[k % STAGES][:], ACT.Copy).then_inc(act_in, 1)

        @block.vector
        def _(v):
            v.sem_inc(v_m.sem, v_m.credit)
            v.sem_inc(v_mod.sem, v_mod.credit)

            def weigh(j, i):
                m = 2 * j + i
                for slot, part, dst in ((0, "c", weighed), (1, "r", gates)):
                    v.wait_ge(s_mod[slot], 16 * (m + 1))
                    out = dst[:, i, bass.ds(j * MC, MC)]
                    for k in range(KT):
                        src, c = w_mod[:, slot, k, :], csil[:, k, 0:1]
                        if k:
                            v.wait_ge(v_mod.sem, v_mod.after(m, f"{part}{k - 1}"))
                        if k == 0 and part == "c":
                            last = v.tensor_scalar(out, src, c, None, ALU.mult)
                        else:
                            last = v.scalar_tensor_tensor(out=out, in0=src, scalar=c, in1=out, op0=ALU.mult, op1=ALU.add)
                        last.then_inc(v_mod.sem, 1)

            for k in range(KA):
                v.wait_ge(act_in, k + 1)
                v.tensor_tensor(in_tail[:, k, :], landing[k % STAGES][:], in_head[:, k, :].bitcast(F32), ALU.subtract).then_inc(v_in, 1)
            v.wait_ge(s_bias, 32)
            with v.Fori(0, KT // 2) as j:
                for i in range(2):
                    m = 2 * j + i
                    v.wait_ge(pe_m.sem, pe_m.after(m, "a"))
                    v.wait_ge(s_gate[0], 16 * (m + 1))
                    v.tensor_tensor(gate[:, 0, :], ps_a[i][:], gate[:, 0, :], ALU.mult).then_inc(v_m.sem, 1)
                    v.wait_ge(pe_m.sem, pe_m.after(m, "b"))
                    v.wait_ge(s_gate[1], 16 * (m + 1))
                    v.tensor_tensor(gate[:, 1, :], ps_b[i][:], gate[:, 1, :], ALU.mult).then_inc(v_m.sem, 1)
                    v.wait_ge(v_m.sem, v_m.after(m, "gb"))
                    v.tensor_tensor(y[:, bass.ds(m, 1), :].rearrange("p a t -> p (a t)"), gate[:, 0, :], gate[:, 1, :], ALU.add).then_inc(v_m.sem, 1)
                    weigh(j, i)


def choose(v, sem, probs, left, best, where, lo, hi):
    for r in range(lo, hi):
        src = left[(r - 1) % 2][:] if r else probs
        eight = slice(8 * r, 8 * r + 8)
        if r:
            v.wait_ge(sem, 3 * r)
        v.max(best[:, eight], src).then_inc(sem, 1)
        v.wait_ge(sem, 3 * r + 1)
        v.max_index(where[:, eight], best[:, eight], src).then_inc(sem, 1)
        if r < ROUNDS - 1:
            v.match_replace(left[r % 2][:], best[:, eight], src, -1.0).then_inc(sem, 1)


def phase_project(nc, dram, keep, y, weighed, probs_t, early):
    STAGES = 4
    EARLY_ROUNDS = {6: (0, 5), 7: (5, 9), 8: (9, 12), 9: (12, 14), 10: (14, ROUNDS)}
    with ExitStack() as ctx:
        def sb(name, shape, dt=F32):
            return ctx.enter_context(nc.sbuf_tensor("o_" + name, shape, dt))

        def psum(name, shape):
            return ctx.enter_context(nc.psum_tensor("o_ps_" + name, shape, F32))

        def sem(name):
            return ctx.enter_context(nc.semaphore("o_" + name))

        w_raw = sb("w_raw", [P, STAGES, D])
        w_head = sb("w_head", [P, KT, D], F32R)
        w_tail = sb("w_tail", [P, KT, D], F32R)
        w_router = sb("w_router", [P, KT, NE])
        y_head = [sb(f"y_head{i}", [P, KT, P], F32R) for i in range(2)]
        y_tail = [sb(f"y_tail{i}", [P, KT, P], F32R) for i in range(2)]
        x_tile = [sb(f"x_tile{i}", [P, D]) for i in range(2)]
        hx = [sb(f"hx{i}", [P, D]) for i in range(2)]
        vn = [sb(f"vn{i}", [P, D]) for i in range(2)]
        v_feat = sb("v_feat", [P, KT, P])
        junk = sb("junk", [P, D])
        sumsq = sb("sumsq", [P, 1])
        meansq = sb("meansq", [P, 1])
        neghalf = sb("neghalf", [P, 1])
        rstd = sb("rstd", [P, 1])
        negmax = sb("negmax", [P, 1])
        expsum = sb("expsum", [P, 1])
        inverse = sb("inverse", [P, 1])
        expd = sb("expd", [P, NE])
        probs = sb("probs", [P, NE])
        left = [sb(f"left{i}", [NE, EARLY]) for i in range(2)]
        ones = sb("ones", [P, P])
        shifted = sb("shift_scale", [P, 2, KT])
        ps_o = [psum(f"out{i}", [P, D]) for i in range(2)]
        ps_v = psum("v", [P, KT, P])
        ps_l = psum("logits", [P, N512])
        ps_p = psum("probs", [P, N512])

        s_w = [sem(f"w_landed{i}") for i in range(STAGES)]
        s_router = sem("router_landed")
        s_x = [sem(f"x_landed{i}") for i in range(2)]
        s_hx = [sem(f"hx_stored{i}") for i in range(2)]
        s_vn = [sem(f"vn_stored{i}") for i in range(2)]
        v_early = sem("v_early")
        pe_mod = sem("pe_modulation_summed")
        v_mod = sem("v_modulation")
        act_w = sem("act_w_head")
        v_w = sem("v_w_tail")
        pool_set = sem("pool_set")
        pe_main = Steps(ctx, nc, "o_pe_main", ["half0", "half1"], lead=2)
        pe_turn = Steps(ctx, nc, "o_pe_turn", ["turn"], lead=2)
        pe_route = Steps(ctx, nc, "o_pe_route", ["logits", "probs"])
        act_split = Steps(ctx, nc, "o_act_split", ["head"])
        act_main = Steps(ctx, nc, "o_act_main", ["square", "vn"])
        act_route = Steps(ctx, nc, "o_act_route", ["feat", "exp"])
        v_split = Steps(ctx, nc, "o_v_split", ["tail"])
        v_main = Steps(ctx, nc, "o_v_main", ["gated", "hx", "mean"], lead=2)
        v_route = Steps(ctx, nc, "o_v_route", ["max", "inverse", "probs", "probs_t"])
        pool_main = Steps(ctx, nc, "o_pool_main", ["rstd"])

        ident, gates = keep["ident"], keep["gates"]
        w_out = dram["w_out"].rearrange("a (k p) n -> p (a k) n", p=P)
        x_flat = dram["x"].rearrange("a t d -> (a t) d")

        block = ctx.enter_context(nc.Block())

        def known(i, lo=0, hi=NT):
            return not isinstance(i, int) or lo <= i < hi

        def iterations(eng, body):
            for i in range(4):
                body(i, i % 2)
            with eng.Fori(2, NT // 2 - 1) as j:
                for slot in range(2):
                    body(2 * j + slot, slot)
            for i in range(NT - 2, NT + 3):
                body(i, i % 2)

        @block.sync
        def _(sp):
            sp.dma_start(w_router[:], dram["w_router"].rearrange("a (k p) e -> p (a k) e", p=P)).then_inc(s_router, 16)
            for k in range(KT):
                if k >= STAGES:
                    sp.wait_ge(v_w, k - STAGES + 1)
                sp.dma_start(w_raw[:, k % STAGES, :], w_out[:, k, :]).then_inc(s_w[k % STAGES], 16)
                if k < 2:
                    sp.dma_start(x_tile[k][:], x_flat[k * P:(k + 1) * P, :]).then_inc(s_x[k], 16)
            with sp.Fori(1, NT // 2) as j:
                for i in range(2):
                    at = sp.snap((2 * j + i) * P * D)
                    sp.wait_ge(v_main.sem, v_main.after(2 * j + i - 2, "hx"))
                    src = x_flat.rearrange("t d -> (t d)")[bass.ds(at, P * D)].rearrange("(p d) -> p d", d=D)
                    sp.dma_start(x_tile[i][:], src).then_inc(s_x[i], 16)

        @block.gpsimd
        def _(pool):
            pool.sem_inc(pool_main.sem, pool_main.credit)
            pool.memset(neghalf[:], -0.5).then_inc(pool_set, 1)
            pool.wait_ge(pool_set, 1)
            with pool.Fori(0, NT) as i:
                pool.wait_ge(v_main.sem, v_main.after(i, "mean"))
                pool.tensor_tensor(rstd[:], meansq[:], neghalf[:], ALU.pow).then_inc(pool_main.sem, 1)

        @block.tensor
        def _(pe):
            pe.sem_inc(pe_main.sem, pe_main.credit)
            pe.sem_inc(pe_route.sem, pe_route.credit)
            pe.wait_ge(s_router, 16)

            pe.wait_ge(v_mod, 1)
            for g in range(2):
                for half in range(2):
                    cols = slice(half * N512, (half + 1) * N512)
                    dst = ps_o[1][:, cols] if g == 0 else ps_v[:, half * KT // 2:(half + 1) * KT // 2, :]
                    pe.matmul(dst, ones[:], gates[:, g, cols], start=True, stop=True)
            for m in range(2 * KT):
                last = pe.matmul(ps_l[:, m:m + 1], weighed[:, m // KT, m % KT * P:(m % KT + 1) * P], ones[:, 0:1], start=True, stop=True)
            last.then_inc(pe_mod, 1)

            pe.sem_inc(pe_turn.sem, pe_turn.credit)

            def half(i, slot, h):
                if h == 0:
                    pe.wait_ge(v_split.sem, v_split.after(i, "tail"))
                    pe.wait_ge(v_main.sem, v_main.after(i - 2, "gated"))
                    if isinstance(i, int) and i == 1:
                        pe.wait_ge(v_mod, 2)
                cols = slice(h * N512, (h + 1) * N512)
                for k in range(KT):
                    if isinstance(i, int) and i == 0:
                        pe.wait_ge(v_w, k + 1)
                    last = matmul3(pe, ps_o[slot][:, cols], (y_head[slot][:, k, :], y_tail[slot][:, k, :]),
                                   (w_head[:, k, cols], w_tail[:, k, cols]), k == 0, k == KT - 1)
                last.then_inc(pe_main.sem, 1)

            def turn(i, slot):
                if isinstance(i, int) and i == 0:
                    pe.wait_ge(v_mod, 3)
                pe.wait_ge(act_main.sem, act_main.after(i, "vn"))
                pe.wait_ge(act_route.sem, act_route.after(i - 1, "feat"))
                for k in range(KT):
                    last = pe.transpose(ps_v[:, k, :], vn[slot][:, k * P:(k + 1) * P], ident[:])
                last.then_inc(pe_turn.sem, 1)

            def logits(i):
                pe.wait_ge(act_route.sem, act_route.after(i, "feat"))
                for k in range(KT):
                    last = pe.matmul(ps_l[:, 0:NE], v_feat[:, k, :], w_router[:, k, :], start=(k == 0), stop=(k == KT - 1))
                last.then_inc(pe_route.sem, 1)

            def turn_probs(i):
                pe.wait_ge(v_route.sem, v_route.after(i, "probs"))
                pe.transpose(ps_p[0:NE, 0:P], probs[:], ident[:]).then_inc(pe_route.sem, 1)

            def body(i, slot):
                if known(i):
                    half(i, slot, 0)
                if known(i - 3):
                    turn_probs(i - 3)
                if known(i):
                    half(i, slot, 1)
                if known(i - 2):
                    logits(i - 2)
                if known(i - 1):
                    turn(i - 1, 1 - slot)

            iterations(pe, body)

        @block.scalar
        def _(act):
            act.sem_inc(act_main.sem, act_main.credit)
            act.sem_inc(act_route.sem, act_route.credit)
            act.sem_inc(act_split.sem, act_split.credit)


            def split(i, slot):
                act.wait_ge(pe_main.sem, pe_main.after(i - 2, "half1"))
                act.activation(y_head[slot][:], y[:, :, bass.ds(i * P, P)], ACT.Copy).then_inc(act_split.sem, 1)

            def main(i, slot):
                act.wait_ge(v_main.sem, v_main.after(i, "hx"))
                act.wait_ge(act_main.sem, act_main.after(i - 1, "vn"))
                act.activation(junk[:], hx[slot][:], ACT.Square, accum_out=sumsq[:]).then_inc(act_main.sem, 1)
                act.dma_start(dram["acc"][bass.ds(i * P, P), :], hx[slot][:]).then_inc(s_hx[slot], 16)
                act.wait_ge(s_vn[slot], 8 * (i - slot) + 16)
                act.wait_ge(pe_turn.sem, pe_turn.after(i - 2, "turn"))
                act.wait_ge(pool_main.sem, pool_main.after(i, "rstd"))
                act.activation(vn[slot][:], hx[slot][:], ACT.Copy, scale=rstd[:]).then_inc(act_main.sem, 1)
                act.wait_ge(act_main.sem, act_main.after(i, "vn"))
                act.dma_start(dram["vn"][bass.ds(i * P, P), :], vn[slot][:]).then_inc(s_vn[slot], 16)

            def features(i):
                if isinstance(i, int) and i == 0:
                    act.wait_ge(v_mod, 5)
                act.wait_ge(pe_turn.sem, pe_turn.after(i, "turn"))
                act.wait_ge(pe_route.sem, pe_route.after(i - 1, "logits"))
                for k in range(KT):
                    last = act.activation(v_feat[:, k, :], ps_v[:, k, :], ACT.Identity, scale=keep["scale2"][:, k:k + 1],
                                          bias=keep["shift2"][:, k:k + 1])
                last.then_inc(act_route.sem, 1)

            def exponentials(i):
                act.wait_ge(v_route.sem, v_route.after(i, "max"))
                act.activation(expd[:], ps_l[:, 0:NE], ACT.Exp, bias=negmax[:], accum_out=expsum[:]).then_inc(act_route.sem, 1)

            def body(i, slot):
                if known(i - 2):
                    features(i - 2)
                if known(i + 1):
                    split(i + 1, 1 - slot)
                if known(i):
                    main(i, slot)
                if known(i - 2):
                    exponentials(i - 2)

            split(0, 0)
            for k in range(KT):
                act.wait_ge(s_w[k % STAGES], 16 * (k // STAGES + 1))
                act.activation(w_head[:, k, :], w_raw[:, k % STAGES, :], ACT.Copy).then_inc(act_w, 1)
            iterations(act, body)
            for i in range(2):
                act.wait_ge(s_hx[i], 16 * (NT // 2 + 1))
                act.wait_ge(s_vn[i], 16 * (NT // 2 + 1))

        @block.vector
        def _(v):
            v.sem_inc(v_main.sem, v_main.credit)
            v.sem_inc(v_route.sem, v_route.credit)
            v.sem_inc(v_split.sem, v_split.credit)
            for i in range(2):
                v.sem_inc(s_hx[i], 16)
                v.sem_inc(s_vn[i], 16)

            def split(i, slot):
                v.wait_ge(act_split.sem, act_split.after(i, "head"))
                v.tensor_tensor(y_tail[slot][:], y[:, :, bass.ds(i * P, P)], y_head[slot][:].bitcast(F32), ALU.subtract).then_inc(v_split.sem, 1)

            def main(i, slot):
                v.wait_ge(pe_main.sem, pe_main.after(i, "half1"))
                v.wait_ge(s_hx[slot], 8 * (i - slot) + 16)
                v.wait_ge(act_main.sem, act_main.after(i - 1, "vn"))
                v.tensor_tensor(hx[slot][:], ps_o[slot][:], gates[:, 0, :], ALU.mult).then_inc(v_main.sem, 1)
                v.wait_ge(s_x[slot], 8 * (i - slot) + 16)
                v.wait_ge(v_main.sem, v_main.after(i, "gated"))
                v.tensor_tensor(hx[slot][:], hx[slot][:], x_tile[slot][:], ALU.add).then_inc(v_main.sem, 1)
                v.wait_ge(act_main.sem, act_main.after(i, "square"))
                v.wait_ge(pool_main.sem, pool_main.after(i - 1, "rstd"))
                v.tensor_scalar(meansq[:], sumsq[:], 1.0 / D, EPS, ALU.mult, ALU.add).then_inc(v_main.sem, 1)

            def route(i):
                v.wait_ge(pe_route.sem, pe_route.after(i, "logits"))
                v.tensor_reduce(negmax[:], ps_l[:, 0:NE], AX.X, ALU.max, negate=True).then_inc(v_route.sem, 1)
                v.wait_ge(act_route.sem, act_route.after(i, "exp"))
                v.reciprocal(inverse[:], expsum[:]).then_inc(v_route.sem, 1)
                v.wait_ge(v_route.sem, v_route.after(i, "inverse"))
                v.tensor_scalar(probs[:], expd[:], inverse[:], None, ALU.mult).then_inc(v_route.sem, 1)

            def keep_probs(i):
                v.wait_ge(pe_route.sem, pe_route.after(i, "probs"))
                v.tensor_copy(probs_t[0:NE, bass.ds(i * P, P)], ps_p[0:NE, 0:P]).then_inc(v_route.sem, 1)

            def body(i, slot):
                if known(i + 1):
                    split(i + 1, 1 - slot)
                if known(i - 3):
                    keep_probs(i - 3)
                if known(i):
                    main(i, slot)
                if known(i - 2):
                    route(i - 2)
                if isinstance(i, int) and i in EARLY_ROUNDS:
                    v.wait_ge(v_route.sem, v_route.after(EARLY // P - 1, "probs_t"))
                    choose(v, v_early, probs_t[0:NE, 0:EARLY], left, early["best"], early["where"], *EARLY_ROUNDS[i])

            v.memset(ones[:], 1.0).then_inc(v_mod, 1)
            split(0, 0)
            for k in range(KT):
                v.wait_ge(act_w, k + 1)
                v.tensor_tensor(w_tail[:, k, :], w_raw[:, k % STAGES, :], w_head[:, k, :].bitcast(F32), ALU.subtract).then_inc(v_w, 1)
            v.wait_ge(pe_mod, 1)
            v.tensor_copy(gates[:, 0, :], ps_o[1][:]).then_inc(v_mod, 1)
            v.tensor_copy(gates[:, 1, :], ps_v[:].rearrange("p k t -> p (k t)")).then_inc(v_mod, 1)
            bias = keep["cols"][:, 3 * KT:5 * KT].rearrange("p (g k) -> p g k", k=KT)
            v.tensor_tensor(shifted[:], ps_l[:, 0:2 * KT].rearrange("p (g k) -> p g k", k=KT), bias, ALU.add).then_inc(v_mod, 1)
            v.wait_ge(v_mod, 4)
            v.tensor_copy(keep["shift2"][:], shifted[:, 0, :])
            v.scalar_tensor_tensor(out=keep["scale2"][:], in0=shifted[:, 1, :], scalar=1.0, in1=keep["cols"][:, R_N2:R_N2 + KT],
                                   op0=ALU.add, op1=ALU.mult).then_inc(v_mod, 1)
            iterations(v, body)


def phase_experts(nc, dram, keep, probs_t, early):
    CK = 2
    NCH = KT // CK
    RAW, SPLIT = 6, 6
    GU = [f"g{c}" for c in range(NCH)] + [f"u{c}" for c in range(NCH)]
    DN = [f"d{c}" for c in range(NCH)]
    TOP_STEPS = 3 * ROUNDS - 1 + 8
    with ExitStack() as ctx:
        def sb(name, shape, dt=F32):
            return ctx.enter_context(nc.sbuf_tensor("e_" + name, shape, dt))

        def psum(name, shape):
            return ctx.enter_context(nc.psum_tensor("e_ps_" + name, shape, F32))

        def sem(name):
            return ctx.enter_context(nc.semaphore("e_" + name))

        w_raw = sb("w_raw", [P, RAW, CK, FF])
        w_head = sb("w_head", [P, SPLIT, CK, FF], F32R)
        w_tail = sb("w_tail", [P, SPLIT, CK, FF], F32R)
        left = [sb(f"left{i}", [NE, T - EARLY]) for i in range(2)]
        late_best = sb("late_best", [NE, CAP])
        late_where = sb("late_where", [NE, CAP], U32)
        place = [sb(f"place{i}", [NE, CAP]) for i in range(2)]
        is_early = sb("is_early", [NE, CAP])
        best = sb("best", [NE, CAP])
        where_f = sb("where_f", [NE, CAP])
        token = sb("token", [P, NE], U32)
        weight = sb("weight", [P, NE])
        token_in = sb("token_in", [P, 1], U32)
        token_out = sb("token_out", [P, 1], U32)
        zero_u = sb("zero_u", [P, 1], U32)
        settled = sb("settled", [P, 2], U32)
        xg = sb("xg", [P, D])
        xm = sb("xm", [P, KT, P])
        x_head = sb("x_head", [P, KT, P], F32R)
        x_tail = sb("x_tail", [P, KT, P], F32R)
        sig = sb("sig", [P, FF])
        hid = sb("hid", [P, FF])
        h_head = sb("h_head", [P, KT, P], F32R)
        h_tail = sb("h_tail", [P, KT, P], F32R)
        rows = sb("rows", [P, D])
        ps_g = psum("gate", [P, FF])
        ps_u = psum("up", [P, FF])
        ps_y = psum("down", [P, D])
        ps_t = psum("turn", [P, KT, P])

        s_gu = [sem(f"w_landed_{n}") for n in GU]
        s_d = [sem(f"w_landed_{n}") for n in DN]
        s_xg = sem("tokens_gathered")
        s_add = sem("rows_added")
        v_top = sem("v_top")
        pool_set = sem("pool_set")
        pe_top = sem("pe_top")
        pool_in = sem("pool_token_in")
        pool_out = sem("pool_token_out")
        pe_gu = Steps(ctx, nc, "e_pe_gu", GU)
        pe_d = Steps(ctx, nc, "e_pe_d", DN)
        pe_xt = Steps(ctx, nc, "e_pe_xt", ["xt"])
        pe_ht = Steps(ctx, nc, "e_pe_ht", ["ht"])
        act_gu = Steps(ctx, nc, "e_act_gu", GU)
        act_d = Steps(ctx, nc, "e_act_d", DN)
        act_sig = Steps(ctx, nc, "e_act_sig", ["sig"])
        act_x = Steps(ctx, nc, "e_act_x", ["mod", "head"])
        act_h = Steps(ctx, nc, "e_act_h", ["head"])
        v_gu = Steps(ctx, nc, "e_v_gu", GU)
        v_d = Steps(ctx, nc, "e_v_d", DN)
        v_hid = Steps(ctx, nc, "e_v_hid", ["silu", "hid"])
        v_x = Steps(ctx, nc, "e_v_x", ["mod", "tail"])
        v_h = Steps(ctx, nc, "e_v_h", ["tail"])
        v_y = Steps(ctx, nc, "e_v_y", ["rows"])

        ident, gates, scale2, shift2 = keep["ident"], keep["gates"], keep["scale2"], keep["shift2"]

        block = ctx.enter_context(nc.Block())

        def known(e, lo, hi):
            return not isinstance(e, int) or lo <= e < hi

        def wait(eng, steps, it, step):
            if known(it, 0, NE):
                eng.wait_ge(steps.sem, steps.after(it, step))

        def iterations(eng, body):
            body(0)
            body(1)
            with eng.Fori(2, NE - 1) as e:
                body(e)
            for e in range(NE - 1, NE + 2):
                body(e)

        def position(name):
            return (GU + DN).index(name)

        def wait_slot(eng, gu_steps, d_steps, it, pos, ring):
            while True:
                pos -= ring
                if pos < 0:
                    pos, it = pos + 3 * NCH, it - 1
                if isinstance(it, int) and it < 0:
                    return
                if not isinstance(it, int) or (it < NE if pos < 2 * NCH else it >= 1):
                    break
            if pos < 2 * NCH:
                eng.wait_ge(gu_steps.sem, gu_steps.after(it, GU[pos]))
            else:
                eng.wait_ge(d_steps.sem, d_steps.after(it - 1, DN[pos - 2 * NCH]))

        @block.sync
        def _(sp):
            stack = {"g": dram["w_e_gate"], "u": dram["w_e_up"], "d": dram["w_e_down"]}
            flat = {k: a.rearrange("a e f n -> (a e f n)") for k, a in stack.items()}

            def load(expert, name, landed):
                pos = position(name)
                size = CK * P * FF
                at = expert * (FF * D) + int(name[1]) * size
                at = at if isinstance(expert, int) else sp.snap(at)
                it = expert + 1 if name[0] == "d" else expert
                wait_slot(sp, v_gu, v_d, it, pos, RAW)
                src = flat[name[0]][bass.ds(at, size)].rearrange("(k p n) -> p k n", p=P, n=FF)
                sp.dma_start(w_raw[:, pos % RAW], src).then_inc(landed, 16)

            def body(e):
                if known(e, 0, NE):
                    for n, name in enumerate(GU):
                        load(e, name, s_gu[n])
                if known(e, 1, NE + 1):
                    for n, name in enumerate(DN):
                        load(e - 1, name, s_d[n])

            iterations(sp, body)

        @block.gpsimd
        def _(pool):
            pool.memset(zero_u[:], 0).then_inc(pool_set, 1)
            pool.wait_ge(pool_set, 1)
            for n, name in enumerate(GU[:SPLIT]):
                pool.wait_ge(act_gu.sem, act_gu.after(0, name))
                pool.tensor_tensor(w_tail[:, n % SPLIT], w_raw[:, n % RAW], w_head[:, n % SPLIT].bitcast(F32), ALU.subtract).then_inc(v_gu.sem, 1)
            pool.wait_ge(v_top, TOP_STEPS + 2)


            def gather(x):
                wait(pool, pe_xt, x - 1, "xt")
                pool.tensor_tensor(token_in[:], token[:, bass.ds(x, 1)], zero_u[:], ALU.add).then_inc(pool_in, 1)
                pool.wait_ge(pool_in, 2 * x + 1)
                pool.tensor_tensor(settled[:, 0:1], zero_u[:], zero_u[:], ALU.add).then_inc(pool_in, 1)
                pool.indirect_dma_start(xg[:], None, dram["vn"], bass.IndirectOffsetOnAxis(ap=token_in[:], axis=0)).then_inc(s_xg, 16)

            def scatter(x):
                if known(x, 1, NE):
                    pool.wait_ge(s_add, 16 * x)
                pool.tensor_tensor(token_out[:], token[:, bass.ds(x, 1)], zero_u[:], ALU.add).then_inc(pool_out, 1)
                wait(pool, v_y, x, "rows")
                pool.wait_ge(pool_out, 2 * x + 1)
                pool.tensor_tensor(settled[:, 1:2], zero_u[:], zero_u[:], ALU.add).then_inc(pool_out, 1)
                pool.indirect_dma_start(dram["acc"], bass.IndirectOffsetOnAxis(ap=token_out[:], axis=0), rows[:], None,
                                        compute_op=ALU.add).then_inc(s_add, 16)

            def body(e):
                if known(e + 1, 1, NE):
                    gather(e + 1)
                if known(e - 2, 0, NE):
                    scatter(e - 2)

            gather(0)
            iterations(pool, body)
            pool.wait_ge(s_add, 16 * NE)

        @block.tensor
        def _(pe):
            for s in (pe_gu, pe_d, pe_xt, pe_ht):
                pe.sem_inc(s.sem, s.credit)

            def product(ps, lhs, slot, c):
                for k in range(CK):
                    kk = CK * c + k
                    for half in range(2):
                        cols = slice(half * N512, (half + 1) * N512)
                        last = matmul3(pe, ps[:, cols], (lhs[0][:, kk, :], lhs[1][:, kk, :]),
                                       (w_head[:, slot, k, cols], w_tail[:, slot, k, cols]), kk == 0, kk == KT - 1)
                return last

            def turn(ps, src):
                for k in range(KT):
                    last = pe.transpose(ps[:, k, :], src[:, k * P:(k + 1) * P], ident[:])
                return last

            def gate_up(e):
                wait(pe, v_x, e, "tail")
                for n, name in enumerate(GU):
                    if name == "g0":
                        wait(pe, v_hid, e - 1, "silu")
                    if name == "u0":
                        wait(pe, v_hid, e - 1, "hid")
                    wait(pe, v_gu, e, name)
                    product(ps_g if name[0] == "g" else ps_u, (x_head, x_tail), n % SPLIT, n % NCH).then_inc(pe_gu.sem, 1)

            def turn_tokens(x):
                pe.wait_ge(s_xg, 16 * (x + 1))
                wait(pe, v_h, x - 2, "tail")
                turn(ps_t, xg).then_inc(pe_xt.sem, 1)

            def down(x):
                wait(pe, v_h, x, "tail")
                wait(pe, v_y, x - 1, "rows")
                for c, name in enumerate(DN):
                    wait(pe, v_d, x, name)
                    product(ps_y, (h_head, h_tail), (2 * NCH + c) % SPLIT, c).then_inc(pe_d.sem, 1)

            def turn_hidden(x):
                wait(pe, v_hid, x, "hid")
                if known(x + 1, 1, NE):
                    wait(pe, act_x, x + 1, "mod")
                    wait(pe, v_x, x + 1, "mod")
                turn(ps_t, hid).then_inc(pe_ht.sem, 1)

            pe.wait_ge(v_top, TOP_STEPS)
            pe.transpose(ps_g[:, 0:NE], where_f[:], ident[0:NE, 0:NE])
            pe.transpose(ps_g[:, NE:2 * NE], best[:], ident[0:NE, 0:NE]).then_inc(pe_top, 1)
            pe.wait_ge(v_top, TOP_STEPS + 2)
            turn_tokens(0)

            def body(e):
                if known(e, 0, NE):
                    gate_up(e)
                if known(e + 1, 1, NE):
                    turn_tokens(e + 1)
                if known(e - 1, 0, NE):
                    down(e - 1)
                if known(e, 0, NE):
                    turn_hidden(e)

            iterations(pe, body)

        @block.scalar
        def _(act):
            for s in (act_gu, act_d, act_sig, act_x, act_h):
                act.sem_inc(s.sem, s.credit)

            def split_gu(e, name):
                n = GU.index(name)
                act.wait_ge(s_gu[n], 16 * (e + 1))
                wait_slot(act, pe_gu, pe_d, e, position(name), SPLIT)
                act.activation(w_head[:, n % SPLIT], w_raw[:, n % RAW], ACT.Copy).then_inc(act_gu.sem, 1)

            def split_d(x, name):
                c = DN.index(name)
                act.wait_ge(s_d[c], 16 * (x + 1))
                wait_slot(act, pe_gu, pe_d, x + 1, position(name), SPLIT)
                act.activation(w_head[:, (2 * NCH + c) % SPLIT], w_raw[:, (2 * NCH + c) % RAW], ACT.Copy).then_inc(act_d.sem, 1)

            def sigmoid(e):
                act.wait_ge(pe_gu.sem, pe_gu.after(e, GU[NCH - 1]))
                wait(act, v_hid, e - 1, "silu")
                act.activation(sig[:], ps_g[:], ACT.Sigmoid).then_inc(act_sig.sem, 1)

            def tokens(x):
                act.wait_ge(pe_xt.sem, pe_xt.after(x, "xt"))
                wait(act, v_x, x - 1, "tail")
                for k in range(KT // 2):
                    last = act.activation(xm[:, k, :], ps_t[:, k, :], ACT.Identity, scale=scale2[:, k:k + 1], bias=shift2[:, k:k + 1])
                last.then_inc(act_x.sem, 1)
                act.wait_ge(act_x.sem, act_x.after(x, "mod"))
                act.wait_ge(v_x.sem, v_x.after(x, "mod"))
                act.activation(x_head[:], xm[:], ACT.Copy).then_inc(act_x.sem, 1)

            def hidden(x):
                act.wait_ge(pe_ht.sem, pe_ht.after(x, "ht"))
                act.activation(h_head[:], ps_t[:], ACT.Copy).then_inc(act_h.sem, 1)

            def body(e):
                gu, d = known(e, 0, NE), known(e - 1, 0, NE)
                for n, name in enumerate(GU):
                    if gu:
                        split_gu(e, name)
                    if name == "g2" and d:
                        hidden(e - 1)
                    if name == "u1" and isinstance(e, int) and e == 0:
                        tokens(0)
                    if name == "u2" and gu:
                        sigmoid(e)
                for name in DN:
                    if d:
                        split_d(e - 1, name)
                    if name == "d2" and known(e + 1, 1, NE):
                        tokens(e + 1)

            iterations(act, body)

        @block.vector
        def _(v):
            for s in (v_gu, v_d, v_hid, v_x, v_h, v_y):
                v.sem_inc(s.sem, s.credit)

            choose(v, v_top, probs_t[0:NE, EARLY:T], left, late_best, late_where, 0, ROUNDS)
            step = 3 * ROUNDS - 1

            def rising(t):
                return bass.AP(t, CAP - 1, [[CAP, NE], [-1, CAP]])

            v.wait_ge(v_top, step)
            v.tensor_copy(place[0][:], early["where"][:]).then_inc(v_top, 1)
            v.tensor_copy(place[1][:], late_where[:]).then_inc(v_top, 1)
            v.tensor_tensor(is_early[:], early["best"][:], rising(late_best), ALU.is_ge).then_inc(v_top, 1)
            v.tensor_tensor(best[:], early["best"][:], rising(late_best), ALU.max).then_inc(v_top, 1)
            v.wait_ge(v_top, step + 2)
            v.tensor_scalar(place[1][:], place[1][:], float(EARLY), None, ALU.add).then_inc(v_top, 1)
            v.wait_ge(v_top, step + 5)
            v.tensor_tensor(place[0][:], place[0][:], rising(place[1]), ALU.subtract).then_inc(v_top, 1)
            v.wait_ge(v_top, step + 6)
            v.tensor_tensor(place[0][:], place[0][:], is_early[:], ALU.mult).then_inc(v_top, 1)
            v.wait_ge(v_top, step + 7)
            v.tensor_tensor(where_f[:], place[0][:], rising(place[1]), ALU.add).then_inc(v_top, 1)
            assert step + 8 == TOP_STEPS
            v.wait_ge(pe_top, 1)
            v.tensor_copy(token[:], ps_g[:, 0:NE]).then_inc(v_top, 1)
            v.tensor_copy(weight[:], ps_g[:, NE:2 * NE]).then_inc(v_top, 1)
            v.wait_ge(v_top, TOP_STEPS + 2)

            def split_gu(e, name):
                n = GU.index(name)
                if isinstance(e, int) and e == 0:
                    if n < SPLIT:
                        return
                    v.wait_ge(v_gu.sem, v_gu.after(0, GU[SPLIT - 1]))
                v.wait_ge(act_gu.sem, act_gu.after(e, name))
                v.tensor_tensor(w_tail[:, n % SPLIT], w_raw[:, n % RAW], w_head[:, n % SPLIT].bitcast(F32), ALU.subtract).then_inc(v_gu.sem, 1)

            def split_d(x, name):
                c = DN.index(name)
                v.wait_ge(act_d.sem, act_d.after(x, name))
                v.tensor_tensor(w_tail[:, (2 * NCH + c) % SPLIT], w_raw[:, (2 * NCH + c) % RAW], w_head[:, (2 * NCH + c) % SPLIT].bitcast(F32),
                                ALU.subtract).then_inc(v_d.sem, 1)

            def silu(e):
                v.wait_ge(act_sig.sem, act_sig.after(e, "sig"))
                v.wait_ge(pe_ht.sem, pe_ht.after(e - 1, "ht"))
                v.tensor_tensor(hid[:], ps_g[:], sig[:], ALU.mult).then_inc(v_hid.sem, 1)

            def gated(e):
                v.wait_ge(pe_gu.sem, pe_gu.after(e, GU[-1]))
                v.wait_ge(v_hid.sem, v_hid.after(e, "silu"))
                v.tensor_tensor(hid[:], hid[:], ps_u[:], ALU.mult).then_inc(v_hid.sem, 1)

            def tokens(x):
                v.wait_ge(pe_xt.sem, pe_xt.after(x, "xt"))
                v.wait_ge(act_x.sem, act_x.after(x - 1, "head"))
                wait(v, v_x, x - 1, "tail")
                for k in range(KT // 2, KT):
                    last = v.tensor_scalar(xm[:, k, :], ps_t[:, k, :], scale2[:, k:k + 1], shift2[:, k:k + 1], ALU.mult, ALU.add)
                last.then_inc(v_x.sem, 1)
                v.wait_ge(act_x.sem, act_x.after(x, "head"))
                v.tensor_tensor(x_tail[:], xm[:], x_head[:].bitcast(F32), ALU.subtract).then_inc(v_x.sem, 1)

            def hidden(x):
                v.wait_ge(act_h.sem, act_h.after(x, "head"))
                v.tensor_tensor(h_tail[:], ps_t[:], h_head[:].bitcast(F32), ALU.subtract).then_inc(v_h.sem, 1)

            def scale_rows(x):
                v.wait_ge(pe_d.sem, pe_d.after(x, DN[-1]))
                if known(x, 1, NE):
                    v.wait_ge(s_add, 16 * x)
                for half in range(2):
                    cols = slice(half * N512, (half + 1) * N512)
                    last = v.scalar_tensor_tensor(out=rows[:, cols], in0=ps_y[:, cols], scalar=weight[:, bass.ds(x, 1)],
                                                  in1=gates[:, 1, cols], op0=ALU.mult, op1=ALU.mult)
                last.then_inc(v_y.sem, 1)

            def body(e):
                gu, d = known(e, 0, NE), known(e - 1, 0, NE)
                for n, name in enumerate(GU):
                    if gu:
                        split_gu(e, name)
                    if name == "g2":
                        if d:
                            hidden(e - 1)
                        if known(e - 2, 0, NE):
                            scale_rows(e - 2)
                    if name == "u1" and isinstance(e, int) and e == 0:
                        tokens(0)
                    if name == "u2" and gu:
                        silu(e)
                for name in DN:
                    if d:
                        split_d(e - 1, name)
                    if name == "d2":
                        if gu:
                            gated(e)
                        if known(e + 1, 1, NE):
                            tokens(e + 1)

            iterations(v, body)


def phase_final(nc, dram):
    with ExitStack() as ctx:
        def sb(name, shape, dt=F32):
            return ctx.enter_context(nc.sbuf_tensor("f_" + name, shape, dt))

        def sem(name):
            return ctx.enter_context(nc.semaphore("f_" + name))

        hx = sb("hx", [P, NT, D])
        gain = sb("gain", [P, D])
        junk = sb("junk", [P, D])
        sumsq = sb("sumsq", [P, NT])
        meansq = sb("meansq", [P, NT])
        neghalf = sb("neghalf", [P, NT])
        rstd = sb("rstd", [P, NT])
        s_in = [sem(f"hx_landed{i}") for i in range(NT // 2)]
        s_gain = sem("gain_landed")
        s_out = sem("out_stored")
        act_sq = sem("act_square")
        v_mean = sem("v_mean")
        v_out = sem("v_out")
        pool_set = sem("pool_set")
        pool_rstd = sem("pool_rstd")

        block = ctx.enter_context(nc.Block())

        @block.sync
        def _(sp):
            for i in range(NT // 2):
                src = dram["acc"][2 * i * P:2 * (i + 1) * P, :].rearrange("(t p) d -> p t d", p=P)
                sp.dma_start(hx[:, 2 * i:2 * i + 2, :], src).then_inc(s_in[i], 16)
                if i == 0:
                    sp.dma_start(gain[:], dram["final_g"].rearrange("(a d) -> a d", a=1).broadcast_to([P, D])).then_inc(s_gain, 16)
            for i in range(NT):
                sp.wait_ge(v_out, i + 1)
                sp.dma_start(dram["out"][0, i * P:(i + 1) * P, :], hx[:, i, :]).then_inc(s_out, 16)
            sp.wait_ge(s_out, 16 * NT)

        @block.gpsimd
        def _(pool):
            pool.memset(neghalf[:], -0.5).then_inc(pool_set, 1)
            pool.wait_ge(pool_set, 1)
            for i in range(NT):
                pool.wait_ge(v_mean, i + 1)
                pool.tensor_tensor(rstd[:, i:i + 1], meansq[:, i:i + 1], neghalf[:, i:i + 1], ALU.pow).then_inc(pool_rstd, 1)

        @block.scalar
        def _(act):
            for i in range(NT):
                act.wait_ge(s_in[i // 2], 16)
                if i:
                    act.wait_ge(act_sq, i)
                act.activation(junk[:], hx[:, i, :], ACT.Square, accum_out=sumsq[:, i:i + 1]).then_inc(act_sq, 1)

        @block.vector
        def _(v):
            def mean(i):
                v.wait_ge(act_sq, i + 1)
                v.tensor_scalar(meansq[:, i:i + 1], sumsq[:, i:i + 1], 1.0 / D, EPS, ALU.mult, ALU.add).then_inc(v_mean, 1)

            def scaled(i):
                v.wait_ge(pool_rstd, i + 1)
                v.scalar_tensor_tensor(out=hx[:, i, :], in0=hx[:, i, :], scalar=rstd[:, i:i + 1], in1=gain[:],
                                       op0=ALU.mult, op1=ALU.mult).then_inc(v_out, 1)

            v.wait_ge(s_gain, 16)
            for i in range(NT):
                mean(i)
                if i >= 2:
                    scaled(i - 2)
            scaled(NT - 2)
            scaled(NT - 1)


_IN = ["x", "c", "ctx", "c_ctx", "lb_logits", "w_mod", "b_mod", "norm1_g", "w_in", "hgrn_norm_g", "w_a", "w_pool",
       "pool_scale", "w_b", "w_out", "norm2_g", "w_router", "w_e_gate", "w_e_up", "w_e_down", "final_g"]

_SCRATCH = {"og": (D, T), "yb": (P * len(WINDOWS), T), "gates": (2, D, T), "acc": (T, D), "vn": (T, D)}


def build(nc, dram):
    with ExitStack() as ctx:
        def sb(stack, name, shape, dt=F32):
            return stack.enter_context(nc.sbuf_tensor(name, shape, dt))

        keep = {"cols": sb(ctx, "cols", [P, P]), "ident": sb(ctx, "ident", [P, P]),
                "scale2": sb(ctx, "scale2", [P, KT]), "shift2": sb(ctx, "shift2", [P, KT]),
                "gates": sb(ctx, "gate_rows", [P, 2, D]),
                "csil": sb(ctx, "csil", [P, KT, 2]),
                "lb": sb(ctx, "lb", [P, 2, NH]), "olb": sb(ctx, "olb", [P, 2, NH])}
        with ExitStack() as mixer:
            ux_head = sb(mixer, "ux_head", [P, KT, TA], F32R)
            ux_tail = sb(mixer, "ux_tail", [P, KT, TA], F32R)
            phase_modulate(nc, dram, keep, ux_head, ux_tail)
            phase_pool_gates(nc, dram, keep, ux_head, ux_tail)
            phase_heads(nc, dram, keep, ux_head, ux_tail)
        probs_t = sb(ctx, "probs_t", [P, T])
        early = {"best": sb(ctx, "early_best", [NE, CAP]), "where": sb(ctx, "early_where", [NE, CAP], U32)}
        with ExitStack() as merge:
            y = sb(merge, "y", [P, KT, T])
            weighed = sb(merge, "weighed", [P, 2, D])
            phase_merge(nc, dram, keep, y, weighed, probs_t)
            phase_project(nc, dram, keep, y, weighed, probs_t, early)
        phase_experts(nc, dram, keep, probs_t, early)
        phase_final(nc, dram)


def constants():
    s = np.arange(P)
    masks = np.stack([((s[:, None] >> (l + 1)) == (s[None, :] >> (l + 1))) & (((s[:, None] ^ s[None, :]) >> l) & 1 == 1)
                      for l in range(LEVELS)], axis=1).astype(np.int32)
    icount = []
    for w in WINDOWS:
        def span(n):
            pos = np.arange(n)
            return np.clip(pos + w // 2 - 1, 0, n - 1) + 1 - np.clip(pos - w // 2, 0, n - 1)
        icount.append((1.0 / (span(ROWS)[:, None] * span(GRID_W)[None, :])).reshape(-1))
    return {"ident": np.eye(P, dtype=np.float32), "masks": masks, "icount": np.stack(icount)[None].astype(np.float32)}


def kernel(**inputs):
    import concourse.bacc as _bacc
    from concourse.bass_utils import run_bass_kernel_spmd as _run

    nc = _bacc.Bacc("TRN2", target_bir_lowering=False, num_devices=1)
    arrays, dram = {}, {}
    for name, a in {**{n: np.ascontiguousarray(inputs[n]) for n in _IN}, **constants()}.items():
        arrays[f"in_{name}"] = a
        dram[name] = nc.dram_tensor(f"in_{name}", a.shape, mybir.dt.from_np(a.dtype), kind="ExternalInput").ap()
    for name, shape in _SCRATCH.items():
        dram[name] = nc.dram_tensor(f"scr_{name}", shape, F32).ap()
    dram["out"] = nc.dram_tensor("out", (1, T, D), F32, kind="ExternalOutput").ap()
    build(nc, dram)
    return _run(nc, [arrays], core_ids=[0]).results[0]["out"]
```
